# Optimizing a Trainium2 kernel written in Bass

```python
import math
import jax
import jax.numpy as jnp
from jax import lax
import numpy as np

D_MODEL = 1024
BATCH = 1
SEQ = 256
DEPTH = 2

GRID_W = 64
CTX_LEN = 256
EPS = 1e-6
M_HEADS = 4
M_DH = D_MODEL // M_HEADS
M_WIDTH = M_HEADS * M_DH
M_CHUNK = 128
A_HEADS = 8
A_DH = D_MODEL // (2 * A_HEADS)
A_WIDTH = A_HEADS * 2 * A_DH
Q_BLOCK = 128
ROPE_BASE = 10000.0
H_WIDTH = D_MODEL
H_EMB = 33
H_FFN = 64
H_DECAY_MIN_PCT = 0.3
H_DECAY_MAX_PCT = 1.5
SHORT_CONV = 3
N_EXPERTS = 32
N_GROUPS = 4
TOPK_GROUPS = 1
TOP_K = 2
D_EXPERT = 512
MOE_BLOCK = 128
IN_SPLITS = (M_WIDTH, M_WIDTH, M_WIDTH, M_WIDTH, 4 * M_HEADS,
             A_WIDTH, A_WIDTH, A_WIDTH,
             H_WIDTH, H_WIDTH, H_WIDTH,
             3 * D_MODEL)
D_IN = sum(IN_SPLITS)

kernel_name = 'hybrid_mlstm_diffattn_hyena_moe_dit'

def _rmsnorm(x, g):
    xf = x.astype(jnp.float32)
    y = xf * lax.rsqrt(jnp.mean(xf * xf, axis=-1, keepdims=True) + EPS)
    return (y * g.astype(jnp.float32)).astype(x.dtype)

def _modulate(xn, shift, scale):
    return xn * (1 + scale) + shift

def _short_conv(u, w, b):
    L = u.shape[1]
    pad = SHORT_CONV // 2
    up = jnp.pad(u, ((0, 0), (pad, pad), (0, 0)))
    y = b
    for j in range(SHORT_CONV):
        y = y + up[:, j:j + L] * w[j]
    return y

def _heads(a, n_heads):
    B, L, W = a.shape
    return a.reshape(B, L, n_heads, W // n_heads).transpose(0, 2, 1, 3)

def _flip(a):
    return jnp.flip(a, axis=2)

def _axial_rope(L, dh):
    rows = L // GRID_W
    row = jnp.broadcast_to(jnp.arange(rows)[:, None], (rows, GRID_W)).reshape(-1).astype(jnp.float32)
    col = jnp.broadcast_to(jnp.arange(GRID_W)[None, :], (rows, GRID_W)).reshape(-1).astype(jnp.float32)
    nf = dh // 4
    inv = ROPE_BASE ** (-jnp.arange(nf, dtype=jnp.float32) / nf)
    ang_r = row[:, None] * inv
    ang_c = col[:, None] * inv
    ang = jnp.concatenate([ang_r, ang_r, ang_c, ang_c], axis=-1)
    return jnp.cos(ang), jnp.sin(ang)

def _rot_half(h):
    h1, h2 = jnp.split(h, 2, axis=-1)
    return jnp.concatenate([-h2, h1], axis=-1)

def _apply_rope(x, cos, sin):
    xr, xc = jnp.split(x, 2, axis=-1)
    rot = jnp.concatenate([_rot_half(xr), _rot_half(xc)], axis=-1)
    return (x.astype(jnp.float32) * cos + rot.astype(jnp.float32) * sin).astype(x.dtype)

def _mlstm_scan(q, k, v, li, lf, state):
    B, H, L, dk = q.shape
    dv = v.shape[-1]
    nc = L // M_CHUNK

    def chunks(a):
        return jnp.moveaxis(a.reshape((B, H, nc, M_CHUNK) + a.shape[3:]), 2, 0)

    mask = jnp.tril(jnp.ones((M_CHUNK, M_CHUNK), dtype=bool))

    def step(carry, inp):
        C, n, m = carry
        qc, kc, vc, lic, lfc = inp
        b = jnp.cumsum(lfc, axis=-1)
        Dm = jnp.where(mask, b[..., :, None] - b[..., None, :] + lic[..., None, :], -jnp.inf)
        inter = b + m[..., None]
        mt = jnp.maximum(inter, jnp.max(Dm, axis=-1))
        S = jnp.einsum('bhtd,bhsd->bhts', qc, kc) * jnp.exp(Dm - mt[..., None])
        wi = jnp.exp(inter - mt)
        num = jnp.einsum('bhts,bhsv->bhtv', S, vc) + wi[..., None] * jnp.einsum('bhtk,bhkv->bhtv', qc, C)
        den = jnp.sum(S, axis=-1) + wi * jnp.einsum('bhtk,bhk->bht', qc, n)
        h = num / jnp.maximum(jnp.abs(den), jnp.exp(-mt))[..., None]
        bQ = b[..., -1]
        ws = bQ[..., None] - b + lic
        m_new = jnp.maximum(bQ + m, jnp.max(ws, axis=-1))
        decay = jnp.exp(bQ + m - m_new)
        kw = kc * jnp.exp(ws - m_new[..., None])[..., None]
        C_new = decay[..., None, None] * C + jnp.einsum('bhsk,bhsv->bhkv', kw, vc)
        n_new = decay[..., None] * n + jnp.sum(kw, axis=2)
        return (C_new, n_new, m_new), h

    state, hs = lax.scan(step, state, (chunks(q), chunks(k), chunks(v), chunks(li), chunks(lf)))
    h = jnp.moveaxis(hs, 0, 2).reshape(B, H, L, dv)
    return h, state

def _mlstm_inputs(mq, mk, mv, mg, conv_w, conv_b, gate_b):
    qk = jax.nn.silu(_short_conv(jnp.concatenate([mq, mk], axis=-1), conv_w, conv_b))
    q, k = jnp.split(qk, 2, axis=-1)
    q = _heads(q, M_HEADS).astype(jnp.float32)
    k = _heads(k, M_HEADS).astype(jnp.float32) * (M_DH ** -0.5)
    v = _heads(mv, M_HEADS).astype(jnp.float32)
    B, L, _ = mg.shape
    g = (mg.astype(jnp.float32) + gate_b.astype(jnp.float32)).reshape(B, L, 4, M_HEADS).transpose(2, 0, 3, 1)
    return q, k, v, g[0], jax.nn.log_sigmoid(g[1]), g[2], jax.nn.log_sigmoid(g[3])

def _mlstm_out(h, o, g):
    B, H, L, dv = h.shape
    y = _rmsnorm(h.transpose(0, 2, 1, 3), g).reshape(B, L, H * dv)
    return (y * jax.nn.sigmoid(o.astype(jnp.float32))).astype(o.dtype)

def _mlstm_branch(parts_l, parts_c, conv_w, conv_b, gate_b, norm_g, need_ctx):
    mq_l, mk_l, mv_l, mo_l, mg_l = parts_l
    mq_c, mk_c, mv_c, mo_c, mg_c = parts_c
    ql, kl, vl, ilf, flf, ilb, flb = _mlstm_inputs(mq_l, mk_l, mv_l, mg_l, conv_w, conv_b, gate_b)
    qc, kc, vc, icf, fcf, icb, fcb = _mlstm_inputs(mq_c, mk_c, mv_c, mg_c, conv_w, conv_b, gate_b)
    B = ql.shape[0]
    zero = (jnp.zeros((B, M_HEADS, M_DH, M_DH), jnp.float32),
            jnp.zeros((B, M_HEADS, M_DH), jnp.float32),
            jnp.zeros((B, M_HEADS), jnp.float32))
    hcf, s_f = _mlstm_scan(qc, kc, vc, icf, fcf, zero)
    hcb, s_b = _mlstm_scan(_flip(qc), _flip(kc), _flip(vc), _flip(icb), _flip(fcb), zero)
    hlf, _ = _mlstm_scan(ql, kl, vl, ilf, flf, s_f)
    hlb, _ = _mlstm_scan(_flip(ql), _flip(kl), _flip(vl), _flip(ilb), _flip(flb), s_b)
    yl = _mlstm_out(hlf + _flip(hlb), mo_l, norm_g)
    yc = _mlstm_out(hcf + _flip(hcb), mo_c, norm_g) if need_ctx else None
    return yl, yc

def _diff_inputs(aq, ak, av, qg, kg):
    B, L, _ = aq.shape
    q = _rmsnorm(aq.reshape(B, L, A_HEADS, 2, A_DH), qg).transpose(0, 2, 3, 1, 4)
    k = _rmsnorm(ak.reshape(B, L, A_HEADS, 2, A_DH), kg).transpose(0, 2, 3, 1, 4)
    v = _heads(av, A_HEADS)
    return q, k, v

def _diff_attend(q, k, v, lam):
    s = jnp.einsum('bhcqd,bhckd->bhcqk', q, k).astype(jnp.float32) * (A_DH ** -0.5)
    p = jax.nn.softmax(s, axis=-1)
    w = p[:, :, 0] - lam * p[:, :, 1]
    return jnp.einsum('bhqk,bhkd->bhqd', w.astype(v.dtype), v)

def _diff_out(o, g, lam_init):
    B, H, L, dv = o.shape
    return (_rmsnorm(o.transpose(0, 2, 1, 3), g) * (1.0 - lam_init)).reshape(B, L, H * dv)

def _diff_branch(parts_l, parts_c, qg, kg, lam_p, sub_g, lam_init, cos, sin, need_ctx):
    ql, kl, vl = _diff_inputs(parts_l[0], parts_l[1], parts_l[2], qg, kg)
    qc, kc, vc = _diff_inputs(parts_c[0], parts_c[1], parts_c[2], qg, kg)
    ql = _apply_rope(ql, cos, sin)
    kl = _apply_rope(kl, cos, sin)
    lp = lam_p.astype(jnp.float32)
    lam = jnp.exp(jnp.sum(lp[0] * lp[1])) - jnp.exp(jnp.sum(lp[2] * lp[3])) + lam_init
    k_all = jnp.concatenate([kc, kl], axis=3)
    v_all = jnp.concatenate([vc, vl], axis=2)
    B, H, _, L, dh = ql.shape
    nb = L // Q_BLOCK
    qb = jnp.moveaxis(ql.reshape(B, H, 2, nb, Q_BLOCK, dh), 3, 0)
    ob = lax.map(lambda qq: _diff_attend(qq, k_all, v_all, lam), qb)
    ol = jnp.moveaxis(ob, 0, 2).reshape(B, H, L, 2 * dh)
    yl = _diff_out(ol, sub_g, lam_init)
    yc = _diff_out(_diff_attend(qc, kc, vc, lam), sub_g, lam_init) if need_ctx else None
    return yl, yc

def _hyena_filters(L, w1, b1, w2, b2, w3, freq, delta):
    t = jnp.linspace(0.0, 1.0, L, dtype=jnp.float32)[:, None]
    bands = (H_EMB - 1) // 2
    w = 2.0 * math.pi * jnp.arange(L, dtype=jnp.float32)[:, None] / L
    f = jnp.linspace(1e-4, bands - 1, bands, dtype=jnp.float32)[None, :]
    z = jnp.concatenate([t, jnp.cos(f * w), -jnp.sin(f * w)], axis=-1)
    hdn = jnp.sin(freq * (z @ w1 + b1))
    hdn = jnp.sin(freq * (hdn @ w2 + b2))
    h = ((hdn @ w3) * jnp.exp(-t * jnp.abs(delta))).astype(jnp.float32)
    h = h.reshape(L, 2, H_WIDTH)
    h = h * lax.rsqrt(jnp.sum(h * h, axis=(0, 1), keepdims=True) + EPS)
    return h[:, 0], h[:, 1]

def _bidir_longconv(u, hf, hb):
    L = u.shape[1]
    n = 2 * L
    taps = jnp.concatenate([hf, jnp.zeros_like(hf[:1]), jnp.flip(hb[1:], axis=0)], axis=0)
    U = jnp.fft.rfft(u.astype(jnp.float32), n=n, axis=1)
    Hf = jnp.fft.rfft(taps, n=n, axis=0)
    return jnp.fft.irfft(U * Hf[None], n=n, axis=1)[:, :L]

def _hyena_seq(hx0, hx1, hv, conv_w, conv_b, filt, bias):
    u = _short_conv(jnp.concatenate([hx0, hx1, hv], axis=-1), conv_w, conv_b)
    x0, x1, v = jnp.split(u.astype(jnp.float32), 3, axis=-1)
    hf, hb = _hyena_filters(u.shape[1], *filt)
    z = v * x1
    z = _bidir_longconv(z, hf, hb) + bias.astype(jnp.float32) * z
    return (x0 * z).astype(hx0.dtype)

def _merge(ym, ya, yh, gpre, mb, wm, wa, wh, wo):
    g = jax.nn.sigmoid((gpre + mb).astype(jnp.float32)).astype(ym.dtype)
    g_m, g_a, g_h = jnp.split(g, 3, axis=-1)
    y = g_m * (ym @ wm) + g_a * (ya @ wa) + g_h * (yh @ wh)
    return y @ wo

def _moe(h, router_w, router_b, w1, w3, w2):
    N, D = h.shape
    E, G, K = N_EXPERTS, N_GROUPS, TOP_K
    s = jax.nn.sigmoid((h @ router_w).astype(jnp.float32))
    sb = s + router_b.astype(jnp.float32)
    gscore = jnp.sum(lax.top_k(sb.reshape(N, G, E // G), 2)[0], axis=-1)
    _, gidx = lax.top_k(gscore, TOPK_GROUPS)
    gmask = jnp.any(gidx[:, :, None] == jnp.arange(G)[None, None, :], axis=1)
    emask = jnp.repeat(gmask, E // G, axis=1)
    _, eidx = lax.top_k(jnp.where(emask, sb, -jnp.inf), K)
    wsel = jnp.take_along_axis(s, eidx, axis=1)
    wsel = wsel / jnp.sum(wsel, axis=-1, keepdims=True)
    A = N * K
    flat_e = eidx.reshape(A)
    flat_t = jnp.repeat(jnp.arange(N, dtype=jnp.int32), K)
    flat_w = wsel.reshape(A)
    order = jnp.argsort(flat_e)
    se = flat_e[order]
    counts = jnp.bincount(flat_e, length=E)
    start = jnp.cumsum(counts) - counts
    padded = (counts + MOE_BLOCK - 1) // MOE_BLOCK * MOE_BLOCK
    pend = jnp.cumsum(padded)
    pstart = pend - padded
    dest = pstart[se] + jnp.arange(A) - start[se]
    P = -(-(A + E * (MOE_BLOCK - 1)) // MOE_BLOCK) * MOE_BLOCK
    tok_buf = jnp.zeros((P,), jnp.int32).at[dest].set(flat_t[order])
    w_buf = jnp.zeros((P,), jnp.float32).at[dest].set(flat_w[order])
    nblk = P // MOE_BLOCK
    blk_e = jnp.minimum(jnp.sum(pend[None, :] <= (jnp.arange(nblk) * MOE_BLOCK)[:, None], axis=1), E - 1)
    xb = h[tok_buf].reshape(nblk, MOE_BLOCK, D)

    def expert_block(args):
        xe, e = args
        return (jax.nn.silu(xe @ w1[e]) * (xe @ w3[e])) @ w2[e]

    yb = lax.map(expert_block, (xb, blk_e)).reshape(P, D)
    return jax.ops.segment_sum(yb * w_buf[:, None].astype(yb.dtype), tok_buf, num_segments=N)

def setup_inputs(seed: int = 0) -> dict:
    key = jax.random.key(seed)
    ks = iter(jax.random.split(key, 48))

    def nrm(shape, scale):
        return jax.random.normal(next(ks), shape, jnp.float32) * scale

    D = D_MODEL
    fb = jnp.linspace(3.0, 6.0, M_HEADS, dtype=jnp.float32)
    m_gate_b = jnp.concatenate([nrm((DEPTH, M_HEADS), 0.1), fb + nrm((DEPTH, M_HEADS), 0.1),
                                nrm((DEPTH, M_HEADS), 0.1), fb + nrm((DEPTH, M_HEADS), 0.1)], axis=-1)
    decay0 = jnp.linspace(math.log(1e-2) / H_DECAY_MIN_PCT, math.log(1e-2) / H_DECAY_MAX_PCT,
                          2 * H_WIDTH, dtype=jnp.float32)
    return {
        'x': nrm((BATCH, SEQ, D), 1.0),
        'c': nrm((BATCH, D), 1.0),
        'ctx': nrm((BATCH, CTX_LEN, D), 1.0),
        'c_ctx': nrm((D,), 1.0),
        'mod_w': nrm((DEPTH, D, 6 * D), 0.5 * D ** -0.5),
        'mod_b': nrm((DEPTH, 6 * D), 0.02),
        'norm1_g': 1.0 + nrm((DEPTH, D), 0.02),
        'norm2_g': 1.0 + nrm((DEPTH, D), 0.02),
        'w_in': nrm((DEPTH, D, D_IN), D ** -0.5),
        'merge_b': nrm((DEPTH, 3 * D), 0.02),
        'm_conv_w': nrm((DEPTH, SHORT_CONV, 2 * M_WIDTH), 0.5),
        'm_conv_b': nrm((DEPTH, 2 * M_WIDTH), 0.02),
        'm_gate_b': m_gate_b,
        'm_norm_g': 1.0 + nrm((DEPTH, M_DH), 0.02),
        'a_qnorm_g': 1.0 + nrm((DEPTH, A_DH), 0.02),
        'a_knorm_g': 1.0 + nrm((DEPTH, A_DH), 0.02),
        'a_lambda': nrm((DEPTH, 4, A_DH), 0.1),
        'a_subln_g': 1.0 + nrm((DEPTH, 2 * A_DH), 0.02),
        'h_conv_w': nrm((DEPTH, SHORT_CONV, 3 * H_WIDTH), 0.5),
        'h_conv_b': nrm((DEPTH, 3 * H_WIDTH), 0.02),
        'h_ffn_w1': nrm((DEPTH, H_EMB, H_FFN), H_EMB ** -0.5),
        'h_ffn_b1': nrm((DEPTH, H_FFN), 0.1),
        'h_ffn_w2': nrm((DEPTH, H_FFN, H_FFN), H_FFN ** -0.5),
        'h_ffn_b2': nrm((DEPTH, H_FFN), 0.1),
        'h_ffn_w3': nrm((DEPTH, H_FFN, 2 * H_WIDTH), H_FFN ** -0.5),
        'h_freq': 1.0 + nrm((DEPTH, H_FFN), 0.02),
        'h_decay': decay0 + nrm((DEPTH, 2 * H_WIDTH), 0.05),
        'h_bias': nrm((DEPTH, H_WIDTH), 1.0),
        'w_br_m': nrm((DEPTH, M_WIDTH, D), M_WIDTH ** -0.5),
        'w_br_a': nrm((DEPTH, A_WIDTH, D), A_WIDTH ** -0.5),
        'w_br_h': nrm((DEPTH, H_WIDTH, D), H_WIDTH ** -0.5),
        'w_out': nrm((DEPTH, D, D), D ** -0.5),
        'router_w': nrm((D, N_EXPERTS), D ** -0.5),
        'router_b': nrm((N_EXPERTS,), 0.01),
        'e_w1': nrm((DEPTH, N_EXPERTS, D, D_EXPERT), D ** -0.5),
        'e_w3': nrm((DEPTH, N_EXPERTS, D, D_EXPERT), D ** -0.5),
        'e_w2': nrm((DEPTH, N_EXPERTS, D_EXPERT, D), D_EXPERT ** -0.5),
    }

def reference(x, c, ctx, c_ctx, mod_w, mod_b, norm1_g, norm2_g, w_in, merge_b,
              m_conv_w, m_conv_b, m_gate_b, m_norm_g,
              a_qnorm_g, a_knorm_g, a_lambda, a_subln_g,
              h_conv_w, h_conv_b, h_ffn_w1, h_ffn_b1, h_ffn_w2, h_ffn_b2, h_ffn_w3,
              h_freq, h_decay, h_bias,
              w_br_m, w_br_a, w_br_h, w_out,
              router_w, router_b, e_w1, e_w3, e_w2):
    B, L, D = x.shape
    Lc = ctx.shape[1]
    rope_cos, rope_sin = _axial_rope(L, A_DH)
    offs = [int(o) for o in np.cumsum(IN_SPLITS)[:-1]]
    xl, xc = x, ctx
    for l in range(DEPTH):
        need_ctx = l < DEPTH - 1
        lam_init = 0.8 - 0.6 * math.exp(-0.3 * l)
        mod_l = jax.nn.silu(c) @ mod_w[l] + mod_b[l]
        mod_c = jax.nn.silu(c_ctx) @ mod_w[l] + mod_b[l]
        sh1, sc1, g1, sh2, sc2, g2 = jnp.split(mod_l[:, None, :], 6, axis=-1)
        sh1c, sc1c, g1c, sh2c, sc2c, g2c = jnp.split(mod_c, 6, axis=-1)
        hl = _modulate(_rmsnorm(xl, norm1_g[l]), sh1, sc1)
        hc = _modulate(_rmsnorm(xc, norm1_g[l]), sh1c, sc1c)
        pl = jnp.split(hl @ w_in[l], offs, axis=-1)
        pc = jnp.split(hc @ w_in[l], offs, axis=-1)
        ym_l, ym_c = _mlstm_branch(pl[0:5], pc[0:5], m_conv_w[l], m_conv_b[l], m_gate_b[l],
                                   m_norm_g[l], need_ctx)
        ya_l, ya_c = _diff_branch(pl[5:8], pc[5:8], a_qnorm_g[l], a_knorm_g[l], a_lambda[l],
                                  a_subln_g[l], lam_init, rope_cos, rope_sin, need_ctx)
        filt = (h_ffn_w1[l], h_ffn_b1[l], h_ffn_w2[l], h_ffn_b2[l], h_ffn_w3[l], h_freq[l], h_decay[l])
        yh_l = _hyena_seq(pl[8], pl[9], pl[10], h_conv_w[l], h_conv_b[l], filt, h_bias[l])
        mix_l = _merge(ym_l, ya_l, yh_l, pl[11], merge_b[l], w_br_m[l], w_br_a[l], w_br_h[l], w_out[l])
        if need_ctx:
            yh_c = _hyena_seq(pc[8], pc[9], pc[10], h_conv_w[l], h_conv_b[l], filt, h_bias[l])
            mix_c = _merge(ym_c, ya_c, yh_c, pc[11], merge_b[l], w_br_m[l], w_br_a[l], w_br_h[l], w_out[l])
            xc = xc + g1c * mix_c
        xl = xl + g1 * mix_l
        tok = _modulate(_rmsnorm(xl, norm2_g[l]), sh2, sc2).reshape(B * L, D)
        if need_ctx:
            tok_c = _modulate(_rmsnorm(xc, norm2_g[l]), sh2c, sc2c).reshape(B * Lc, D)
            tok = jnp.concatenate([tok, tok_c], axis=0)
        f = _moe(tok, router_w, router_b, e_w1[l], e_w3[l], e_w2[l])
        xl = xl + g2 * f[:B * L].reshape(B, L, D)
        if need_ctx:
            xc = xc + g2c * f[B * L:].reshape(B, Lc, D)
    return xl


_drawn_inputs = setup_inputs


def setup_inputs(seed=0):
    import zlib

    import numpy as np

    out = dict(_drawn_inputs(seed))
    spreads = {}
    factors = {'merge_b': 5.27,
     'm_conv_b': 4.705,
     'm_norm_g': 5.175,
     'a_qnorm_g': 6.125,
     'a_knorm_g': 5.353,
     'a_lambda': 5.169,
     'a_subln_g': 5.099,
     'h_freq': 3.213}
    for name, (base, spread) in spreads.items():
        noise = np.random.default_rng([zlib.crc32(name.encode()), seed]).standard_normal(out[name].shape)
        drawn = base * np.exp(spread * noise) if base else spread * noise
        out[name] = jnp.asarray(drawn.astype(out[name].dtype))
    for name, factor in factors.items():
        out[name] = (out[name] * factor).astype(out[name].dtype)
    return out
```

```python
import math
from contextlib import ExitStack, contextmanager

import numpy as np

import concourse.bass as bass
from concourse import mybir

P = 128
D = 1024
KC = D // P
SEQ = 256
NTOK = 2 * SEQ
DEPTH = 2
EPS = 1e-6
M_HEADS, M_DH = 4, 256
A_HEADS, A_DH = 8, 64
N_EXP, N_GRP, D_EXP, TOP_K = 32, 4, 512, 2
GRP = N_EXP // N_GRP
H_EMB, H_FFN = 33, 64
GRID_W = 64
SLOT = 128
SORTED = TOP_K * NTOK
SORTED_PAD = SORTED + SLOT

F32 = mybir.dt.float32
I32 = mybir.dt.int32
U32 = mybir.dt.uint32
ALU = mybir.AluOpType
ACT = mybir.ActivationFunctionType
AX = mybir.AxisListType
LN_EXP = "natural_log_exp_and_others"

C_N1, C_N2, C_MB = 0, 8, 16
C_MCW, C_MCB = 40, 88
C_HCW, C_HCB, C_HBIAS = 104, 176, 200
C_QG, C_KG, C_SUB, C_MN = 208, 209, 210, 211
C_FREQ, C_FB1, C_FB2, C_GB = 213, 214, 215, 216
N_COLS = 217
SH1, SC1, G1, SH2, SC2, G2 = (8 * i for i in range(6))


def pairs(eng, n, body):
    with eng.Fori(0, n // 2) as i:
        for s in range(2):
            body(i * 2 + s, s)


def prefetch(sp, n, load, free, early, tile_in):
    for s in range(2):
        early.hand_over(sp, s, tile_in[s])
    with sp.Fori(0, n // 2 - 1) as i:
        for s in range(2):
            free(i * 2 + s)
            load(i * 2 + (s + 2), s)


class Early:

    def __init__(self, nc, n):
        self.sems = [nc.alloc_semaphore(f"early_in{i}") for i in range(n)]
        self.counts = [0] * n

    def issue(self, sp, i, dst, src):
        sp.dma_start(dst, src).then_inc(self.sems[i], 16)
        self.counts[i] += 16

    def hand_over(self, sp, i, sem):
        sp.wait_ge(self.sems[i], self.counts[i])
        sp.sem_inc(sem, 16)


class Chain:

    def __init__(self, eng, sem, base=0):
        self.eng, self.sem, self.base, self.n = eng, sem, base, 0

    def then(self, ins):
        ins.then_inc(self.sem, 1)
        self.n += 1

    def wait(self):
        self.eng.wait_ge(self.sem, self.base + self.n)


class Core:

    def __init__(self, A):
        self.A = A


@contextmanager
def stage(nc, *names):
    sems = [nc.alloc_semaphore(name) for name in names]
    yield sems
    for s in sems:
        nc.sync.sem_clear(s)
    nc.all_engine_barrier()
    for s in sems:
        nc.release_semaphore(s)


def accumulate(pe, out, lhs, rhs, n):
    for k in range(n):
        last = pe.matmul(out, lhs(k), rhs(k), start=(k == 0), stop=(k == n - 1))
    return last


def hyena_tile(K, l, u, s):
    return K.ring(s), K.A["d_wh"][l, bass.ds(u, 1)].rearrange("a p n -> p (a n)")


def merge_tile(K, l, branch, u, s):
    return K.ring(s, KC * 256), K.A["d_wm"][l, branch, bass.ds(u, 1)].rearrange("a p n -> p (a n)")


def out_tile(K, l, u, s):
    return K.ring(s, KC * 256), K.A["d_wo"][l, bass.ds(u, 1)].rearrange("a p n -> p (a n)")


def attention_tile(K, l, u, s):
    return K.ring(s), K.A["d_wa"][l, bass.ds(u, 1)].rearrange("a p n -> p (a n)")


def mlstm_tile(K, l, h, s):
    if s < 2:
        return K.ring(s), K.A["d_wma"][l, bass.ds(h, 1), s].rearrange("a p n -> p (a n)")
    return K.ring(2, KC * 256), K.A["d_wmc"][l, bass.ds(h, 1)].rearrange("a p n -> p (a n)")


def mod_tile(K, u, s):
    return K.ring(s), K.A["d_modw"][bass.ds(u, 1)].rearrange("a p n -> p (a n)")


def spans(l):
    return (0, 2) if l < DEPTH - 1 else (SEQ, 1)


def stage_modulation(nc, K):
    WIDE = 48
    SLOTS = 4
    names = ["cond_in", "constants_in", "ones_set", "tanh_done", "silu_done", "projected", "copied", "mod_done"] + [f"tile_in{s}" for s in range(SLOTS)]
    with stage(nc, *names) as (cond_in, constants_in, ones_set, tanh_done, silu_done, projected, copied, mod_done, *tile_in), nc.Block() as block:
        cT = K.f(112, KC * 2).rearrange("p (k s) -> p k s", s=2)
        th = K.f(113, KC * 2).rearrange("p (k s) -> p k s", s=2)
        modb = K.f(114, 96)
        sil = K.f(116, KC * 2 * WIDE).rearrange("p (k n) -> p k n", k=KC)
        slots = [K.ring(s) for s in range(SLOTS)]
        n_tiles = DEPTH * 16
        CH = 3

        @block.sync
        def _(sp):
            sp.dma_start(cT, K.A["cT"]).then_inc(cond_in, 16)
            sp.dma_start(modb, K.A["d_modb"]).then_inc(cond_in, 16)

            def load(u, s):
                sp.dma_start(*mod_tile(K, u, s)).then_inc(tile_in[s], 16)
            for s in range(SLOTS):
                load(s, s)
            constants = [(K.X[:, :, :], K.A["xT"]), (K.ident, K.A["d_ident"]), (K.group64, K.A["d_group64"]),
                         (K.rot, K.A["d_rot"]), (K.before, K.A["d_before"]), (K.iota, K.A["d_iota"]),
                         (K.cols, K.A["d_cols"]), (K.lam4, K.A["d_lam4"]), (K.pidx, K.A["d_pidx"])]
            for dst, src in constants:
                sp.dma_start(dst, src).then_inc(constants_in, 16)
            with sp.Fori(0, n_tiles // SLOTS - 1) as i:
                for s in range(SLOTS):
                    sp.wait_ge(projected, i * SLOTS + (s + 1))
                    load(i * SLOTS + (s + SLOTS), s)
            sp.wait_ge(constants_in, 16 * len(constants))

        @block.scalar
        def _(act):
            act.wait_ge(cond_in, 32)
            act.activation(th, cT, ACT.Tanh, scale=0.5).then_inc(tanh_done, 1)

        @block.vector
        def _(v):
            v.wait_ge(tanh_done, 1)
            v.scalar_tensor_tensor(out=th, in0=th, scalar=1.0, in1=cT, op0=ALU.add, op1=ALU.mult).then_inc(silu_done, 1)
            v.wait_ge(silu_done, 1)
            v.tensor_scalar(sil.rearrange("p k (s n) -> p (k s) n", s=2),
                            th.rearrange("p k (s a) -> p (k s) a", a=1).to_broadcast([P, 2 * KC, WIDE]), 0.5, None,
                            ALU.mult).then_inc(silu_done, 1)
            v.memset(K.ones, 1.0).then_inc(ones_set, 1)
            v.memset(K.half_mb, 0.0).then_inc(ones_set, 1)
            v.memset(K.eps, EPS).then_inc(ones_set, 1)
            v.wait_ge(ones_set, 3)
            v.wait_ge(constants_in, 16 * 9)
            for l in range(DEPTH):
                v.tensor_scalar(K.half_mb[:, l, :], K.cols[:, l, C_MB:C_MB + 24], 0.5, None, ALU.mult).then_inc(ones_set, 1)

            def tile(u, s):
                v.wait_ge(projected, u + 1)
                v.tensor_copy(K.mod[:, bass.ds(u * CH, CH), :],
                              K.ps[:, s, 0:CH * 2 * WIDE].rearrange("p (j s n) -> p j s n", s=2, n=WIDE)[:, :, :, 0]).then_inc(copied, 1)
            pairs(v, n_tiles, tile)
            v.wait_ge(copied, n_tiles + 2)
            for s in range(2):
                v.tensor_tensor(K.mod[:, :, s], K.mod[:, :, s], modb, ALU.add).then_inc(mod_done, 1)
            v.wait_ge(mod_done, 2)
            for l in range(DEPTH):
                for i, (sc, g) in enumerate(((SC1, C_N1), (SC2, C_N2))):
                    for s in range(2):
                        v.scalar_tensor_tensor(out=K.gain[:, l, i, :, s], in0=K.mod[:, 48 * l + sc:48 * l + sc + KC, s],
                                               scalar=1.0, in1=K.cols[:, l, g:g + KC], op0=ALU.add,
                                               op1=ALU.mult).then_inc(mod_done, 1)
            v.wait_ge(mod_done, 2 + 4 * DEPTH)

        @block.tensor
        def _(pe):
            pe.wait_ge(silu_done, 2)
            pe.sem_inc(copied, 2)
            with pe.Fori(0, n_tiles // SLOTS) as i:
                for s in range(SLOTS):
                    u = i * SLOTS + s
                    pe.wait_ge(tile_in[s], i * 16 + 16)
                    pe.wait_ge(copied, u + 1)
                    w = slots[s].rearrange("p (k c) -> p k c", k=KC)
                    for c in range(CH):
                        last = accumulate(pe, K.ps[:, s % 2, c * 2 * WIDE:(c + 1) * 2 * WIDE],
                                          lambda k: w[:, k, c * P:c * P + P], lambda k: sil[:, k, :], KC)
                    last.then_inc(projected, 1)


def stage_norm(nc, K, l, half):
    t0, ns = (0, 2) if half == 0 else spans(l)
    nt = ns * SEQ
    with stage(nc, "squared", "summed", "meaned", "rooted", "rstd_done", "scaled", "normed") as (
            squared, summed, meaned, rooted, rstd_done, scaled, normed), nc.Block() as block:
        total = K.ps[:, 0, t0:NTOK]
        rstd = K.f(198, NTOK)[:, t0:NTOK]

        @block.sync
        def _(sp):
            if half == 0:
                for dst, src in filter_consts(K, l):
                    K.early.issue(sp, 3, dst, src)

        @block.scalar
        def _(act):
            for k in range(KC):
                act.activation(K.H[:, k, t0:], K.X[:, k, t0:], ACT.Square).then_inc(squared, 1)
            act.wait_ge(meaned, 1)
            act.activation(rstd, rstd, ACT.Sqrt).then_inc(rooted, 1)
            for k in range(KC):
                act.wait_ge(scaled, k + 1)
                for s in range(2 - ns, 2):
                    t = slice(s * SEQ, s * SEQ + SEQ)
                    act.activation(K.H[:, k, t], K.H[:, k, t], ACT.Identity, scale=K.gain[:, l, half, k, s:s + 1],
                                   bias=K.mod[:, 48 * l + (SH1, SH2)[half] + k, s:s + 1]).then_inc(normed, 1)
            act.wait_ge(normed, KC * ns)

        @block.tensor
        def _(pe):
            for k in range(KC):
                pe.wait_ge(squared, k + 1)
                last = pe.matmul(total, K.ones, K.H[:, k, t0:], start=(k == 0), stop=(k == KC - 1))
            last.then_inc(summed, 1)

        @block.vector
        def _(v):
            v.wait_ge(summed, 1)
            v.tensor_scalar(rstd, total, 1.0 / D, EPS, ALU.mult, ALU.add).then_inc(meaned, 1)
            v.wait_ge(rooted, 1)
            v.reciprocal(rstd, rstd).then_inc(rstd_done, 1)
            v.wait_ge(rstd_done, 1)
            for k in range(KC):
                v.tensor_tensor(K.H[:, k, t0:], K.X[:, k, t0:], rstd, ALU.mult).then_inc(scaled, 1)


def filter_consts(K, l):
    A = K.A
    return [(K.f(100, SEQ)[0:H_EMB, :], A["d_zT"]), (K.f(101, H_FFN)[0:H_EMB, :], A["d_fw1"][l]),
            (K.f(102, H_FFN)[0:H_FFN, :], A["d_fw2"][l]), (K.f(103, SEQ)[0:1, :], A["d_negt"]),
            (K.f(104, 2 * D)[0:H_FFN, :], A["d_fw3"][l]), (K.f(112, 2 * D)[0:1, :], A["d_delta"][l:l + 1]),
            (K.dft, A["d_dft"])]


def stage_filter(nc, K, l):
    names = ("consts_in", "layer_done", "sin_in", "sin_done", "decay_done", "taps_made", "taps_summed", "rn_step",
             "spectra_done", "copied", "chain", "acts", "hidden")
    with stage(nc, *names) as (consts_in, layer_done, sin_in, sin_done, decay_done, taps_made, taps_summed, rn_step,
                               spectra_done, copied, chain, acts, hidden), nc.Block() as block:
        zT, w1, w2, neg_t, w3, delta, _ = (dst for dst, _ in filter_consts(K, l))
        arg = K.f(120, SEQ)[0:H_FFN, :]
        turns_i = K.i(121, SEQ)[0:H_FFN, :]
        turns = K.f(122, SEQ)[0:H_FFN, :]
        hid = [K.f(123, SEQ)[0:H_FFN, :], K.f(124, SEQ)[0:H_FFN, :]]
        fix = K.f(125, SEQ)[0:H_FFN, :]
        decay = [K.f(126, 512), K.f(128, 512)]
        taps = K.f(130, 2 * 2 * D).rearrange("p (t n) -> p t n", t=2)
        taps2 = K.f(146, 2 * 2 * D).rearrange("p (t n) -> p t n", t=2)
        sums = K.f(146, 2 * 2 * D).rearrange("p (t n) -> p t n", t=2)
        two_pi_hi = 6.28125
        two_pi_lo = 2 * math.pi - two_pi_hi

        @block.sync
        def _(sp):
            for s in range(2):
                K.early.issue(sp, s, *hyena_tile(K, l, s, s))
            K.early.hand_over(sp, 3, consts_in)
            sp.wait_ge(consts_in, 16)

        @block.tensor
        def _(pe):
            pe.wait_ge(consts_in, 16)
            pe.matmul(K.ps[0:H_FFN, 0, 0:SEQ], w1, zT, start=True, stop=True).then_inc(layer_done, 1)
            pe.wait_ge(sin_done, 1)
            pe.matmul(K.ps[0:H_FFN, 1, 0:SEQ], w2, hid[0], start=True, stop=True).then_inc(layer_done, 1)
            pe.wait_ge(sin_done, 2)
            for tt in range(2):
                for n in range(4):
                    q = 4 * tt + n
                    if q >= 2:
                        pe.wait_ge(taps_made, q - 1)
                    t, c = slice(tt * P, tt * P + P), slice(n * 512, n * 512 + 512)
                    if q == 0:
                        pe.wait_ge(chain, 1)
                    pe.matmul(K.ps[:, 2 + q % 2, :], neg_t[:, t], delta[:, c], start=True, stop=True)
                    pe.matmul(K.ps[:, 4 + q % 2, :], hid[1][:, t], w3[:, c], start=True, stop=True).then_inc(hidden, 1)
            pe.wait_ge(acts, 4)
            for c in range(KC):
                for q in range(4):
                    last = pe.matmul(K.ps[:, 6, c:c + 1], taps2[:, q // 2, (q % 2) * D + c * P:(q % 2) * D + c * P + P],
                                     K.ones[:, 0:1], start=(q == 0), stop=(q == 3))
            last.then_inc(taps_summed, 1)
            pe.wait_ge(rn_step, 5)
            for q in range(8):
                cs, ft, half = q // 4, q // 2 % 2, q % 2
                bank = (0, 1, 2, 3, 4, 5, 7, 6)[q]
                last = accumulate(pe, K.ps[:, bank, :], lambda t: K.dft[:, cs, t, ft * P:ft * P + P],
                                  lambda t: sums[:, t, cs * D + half * 512:cs * D + half * 512 + 512], 2)
                last.then_inc(spectra_done, 1)

        @block.vector
        def _(v):
            ch = Chain(v, chain)
            v.wait_ge(consts_in, 16)
            ch.then(v.scalar_tensor_tensor(out=delta, in0=delta, scalar=-1.0, in1=delta, op0=ALU.mult, op1=ALU.max))
            for i, b in enumerate((C_FB1, C_FB2)):
                v.wait_ge(layer_done, i + 1)
                ch.then(v.tensor_scalar(arg, K.ps[0:H_FFN, i, 0:SEQ], K.cols[0:H_FFN, l, b:b + 1],
                                        K.cols[0:H_FFN, l, C_FREQ:C_FREQ + 1], ALU.add, ALU.mult))
                ch.wait()
                ch.then(v.tensor_scalar(turns_i, arg, 1.0 / (2 * math.pi), None, ALU.mult))
                ch.wait()
                ch.then(v.tensor_copy(turns, turns_i))
                ch.wait()
                for part in (two_pi_hi, two_pi_lo):
                    ch.then(v.scalar_tensor_tensor(out=arg, in0=turns, scalar=-part, in1=arg, op0=ALU.mult, op1=ALU.add))
                    ch.wait()
                for op, bound, turn in ((ALU.is_gt, math.pi, -2 * math.pi), (ALU.is_lt, -math.pi, 2 * math.pi)):
                    ch.then(v.tensor_scalar(fix, arg, bound, turn, op, ALU.mult))
                    ch.wait()
                    ch.then(v.tensor_tensor(arg, arg, fix, ALU.add))
                    ch.wait()
                v.tensor_scalar(arg, arg, 3.1415925, -3.1415925, ALU.min, ALU.max).then_inc(sin_in, 1)
                if i == 0:
                    v.wait_ge(sin_done, 1)
            for q in range(8):
                v.wait_ge(decay_done, q + 1)
                v.wait_ge(hidden, q + 1)
                v.tensor_tensor(taps[:, q // 4, (q % 4) * 512:(q % 4) * 512 + 512], K.ps[:, 4 + q % 2, :], decay[q % 2],
                                ALU.mult).then_inc(taps_made, 1)
            v.wait_ge(taps_summed, 1)
            v.tensor_scalar(K.rn, K.ps[:, 6, 0:KC], EPS, None, ALU.add).then_inc(rn_step, 1)
            v.memset(taps[0:1, 0, D:2 * D], 0.0).then_inc(rn_step, 1)
            v.wait_ge(acts, 5)
            v.wait_ge(rn_step, 2)
            v.reciprocal(K.rn, K.rn).then_inc(rn_step, 1)
            v.tensor_tensor(sums[:, :, 0:D], taps[:, :, 0:D], taps[:, :, D:2 * D], ALU.add).then_inc(rn_step, 1)
            v.tensor_tensor(sums[:, :, D:2 * D], taps[:, :, 0:D], taps[:, :, D:2 * D], ALU.subtract).then_inc(rn_step, 1)

        @block.scalar
        def _(act):
            for i in range(2):
                act.wait_ge(sin_in, i + 1)
                act.activation(hid[i], arg, ACT.Sin).then_inc(sin_done, 1)
            for q in range(8):
                act.wait_ge(hidden, q + 1)
                if q >= 2:
                    act.wait_ge(taps_made, q - 1)
                act.activation(decay[q % 2], K.ps[:, 2 + q % 2, :], ACT.Exp).then_inc(decay_done, 1)
            act.wait_ge(taps_made, 8)
            for q in range(4):
                act.activation(taps2[:, q // 2, (q % 2) * D:(q % 2) * D + D], taps[:, q // 2, (q % 2) * D:(q % 2) * D + D],
                               ACT.Square).then_inc(acts, 1)
            act.wait_ge(rn_step, 1)
            act.activation(K.rn, K.rn, ACT.Sqrt).then_inc(acts, 1)
            for q in range(8):
                cs, ft, half = q // 4, q // 2 % 2, q % 2
                bank = (0, 1, 2, 3, 4, 5, 7, 6)[q]
                act.wait_ge(spectra_done, q + 1)
                act.activation(K.spec[:, cs, ft, half * 512:half * 512 + 512], K.ps[:, bank, :], ACT.Copy).then_inc(copied, 1)
            act.wait_ge(copied, 8)


def stage_hyena(nc, K, l):
    t0, ns = spans(l)
    nt = ns * SEQ
    names = ("tile_in0", "tile_in1", "tile_used", "projected", "centred", "convolved", "z_ready", "z_turned",
             "z_copied", "analysed", "mixed", "synthesised", "descaled", "unit_out", "chain")
    with stage(nc, *names) as (tile_in0, tile_in1, tile_used, projected, centred, convolved, z_ready, z_turned,
                               z_copied, analysed, mixed, synthesised, descaled, unit_out, chain), nc.Block() as block:
        tile_in = [tile_in0, tile_in1]
        slots = [K.ring(s).rearrange("p (k c) -> p k c", k=KC) for s in range(2)]
        seqs = lambda a: a.rearrange("p (s t) -> p s t", t=SEQ)
        x0 = [K.f(100 + 2 * s, nt) for s in range(2)]
        x1 = K.f(104, nt)
        vv = K.f(106, nt)
        z = [K.f(108 + 2 * s, nt) for s in range(2)]
        ztok = K.f(112, nt).rearrange("p (t s c) -> p t s c", t=2, c=P)
        yr = K.f(114, 2 * nt // 2).rearrange("p (f s c) -> p f s c", f=2, c=P)
        yi = K.f(116, 2 * nt // 2).rearrange("p (f s c) -> p f s c", f=2, c=P)
        tmp = K.f(118, 2 * nt // 2).rearrange("p (f s c) -> p f s c", f=2, c=P)
        tmp2 = K.f(120, 2 * nt // 2).rearrange("p (f s c) -> p f s c", f=2, c=P)
        yc = K.f(122, nt)
        turned = K.ps[:, 3, 0:nt]
        zr = K.ps[:, 4, 0:nt].rearrange("p (f s c) -> p f s c", f=2, c=P)
        zi = K.ps[:, 5, 0:nt].rearrange("p (f s c) -> p f s c", f=2, c=P)
        back = K.ps[:, 6, 0:nt]
        CHAIN = 8

        def projection(j, s):
            return K.ps[:, 7 if j == 0 and s == 1 else j, 0:nt]

        @block.sync
        def _(sp):
            def load(u, s):
                sp.dma_start(*hyena_tile(K, l, u, s)).then_inc(tile_in[s], 16)
            prefetch(sp, KC, load, lambda u: sp.wait_ge(projected, u * 3 + 3), K.early, tile_in)
            for s in range(2):
                sp.wait_ge(projected, (KC - 2 + s) * 3 + 3)
                K.early.issue(sp, s, *merge_tile(K, l, 2, s, s))

        @block.tensor
        def _(pe):
            def project(u, s, j, before=None):
                if j == 0:
                    pe.wait_ge(tile_in[s], (u - s) * 8 + 16)
                if before is not None:
                    pe.wait_ge(convolved, before * 3 + j + 1)
                last = accumulate(pe, projection(j, s), lambda k: slots[s][:, k, j * P:j * P + P],
                                  lambda k: K.H[:, k, t0:], KC)
                last.then_inc(projected, 1)

            def turn(u, s):
                pe.wait_ge(z_ready, u + 1)
                pe.wait_ge(z_copied, u)
                for q in range(2 * ns):
                    last = pe.transpose(turned[:, q * P:q * P + P], z[s][:, q * P:q * P + P], K.ident)
                last.then_inc(z_turned, 1)

            def analyse(u):
                pe.wait_ge(z_copied, u + 1)
                pe.wait_ge(mixed, u * 2)
                for cs, out in enumerate((zr, zi)):
                    for ft in range(2):
                        last = accumulate(pe, out[:, ft], lambda t: K.dft[:, cs, t, ft * P:ft * P + P],
                                          lambda t: ztok[:, t], 2)
                last.then_inc(analysed, 1)

            def synthesise(u):
                pe.wait_ge(mixed, u * 2 + 2)
                pe.wait_ge(descaled, u)
                for q in range(ns):
                    last = accumulate(pe, back[:, q * SEQ:q * SEQ + SEQ],
                                      lambda f: (yr if f < 2 else yi)[:, f % 2, q, :],
                                      lambda f: K.dft[:, 2 + f // 2, f % 2, :], 4)
                last.then_inc(synthesised, 1)

            def step(u, s, more=True, first=False):
                if more:
                    project(u + 1, 1 - s, 0, None if first else u - 1)
                turn(u, s)
                if more:
                    project(u + 1, 1 - s, 1, u)
                analyse(u)
                if more:
                    project(u + 1, 1 - s, 2, u)
                synthesise(u)

            for j in range(3):
                project(0, 0, j)
            step(0, 0, first=True)
            with pe.Fori(0, KC // 2 - 1) as i:
                for s in range(1, 3):
                    step(i * 2 + s, s % 2)
            step(KC - 1, 1, more=False)

        @block.scalar
        def _(act):
            def unit(u, s):
                for j, out in enumerate((x0[s], x1, vv)):
                    act.wait_ge(projected, u * 3 + j + 1)
                    if j == 0:
                        act.wait_ge(unit_out, u + 1)
                    else:
                        act.wait_ge(z_ready, u)
                    col = u + (C_HCW + 24 + 8 * j)
                    act.activation(out, projection(j, s), ACT.Identity, scale=K.cols[:, l, bass.ds(col, 1)],
                                   bias=K.cols[:, l, bass.ds(u + (C_HCB + 8 * j), 1)]).then_inc(centred, 1)
                act.wait_ge(z_turned, u + 1)
                act.wait_ge(analysed, u)
                act.activation(ztok.rearrange("p t s c -> p s t c"),
                               turned.rearrange("p (s t c) -> p s t c", t=2, c=P), ACT.Copy).then_inc(z_copied, 1)
                act.wait_ge(synthesised, u + 1)
                act.wait_ge(unit_out, u + 2)
                act.activation(yc, back, ACT.Copy, scale=K.rn[:, bass.ds(u, 1)]).then_inc(descaled, 1)
            pairs(act, KC, unit)

        @block.vector
        def _(v):
            v.sem_inc(unit_out, 2)

            def unit(u, s):
                ch = Chain(v, chain, u * CHAIN)
                for j, out in enumerate((x0[s], x1, vv)):
                    src, dst = seqs(projection(j, s)), seqs(out)
                    v.wait_ge(centred, u * 3 + j + 1)
                    ch.then(v.scalar_tensor_tensor(out=dst[:, :, 1:], in0=src[:, :, 0:SEQ - 1],
                                                   scalar=K.cols[:, l, bass.ds(u + (C_HCW + 8 * j), 1)],
                                                   in1=dst[:, :, 1:], op0=ALU.mult, op1=ALU.add))
                    ch.wait()
                    v.scalar_tensor_tensor(out=dst[:, :, 0:SEQ - 1], in0=src[:, :, 1:],
                                           scalar=K.cols[:, l, bass.ds(u + (C_HCW + 48 + 8 * j), 1)],
                                           in1=dst[:, :, 0:SEQ - 1], op0=ALU.mult, op1=ALU.add).then_inc(convolved, 1)
                v.wait_ge(convolved, u * 3 + 3)
                v.tensor_tensor(z[s], x1, vv, ALU.mult).then_inc(z_ready, 1)
                v.wait_ge(analysed, u + 1)
                v.wait_ge(synthesised, u)
                taps = lambda cs: K.spec[:, cs, :, bass.ds(u * P, P)].rearrange("p f (s c) -> p f s c", s=1).to_broadcast([P, 2, ns, P])
                hr, hi = taps(0), taps(1)
                ch.then(v.tensor_tensor(yr, zr, hr, ALU.mult))
                ch.then(v.tensor_tensor(tmp, zi, hi, ALU.mult))
                ch.then(v.tensor_tensor(yi, zi, hr, ALU.mult))
                ch.then(v.tensor_tensor(tmp2, zr, hi, ALU.mult))
                ch.wait()
                v.tensor_tensor(yr, yr, tmp, ALU.subtract).then_inc(mixed, 1)
                v.tensor_tensor(yi, yi, tmp2, ALU.add).then_inc(mixed, 1)
                v.wait_ge(descaled, u + 1)
                ch.then(v.scalar_tensor_tensor(out=yc, in0=z[s], scalar=K.cols[:, l, bass.ds(u + C_HBIAS, 1)],
                                               in1=yc, op0=ALU.mult, op1=ALU.add))
                ch.wait()
                v.tensor_tensor(K.YB[:, bass.ds(u, 1), t0:].rearrange("p a t -> p (a t)"), yc, x0[s],
                                ALU.mult).then_inc(unit_out, 1)
                assert ch.n == CHAIN, ch.n
            pairs(v, KC, unit)


def stage_merge(nc, K, l, branch, first):
    t0, ns = spans(l)
    nt = ns * SEQ
    with stage(nc, "tile_in0", "tile_in1", "projected", "tanh_done", "gated", "merged") as (
            tile_in0, tile_in1, projected, tanh_done, gated, merged), nc.Block() as block:
        tile_in = [tile_in0, tile_in1]
        slots = [K.ring(s, KC * 256).rearrange("p (k c) -> p k c", k=KC) for s in range(2)]
        th = [K.f(190 + 2 * s, nt) for s in range(2)]

        @block.sync
        def _(sp):
            def load(u, s):
                sp.dma_start(*merge_tile(K, l, branch, u, s)).then_inc(tile_in[s], 16)
            if branch == 1:
                for dst, src in gate_consts(K, l):
                    K.early.issue(sp, 3, dst, src)
            prefetch(sp, KC, load, lambda u: sp.wait_ge(projected, u * 2 + 2), K.early, tile_in)
            for s in range(2):
                sp.wait_ge(projected, (KC - 2 + s) * 2 + 2)
                if branch != 1:
                    K.early.issue(sp, s, *(attention_tile if branch == 2 else out_tile)(K, l, s, s))

        @block.tensor
        def _(pe):
            pe.sem_inc(merged, 2)

            def unit(u, s):
                pe.wait_ge(tile_in[s], (u - s) * 8 + 16)
                pe.wait_ge(merged, u + 1)
                accumulate(pe, K.ps[:, 2 * s, 0:nt], lambda k: slots[s][:, k, P:2 * P], lambda k: K.H[:, k, t0:],
                           KC).then_inc(projected, 1)
                accumulate(pe, K.ps[:, 2 * s + 1, 0:nt], lambda k: slots[s][:, k, 0:P], lambda k: K.YB[:, k, t0:],
                           KC).then_inc(projected, 1)
            pairs(pe, KC, unit)

        @block.scalar
        def _(act):
            def unit(u, s):
                act.wait_ge(projected, u * 2 + 1)
                act.wait_ge(merged, u + 1)
                act.activation(th[s], K.ps[:, 2 * s, 0:nt], ACT.Tanh, scale=0.5,
                               bias=K.half_mb[:, l, bass.ds(u + 8 * branch, 1)]).then_inc(tanh_done, 1)
            pairs(act, KC, unit)

        @block.vector
        def _(v):
            def unit(u, s):
                y = K.Y[:, bass.ds(u, 1), t0:].rearrange("p a t -> p (a t)")
                v.wait_ge(tanh_done, u + 1)
                v.wait_ge(projected, u * 2 + 2)
                v.scalar_tensor_tensor(out=th[s], in0=th[s], scalar=1.0, in1=K.ps[:, 2 * s + 1, 0:nt], op0=ALU.add,
                                       op1=ALU.mult).then_inc(gated, 1)
                v.wait_ge(gated, u + 1)
                if first:
                    v.tensor_scalar(y, th[s], 0.5, None, ALU.mult).then_inc(merged, 1)
                else:
                    v.scalar_tensor_tensor(out=y, in0=th[s], scalar=0.5, in1=y, op0=ALU.mult,
                                           op1=ALU.add).then_inc(merged, 1)
            pairs(v, KC, unit)
            v.wait_ge(merged, KC + 2)


def stage_out(nc, K, l):
    t0, ns = spans(l)
    nt = ns * SEQ
    with stage(nc, "tile_in0", "tile_in1", "projected", "added") as (tile_in0, tile_in1, projected, added), nc.Block() as block:
        tile_in = [tile_in0, tile_in1]
        slots = [K.ring(s, KC * 256).rearrange("p (k c) -> p k c", k=KC) for s in range(2)]

        @block.sync
        def _(sp):
            def load(u, s):
                sp.dma_start(*out_tile(K, l, u, s)).then_inc(tile_in[s], 16)
            prefetch(sp, KC // 2, load, lambda u: sp.wait_ge(projected, u * 2 + 2), K.early, tile_in)
            for dst, src in moe_consts(K, l):
                K.early.issue(sp, 3, dst, src)
            for n, (dst, src) in enumerate(expert_tiles(K, l, 0, 0)):
                K.early.issue(sp, n // 2, dst, src)

        @block.tensor
        def _(pe):
            pe.sem_inc(added, 4 * ns)

            def tile(u, s):
                pe.wait_ge(tile_in[s], (u - s) * 8 + 16)
                for c in range(2):
                    pe.wait_ge(added, (u * 2 + c + 1) * ns)
                    accumulate(pe, K.ps[:, 2 * s + c, 0:nt], lambda k: slots[s][:, k, c * P:c * P + P],
                               lambda k: K.Y[:, k, t0:], KC).then_inc(projected, 1)
            pairs(pe, KC // 2, tile)

        @block.vector
        def _(v):
            def tile(u, s):
                for c in range(2):
                    v.wait_ge(projected, u * 2 + c + 1)
                    for q in range(2 - ns, 2):
                        x = K.X[:, bass.ds(u * 2 + c, 1), q * SEQ:q * SEQ + SEQ].rearrange("p a t -> p (a t)")
                        v.scalar_tensor_tensor(out=x, in0=K.ps[:, 2 * s + c, q * SEQ - t0:q * SEQ - t0 + SEQ],
                                               scalar=K.mod[:, bass.ds(u * 2 + (48 * l + G1 + c), 1), q:q + 1].rearrange("p a b -> p (a b)"),
                                               in1=x, op0=ALU.mult, op1=ALU.add).then_inc(added, 1)
            pairs(v, KC // 2, tile)
            v.wait_ge(added, ns * (KC + 4))


def stage_attention(nc, K, l):
    t0, ns = spans(l)
    nt = ns * SEQ
    lam_init = 0.8 - 0.6 * math.exp(-0.3 * l)
    qtiles = [(SEQ, NTOK), (SEQ + P, NTOK)] + ([(0, SEQ), (P, SEQ)] if ns == 2 else [])
    nq = len(qtiles)
    names = ("consts_in", "tile_in0", "tile_in1", "lam_step", "lam_sum", "q_projected", "k_projected", "v_projected",
             "squared", "v_copied", "summed", "rooted", "normed", "rotated", "roped", "scored", "maxed", "exped",
             "weighted", "turned", "copied", "mixed", "o_squared", "o_summed", "o_rooted", "unit_out", "chain", "acts",
             "q_split", "zeroed", "root_logs", "o_logs")
    with stage(nc, *names) as (consts_in, tile_in0, tile_in1, lam_step, lam_sum, q_projected, k_projected, v_projected,
                               squared, v_copied, summed, rooted, normed, rotated, roped, scored, maxed, exped,
                               weighted, turned, copied, mixed, o_squared, o_summed, o_rooted, unit_out, chain,
                               acts, q_split, zeroed, root_logs, o_logs), nc.Block() as block:
        tile_in = [tile_in0, tile_in1]
        slots = [K.ring(s).rearrange("p (k c) -> p k c", k=KC) for s in range(2)]
        rope = K.f(190, 2 * SEQ).rearrange("p (c t) -> p c t", c=2)
        sq = [K.f(100, NTOK), K.f(102, NTOK)]
        rs = [K.f(138, NTOK), K.f(140, NTOK)]
        qk = [[K.f(104 + 2 * s, NTOK) for s in range(2)], [K.f(108 + 2 * s, NTOK) for s in range(2)]]
        qz = [[K.f(149 + 4 * s + 2 * c, NTOK) for c in range(2)] for s in range(2)]
        vt = [K.f(112 + 2 * s, NTOK).rearrange("p (t d) -> p t d", d=P) for s in range(2)]
        pr = [K.f(116 + 4 * s, 2 * NTOK).rearrange("p (c k) -> p c k", c=2) for s in range(2)]
        w = [K.f(124 + 2 * s, NTOK) for s in range(2)]
        wt_lat = K.f(128, 4 * SEQ).rearrange("p (b q) -> p b q", b=4)
        wt_ctx = K.f(132, 2 * SEQ).rearrange("p (b q) -> p b q", b=2)
        st = K.f(134, 8 * nq).rearrange("p (n k c) -> p n k c", k=4, c=2)
        osq, ors = K.f(136, NTOK), K.f(142, NTOK)
        tmp = [K.f(144, SEQ), K.f(145, SEQ)]
        lam = K.f(146, 8)
        prod = K.f(147, 2)[0:A_DH, :]
        gsub = K.f(148, 1)
        widths = (nt, NTOK)
        starts = (t0, 0)
        CHAIN = 4 * nq + 4

        @block.sync
        def _(sp):
            sp.dma_start(rope, K.A["d_rope"]).then_inc(consts_in, 16)

            def load(u, s):
                sp.dma_start(*attention_tile(K, l, u, s)).then_inc(tile_in[s], 16)
            prefetch(sp, KC, load, lambda u: sp.wait_ge(k_projected, u + 1), K.early, tile_in)
            for s in range(2):
                sp.wait_ge(k_projected, KC - 1 + s)
                K.early.issue(sp, s, *merge_tile(K, l, 1, s, s))
            sp.wait_ge(consts_in, 16)

        @block.tensor
        def _(pe):
            def project_v(u, s, ts, wait=True):
                if 0 in ts:
                    pe.wait_ge(tile_in[s], (u - s) * 8 + 16)
                    if wait:
                        pe.wait_ge(v_copied, u)
                for t in ts:
                    last = accumulate(pe, K.ps[:, 2, t * P:t * P + P], lambda k: K.H[:, k, t * P:t * P + P],
                                      lambda k: slots[s][:, k, 2 * P:], KC)
                if 3 in ts:
                    last.then_inc(v_projected, 1)

            def project(j, s, ks, done):
                t = starts[j]
                for k in ks:
                    last = pe.matmul(K.ps[:, j, t:], slots[s][:, k, j * P:j * P + P], K.H[:, k, t:], start=(k == 0), stop=(k == KC - 1))
                if KC - 1 in ks:
                    last.then_inc(done, 1)

            def sums(u):
                for j in range(2):
                    pe.wait_ge(squared, u * 2 + (j + 1))
                    if j == 0:
                        pe.wait_ge(exped, u * nq)
                    pe.matmul(K.ps[:, 4 + j, starts[j]:], K.group64, sq[j][:, starts[j]:], start=True, stop=True).then_inc(summed, 1)

            def rotate(u, s):
                pe.wait_ge(normed, u * 2 + 2)
                pe.wait_ge(o_rooted, u)
                for j in range(2):
                    last = pe.matmul(K.ps[:, 3, j * SEQ:j * SEQ + SEQ], K.rot, qk[j][s][:, SEQ:], start=True, stop=True)
                last.then_inc(rotated, 1)

            def score(u, s, n):
                q0, keys = qtiles[n]
                if n == 0:
                    pe.wait_ge(roped, u * 3 + 3)
                    pe.wait_ge(q_split, u + 1)
                pe.wait_ge(exped, u * nq + n)
                for c in range(2):
                    last = pe.matmul(K.ps[:, 4 + c, 0:keys], qz[s][c][:, q0:q0 + P], qk[1][s][:, 0:keys],
                                     start=True, stop=True)
                last.then_inc(scored, 1)

            def turn(u, n):
                pe.wait_ge(weighted, u * nq + n + 1)
                pe.wait_ge(copied, u * nq + n)
                for b in range(qtiles[n][1] // P):
                    last = pe.transpose(K.ps[:, 6, b * P:b * P + P], w[n % 2][:, b * P:b * P + P], K.ident)
                last.then_inc(turned, 1)

            def mix(u, s):
                pe.wait_ge(copied, u * nq + nq)
                pe.wait_ge(unit_out, u)
                last = accumulate(pe, K.ps[:, 7, SEQ:], lambda b: vt[s][:, b, :], lambda b: wt_lat[:, b, :], 4)
                if ns == 2:
                    last = accumulate(pe, K.ps[:, 7, 0:SEQ], lambda b: vt[s][:, b, :], lambda b: wt_ctx[:, b, :], 2)
                last.then_inc(mixed, 1)

            def o_sums(u):
                pe.wait_ge(o_squared, u + 1)
                pe.wait_ge(roped, u * 3 + 3)
                pe.matmul(K.ps[:, 3, t0:], K.ones, osq[:, t0:], start=True, stop=True).then_inc(o_summed, 1)

            def step(u, s, first=False, more=True):
                v = (lambda *ts: project_v(u + 1, 1 - s, ts)) if more else (lambda *ts: None)
                q, k = (lambda *ks: project(0, 1 - s, ks, q_projected), lambda *ks: project(1, 1 - s, ks, k_projected)) if more else (
                    lambda *ks: None, lambda *ks: None)
                sums(u)
                if not first:
                    o_sums(u - 1)
                v(0, 1)
                rotate(u, s)
                v(2, 3)
                score(u, s, 0)
                pieces = [lambda: q(0, 1, 2, 3), lambda: q(4, 5, 6, 7), lambda: k(0, 1, 2, 3), lambda: k(4, 5, 6, 7)]
                for n in range(nq):
                    pieces[n]()
                    if n == nq - 1:
                        for piece in pieces[nq:]:
                            piece()
                    else:
                        score(u, s, n + 1)
                    turn(u, n)
                mix(u, s)

            pe.wait_ge(lam_step, 2)
            pe.matmul(K.ps[:, 0, 0:2], K.ones[0:A_DH, :], prod, start=True, stop=True).then_inc(lam_sum, 1)
            pe.wait_ge(acts, 1)
            project_v(0, 0, range(4), wait=False)
            project(0, 0, range(KC), q_projected)
            project(1, 0, range(KC), k_projected)
            step(0, 0, first=True)
            with pe.Fori(0, KC // 2 - 1) as i:
                for s in range(1, 3):
                    step(i * 2 + s, s % 2)
            step(KC - 1, 1, more=False)
            o_sums(KC - 1)

        @block.scalar
        def _(act):
            act.preload_act_table_set(LN_EXP)
            act.wait_ge(lam_sum, 1)
            act.activation(lam[:, 0:2], K.ps[:, 0, 0:2], ACT.Exp).then_inc(acts, 1)

            def squares(u, s):
                for j, done in enumerate((q_projected, k_projected)):
                    act.wait_ge(done, u + 1)
                    act.activation(sq[j][:, starts[j]:], K.ps[:, j, starts[j]:], ACT.Square).then_inc(squared, 1)
                act.wait_ge(v_projected, u + 1)
                act.activation(vt[s], K.ps[:, 2, :].rearrange("p (t d) -> p t d", d=P), ACT.Copy).then_inc(v_copied, 1)

            def exps(u, n):
                keys = qtiles[n][1]
                act.wait_ge(maxed, u * nq + n + 1)
                act.wait_ge(weighted, u * nq + (n - 1) if n else u * nq)
                for c in range(2):
                    last = act.activation(pr[n % 2][:, c, 0:keys], K.ps[:, 4 + c, 0:keys], ACT.Exp, scale=A_DH ** -0.5,
                                          bias=st[:, n, 0, c:c + 1], accum_out=st[:, n, 1, c:c + 1])
                last.then_inc(exped, 1)

            def copy(u, n):
                q0, keys = qtiles[n]
                act.wait_ge(turned, u * nq + n + 1)
                if n == 0:
                    act.wait_ge(mixed, u)
                wt = wt_lat if keys == NTOK else wt_ctx
                act.activation(wt[:, :, q0 % SEQ:q0 % SEQ + P],
                               K.ps[:, 6, 0:keys].rearrange("p (b q) -> p b q", q=P), ACT.Copy).then_inc(copied, 1)

            def o_root(u):
                act.wait_ge(o_summed, u + 1)
                act.wait_ge(unit_out, u)
                act.activation(ors[:, t0:], K.ps[:, 3, t0:], ACT.Ln, scale=1.0 / P, bias=K.eps).then_inc(o_logs, 1)
                act.wait_ge(o_logs, u + 1)
                act.activation(ors[:, t0:], ors[:, t0:], ACT.Exp, scale=-0.5).then_inc(o_rooted, 1)

            def step(u, s, first=False, more=True):
                for j in range(2):
                    act.wait_ge(summed, u * 2 + j + 1)
                    t = slice(starts[j], NTOK)
                    act.activation(rs[j][:, t], K.ps[:, 4 + j, t], ACT.Ln, scale=1.0 / A_DH, bias=K.eps).then_inc(root_logs, 1)
                    act.wait_ge(root_logs, u * 2 + (j + 1))
                    act.activation(rs[j][:, t], rs[j][:, t], ACT.Exp, scale=-0.5).then_inc(rooted, 1)
                if not first:
                    o_root(u - 1)
                if ns == 2:
                    act.wait_ge(normed, u * 2 + 1)
                    if first:
                        act.wait_ge(zeroed, 4)
                    for c in range(2):
                        part = slice(c * A_DH, c * A_DH + A_DH)
                        last = act.activation(qz[s][c][part, 0:SEQ], qk[0][s][part, 0:SEQ], ACT.Copy)
                    last.then_inc(q_split, 1)
                exps(u, 0)
                for n in range(1, nq):
                    exps(u, n)
                    copy(u, n - 1)
                copy(u, nq - 1)
                act.wait_ge(mixed, u + 1)
                act.activation(osq[:, t0:], K.ps[:, 7, t0:], ACT.Square).then_inc(o_squared, 1)
                if more:
                    squares(u + 1, 1 - s)

            squares(0, 0)
            step(0, 0, first=True)
            with act.Fori(0, KC // 2 - 1) as i:
                for s in range(1, 3):
                    step(i * 2 + s, s % 2)
            step(KC - 1, 1, more=False)
            o_root(KC - 1)

        @block.vector
        def _(v):
            v.tensor_tensor(prod, K.lam4[:, l, 0:4:2], K.lam4[:, l, 1:4:2], ALU.mult).then_inc(lam_step, 1)
            v.tensor_scalar(gsub, K.cols[:, l, C_SUB:C_SUB + 1], 1.0 - lam_init, None, ALU.mult).then_inc(lam_step, 1)
            v.wait_ge(acts, 1)
            v.tensor_tensor(lam[:, 2:3], lam[:, 1:2], lam[:, 0:1], ALU.subtract).then_inc(lam_step, 1)
            v.wait_ge(lam_step, 3)
            v.tensor_scalar(lam[:, 3:4], lam[:, 2:3], -lam_init, None, ALU.add).then_inc(lam_step, 1)
            v.wait_ge(lam_step, 4)
            for s in range(2):
                for c in range(2):
                    v.memset(qz[s][c][A_DH - c * A_DH:P - c * A_DH, :], 0.0).then_inc(zeroed, 1)
            v.wait_ge(consts_in, 16)

            def output(u):
                v.wait_ge(o_rooted, u + 1)
                v.scalar_tensor_tensor(out=K.YB[:, bass.ds(u, 1), t0:].rearrange("p a t -> p (a t)"), in0=K.ps[:, 7, t0:],
                                       scalar=gsub, in1=ors[:, t0:], op0=ALU.mult, op1=ALU.mult).then_inc(unit_out, 1)

            def unit(u, s, first=False):
                ch = Chain(v, chain, u * CHAIN)
                for j, g in enumerate((C_QG, C_KG)):
                    v.wait_ge(rooted, u * 2 + j + 1)
                    t = slice(starts[j], NTOK)
                    v.scalar_tensor_tensor(out=qk[j][s][:, t], in0=K.ps[:, j, t], scalar=K.cols[:, l, g:g + 1],
                                           in1=rs[j][:, t], op0=ALU.mult, op1=ALU.mult).then_inc(normed, 1)
                v.wait_ge(rotated, u + 1)
                for j in range(2):
                    lat = qk[j][s][:, SEQ:]
                    ch.then(v.tensor_tensor(tmp[j], K.ps[:, 3, j * SEQ:j * SEQ + SEQ], rope[:, 1, :], ALU.mult))
                    ch.then(v.tensor_tensor(lat, lat, rope[:, 0, :], ALU.mult))
                    ch.wait()
                    if j == 1:
                        v.tensor_tensor(lat, lat, tmp[j], ALU.add).then_inc(roped, 1)
                    else:
                        for c in range(2):
                            part = slice(c * A_DH, c * A_DH + A_DH)
                            v.tensor_tensor(qz[s][c][part, SEQ:], lat[part, :], tmp[j][part, :], ALU.add).then_inc(roped, 1)
                if ns == 1:
                    v.sem_inc(q_split, 1)
                if not first:
                    output(u - 1)
                for n, (q0, keys) in enumerate(qtiles):
                    v.wait_ge(scored, u * nq + n + 1)
                    ch.then(v.tensor_reduce(st[:, n, 2, :], K.ps[:, 4:6, 0:keys], AX.X, ALU.max))
                    ch.wait()
                    v.tensor_scalar(st[:, n, 0, :], st[:, n, 2, :], -A_DH ** -0.5, None, ALU.mult).then_inc(maxed, 1)
                    v.wait_ge(exped, u * nq + n + 1)
                    ch.then(v.reciprocal(st[:, n, 3, :], st[:, n, 1, :]))
                    ch.wait()
                    ch.then(v.tensor_tensor(st[:, n, 3, 1:2], st[:, n, 3, 1:2], lam[:, 3:4], ALU.mult))
                    if n >= 2:
                        v.wait_ge(turned, u * nq + n - 1)
                    else:
                        v.wait_ge(turned, u * nq)
                    ch.then(v.tensor_scalar(w[n % 2][:, 0:keys], pr[n % 2][:, 0, 0:keys], st[:, n, 3, 0:1], None, ALU.mult))
                    ch.wait()
                    v.scalar_tensor_tensor(out=w[n % 2][:, 0:keys], in0=pr[n % 2][:, 1, 0:keys], scalar=st[:, n, 3, 1:2],
                                           in1=w[n % 2][:, 0:keys], op0=ALU.mult, op1=ALU.add).then_inc(weighted, 1)
                assert ch.n == CHAIN, ch.n
            unit(0, 0, first=True)
            with v.Fori(0, KC // 2 - 1) as i:
                for s in range(1, 3):
                    unit(i * 2 + s, s % 2)
            unit(KC - 1, 1)
            output(KC - 1)
            v.wait_ge(unit_out, KC)


def gate_consts(K, l):
    return [(K.f(100, KC * P), K.A["d_wg"][l]), (K.f(104, 8 * P)[0:36, :].rearrange("p (r m) -> p r m", r=8), K.A["d_sel"]),
            (K.masks, K.A["d_masks"])]


def stage_gates(nc, K, l):
    names = ("weights_in", "projected", "biased", "logged", "acts", "scanned", "turned", "spread", "copied")
    with stage(nc, *names) as (weights_in, projected, biased, logged, acts, scanned, turned, spread, copied), nc.Block() as block:
        wg = K.f(100, KC * P).rearrange("p (k c) -> p k c", k=KC)
        sel = K.f(104, 8 * P)[0:36, :].rearrange("p (r m) -> p r m", r=8)
        g = K.f(108, NTOK)
        mag = K.f(110, NTOK)
        low = K.f(112, NTOK)
        B, A, M, E, zero = (K.f(114 + 2 * i, NTOK)[0:36, :] for i in range(5))

        @block.sync
        def _(sp):
            for s in range(3):
                K.early.issue(sp, s, *mlstm_tile(K, l, 0, s))
            K.early.hand_over(sp, 3, weights_in)
            sp.wait_ge(weights_in, 16)

        @block.tensor
        def _(pe):
            pe.wait_ge(weights_in, 16)
            accumulate(pe, K.ps[:, 0, :], lambda k: wg[:, k, :], lambda k: K.H[:, k, :], KC).then_inc(projected, 1)
            pe.wait_ge(scanned, 9)
            pe.wait_ge(acts, 3)
            for j, rows in enumerate((A, E)):
                for t in range(4):
                    last = pe.transpose(K.ps[:, 1, (j * 4 + t) * 36:(j * 4 + t) * 36 + 36], rows[:, t * P:t * P + P],
                                        K.ident[0:36, 0:36])
            last.then_inc(turned, 1)
            for r in range(8):
                if r >= 4:
                    pe.wait_ge(copied, r - 3)
                pe.matmul(K.ps[:, 2 + r % 4, :], sel[:, r, :], M, start=True, stop=True).then_inc(spread, 1)

        @block.scalar
        def _(act):
            act.preload_act_table_set(LN_EXP)
            act.wait_ge(biased, 3)
            act.activation(mag[64:100, :], mag[64:100, :], ACT.Exp, scale=-1.0).then_inc(acts, 1)
            act.wait_ge(acts, 1)
            act.activation(mag[64:100, :], mag[64:100, :], ACT.Ln, bias=1.0).then_inc(acts, 1)
            act.wait_ge(scanned, 9)
            act.activation(E, E, ACT.Exp, scale=-1.0).then_inc(acts, 1)
            for r in range(8):
                act.wait_ge(spread, r + 1)
                act.activation(K.neg_m[:, r, :], K.ps[:, 2 + r % 4, :], ACT.Copy).then_inc(copied, 1)
            act.wait_ge(copied, 8)

        @block.vector
        def _(v):
            v.memset(zero, 0.0).then_inc(scanned, 1)
            v.memset(B, 0.0).then_inc(scanned, 1)
            v.memset(M, 0.0).then_inc(scanned, 1)
            v.wait_ge(projected, 1)
            v.tensor_scalar(g, K.ps[:, 0, :], K.cols[:, l, C_GB:C_GB + 1], None, ALU.add).then_inc(biased, 1)
            v.wait_ge(biased, 1)
            x = g[64:100, :]
            v.scalar_tensor_tensor(out=mag[64:100, :], in0=x, scalar=-1.0, in1=x, op0=ALU.mult, op1=ALU.max).then_inc(biased, 1)
            v.tensor_scalar(low[64:100, :], x, 0.0, None, ALU.min).then_inc(biased, 1)
            v.wait_ge(biased, 3)
            v.wait_ge(acts, 2)
            v.tensor_tensor(low[0:36, :], low[64:100, :], mag[64:100, :], ALU.subtract).then_inc(logged, 1)
            v.wait_ge(logged, 1)
            v.wait_ge(scanned, 3)
            fwd, bwd, bctx, blat = slice(0, 4), slice(32, 36), slice(SEQ - 1, None, -1), slice(NTOK - 1, SEQ - 1, -1)

            def scan(out, src, other, op, sem_now):
                v.tensor_tensor_scan(out[fwd, :], src[fwd, :], other[fwd, :], 0.0, op, op).then_inc(scanned, 1)
                v.tensor_tensor_scan(out[bwd, bctx], src[bwd, bctx], other[bwd, bctx], 0.0, op, op).then_inc(scanned, 1)
                v.wait_ge(scanned, sem_now + 2)
                v.tensor_tensor_scan(out[bwd, blat], src[bwd, blat], other[bwd, blat], out[bwd, 0:1], op,
                                     op).then_inc(scanned, 1)
                v.wait_ge(scanned, sem_now + 3)
            scan(B, low[0:36, :], zero, ALU.add, 3)
            v.tensor_tensor(A, g[0:36, :], B, ALU.subtract).then_inc(logged, 1)
            v.wait_ge(logged, 2)
            v.tensor_tensor_scan(M[fwd, :], A[fwd, :], A[fwd, :], 0.0, ALU.max, ALU.max).then_inc(logged, 1)
            v.tensor_tensor_scan(M[bwd, bctx], A[bwd, bctx], A[bwd, bctx], 0.0, ALU.max, ALU.max).then_inc(logged, 1)
            v.wait_ge(logged, 4)
            v.tensor_tensor_scan(M[bwd, blat], A[bwd, blat], A[bwd, blat], M[bwd, 0:1], ALU.max, ALU.max).then_inc(scanned, 1)
            v.wait_ge(scanned, 7)
            v.tensor_tensor(E, B, M, ALU.add).then_inc(scanned, 1)
            v.wait_ge(scanned, 8)
            v.tensor_scalar(M, M, -1.0, None, ALU.mult).then_inc(scanned, 1)
            v.wait_ge(turned, 1)
            cols = K.ps[:, 1, 0:288].rearrange("p (j t r) -> p j t r", j=2, t=4)
            v.tensor_copy(K.gate_cols, cols).then_inc(logged, 1)
            v.wait_ge(logged, 5)


def stage_mlstm(nc, K, l):
    t0, ns = spans(l)
    nt = ns * SEQ
    tiles = list(range(4 - 2 * ns, 4))
    names = ("tile_a", "tile_b", "tile_c", "qk_projected", "centred", "tapped", "tanhed", "qk_ready", "v_projected",
             "v_copied", "o_projected", "o_tanhed", "o_ready", "scored", "bounded", "exped", "weighted", "summed",
             "normed", "half_tapped", "den_step", "ones_set")
    with stage(nc, *names) as (tile_a, tile_b, tile_c, qk_projected, centred, tapped, tanhed, qk_ready, v_projected,
                               v_copied, o_projected, o_tanhed, o_ready, scored, bounded, exped, weighted, summed,
                               normed, half_tapped, den_step, ones_set), nc.Block() as block:
        wa, wb = (K.ring(s).rearrange("p (k c) -> p k c", k=KC) for s in range(2))
        wc = K.ring(2, KC * 256).rearrange("p (k c) -> p k c", k=KC)
        q, k_ = (K.f(a, 2 * NTOK).rearrange("p (c t) -> p c t", c=2) for a in (186, 190))
        qk = [q, q, k_, k_]
        first = [t0, t0, 0, 0]
        th = K.f(194, NTOK)
        V = K.f(100, 4 * 257).rearrange("p (t d) -> p t d", t=4)
        U = [K.f(105 + 2 * i, NTOK) for i in range(2)]
        W = [K.f(109 + 8 * i, 4 * NTOK).rearrange("p (b t) -> p b t", b=4) for i in range(2)]
        den = K.f(125, 16)
        parts = [(b, t0 if b < 2 else SEQ) for b in range(4)]
        banks = [K.ps[:, 4, :], K.ps[:, 5, :], K.ps[:, 6, :], K.ps[:, 6, :]]

        def score_of(b, ta, tb):
            off = 0 if b < 3 else SEQ
            return banks[b][:, off + ta - parts[b][1]:off + tb - parts[b][1]]

        def sources(t, d):
            own = [b for b in range(4) if b // 2 == t // 2 and (b <= t if d == 0 else b >= t)]
            return ([0, 1] if t >= 2 else []) + own
        outs = [(t, d) for t in tiles for d in range(2)]
        NO = len(outs)

        @block.sync
        def _(sp):
            for s, sem in enumerate((tile_a, tile_b, tile_c)):
                K.early.hand_over(sp, s, sem)
            with sp.Fori(0, M_HEADS - 1) as h:
                sp.wait_ge(qk_projected, h * 4 + 3)
                sp.dma_start(*mlstm_tile(K, l, h + 1, 0)).then_inc(tile_a, 16)
                sp.wait_ge(v_projected, h + 1)
                sp.dma_start(*mlstm_tile(K, l, h + 1, 1)).then_inc(tile_b, 16)
                sp.wait_ge(o_projected, h * 2 + 2)
                sp.dma_start(*mlstm_tile(K, l, h + 1, 2)).then_inc(tile_c, 16)

        @block.tensor
        def _(pe):
            def project_qk(h, peeled=False):
                pe.wait_ge(tile_a, h * 16 + 16)
                for j in range(4):
                    if j == 3:
                        pe.wait_ge(tile_b, h * 16 + 16)
                    if not peeled:
                        pe.wait_ge(tapped, h * 4 + (j - 3))
                    w, c = ((wa, j * P), (wb, 0))[j == 3]
                    accumulate(pe, K.ps[:, j, first[j]:], lambda k: w[:, k, c:c + P], lambda k: K.H[:, k, first[j]:],
                               KC).then_inc(qk_projected, 1)

            def project_vo(h, peeled=False):
                if not peeled:
                    pe.wait_ge(normed, h * NO)
                for t in range(4):
                    last = accumulate(pe, K.ps[:, 4 + t // 2, t % 2 * 256:t % 2 * 256 + 256],
                                      lambda k: K.H[:, k, t * P:t * P + P], lambda k: wb[:, k, P:], KC)
                last.then_inc(v_projected, 1)
                pe.wait_ge(tile_c, h * 16 + 16)
                for c in range(2):
                    accumulate(pe, K.ps[:, 6 + c, t0:], lambda k: wc[:, k, c * P:c * P + P], lambda k: K.H[:, k, t0:],
                               KC).then_inc(o_projected, 1)

            def score(h):
                pe.wait_ge(qk_ready, h * 4 + 4)
                pe.wait_ge(v_copied, h * 2 + 2)
                pe.wait_ge(o_tanhed, h * 2 + 2)
                for b, ta in parts:
                    last = accumulate(pe, score_of(b, ta, NTOK), lambda c: k_[:, c, b * P:b * P + P], lambda c: q[:, c, ta:], 2)
                last.then_inc(scored, 1)

            def mix(h):
                for n, (t, d) in enumerate(outs):
                    if n == 0:
                        pe.wait_ge(weighted, h * 8 + 8)
                    if n >= 4:
                        pe.wait_ge(normed, h * NO + (n - 3))
                    src = sources(t, d)
                    bank = K.ps[:, (7, 4, 5, 6)[n % 4], 0:257]
                    accumulate(pe, bank, lambda i: W[d][:, src[i], t * P:t * P + P], lambda i: V[:, src[i], :],
                               len(src)).then_inc(summed, 1)

            pe.wait_ge(ones_set, 1)
            project_qk(0, True)
            project_vo(0, True)
            score(0)
            with pe.Fori(0, M_HEADS - 1) as h:
                project_qk(h + 1)
                mix(h)
                project_vo(h + 1)
                score(h + 1)
            mix(M_HEADS - 1)

        @block.scalar
        def _(act):
            def prepare(h, peeled=False):
                def centre(j):
                    act.wait_ge(qk_projected, h * 4 + (j + 1))
                    if j % 2 == 0 and not peeled:
                        act.wait_ge(scored, h)
                    col = h * 2 + (C_MCW + 16 + 8 * (j // 2) + j % 2)
                    act.activation(qk[j][:, j % 2, first[j]:], K.ps[:, j, first[j]:], ACT.Identity,
                                   scale=K.cols[:, l, bass.ds(col, 1)],
                                   bias=K.cols[:, l, bass.ds(h * 2 + (C_MCB + 8 * (j // 2) + j % 2), 1)]).then_inc(centred, 1)
                centre(0)
                for j in range(4):
                    if j < 3:
                        centre(j + 1)
                    act.wait_ge(tapped, h * 4 + (j + 1))
                    act.wait_ge(qk_ready, h * 4 + j)
                    act.activation(th[:, first[j]:], qk[j][:, j % 2, first[j]:], ACT.Tanh, scale=0.5).then_inc(tanhed, 1)

            def values(h, peeled=False):
                act.wait_ge(v_projected, h + 1)
                for i in range(2):
                    act.activation(V[:, 2 * i:2 * i + 2, 0:256], K.ps[:, 4 + i, :].rearrange("p (t d) -> p t d", t=2),
                                   ACT.Copy).then_inc(v_copied, 1)
                for c in range(2):
                    act.wait_ge(o_projected, h * 2 + (c + 1))
                    act.activation(K.og[:, bass.ds(h * 2 + c, 1), t0:].rearrange("p a t -> p (a t)"), K.ps[:, 6 + c, t0:],
                                   ACT.Tanh, scale=0.5).then_inc(o_tanhed, 1)

            def weights(h):
                for n in range(8):
                    d, b = n // 4, n % 4
                    u = U[n % 2]
                    a = K.gate_cols[:, 0, b, bass.ds(h + 32 * d, 1)]
                    act.wait_ge(bounded, h * 8 + (n + 1))
                    if b >= 2:
                        last = act.activation(u[:, SEQ:], u[:, SEQ:], ACT.Exp)
                    elif ns == 2:
                        act.activation(u[:, 0:SEQ], u[:, 0:SEQ], ACT.Exp)
                    if b < 2:
                        last = act.activation(u[:, SEQ:], K.neg_m[:, bass.ds(h + 4 * d, 1), SEQ:].rearrange("p a t -> p (a t)"),
                                              ACT.Exp, bias=a)
                    last.then_inc(exped, 1)

            prepare(0, True)
            values(0, True)
            weights(0)
            with act.Fori(0, M_HEADS - 1) as h:
                prepare(h + 1)
                act.wait_ge(summed, h * NO + NO)
                values(h + 1)
                weights(h + 1)

        @block.vector
        def _(v):
            v.memset(V[:, :, 256:257], 1.0).then_inc(ones_set, 1)

            def prepare(h):
                for j in range(4):
                    n = (NTOK - first[j]) // SEQ
                    src = K.ps[:, j, first[j]:].rearrange("p (s t) -> p s t", s=n)
                    dst = qk[j][:, j % 2, first[j]:].rearrange("p (s t) -> p s t", s=n)
                    tap = lambda i: K.cols[:, l, bass.ds(h * 2 + (C_MCW + 16 * i + 8 * (j // 2) + j % 2), 1)]
                    v.wait_ge(centred, h * 4 + (j + 1))
                    v.scalar_tensor_tensor(out=dst[:, :, 1:], in0=src[:, :, 0:SEQ - 1], scalar=tap(0), in1=dst[:, :, 1:],
                                           op0=ALU.mult, op1=ALU.add).then_inc(half_tapped, 1)
                    v.wait_ge(half_tapped, h * 4 + (j + 1))
                    v.scalar_tensor_tensor(out=dst[:, :, 0:SEQ - 1], in0=src[:, :, 1:], scalar=tap(2),
                                           in1=dst[:, :, 0:SEQ - 1], op0=ALU.mult, op1=ALU.add).then_inc(tapped, 1)
                    v.wait_ge(tanhed, h * 4 + (j + 1))
                    x = qk[j][:, j % 2, first[j]:]
                    v.scalar_tensor_tensor(out=x, in0=th[:, first[j]:], scalar=1.0, in1=x, op0=ALU.add,
                                           op1=ALU.mult).then_inc(qk_ready, 1)

            def weights(h):
                for c in range(2):
                    v.wait_ge(o_tanhed, h * 2 + (c + 1))
                    og = K.og[:, bass.ds(h * 2 + c, 1), t0:].rearrange("p a t -> p (a t)")
                    v.tensor_scalar(og, og, 0.5, 0.5, ALU.mult, ALU.add).then_inc(o_ready, 1)

                def bound(n):
                    d, b = n // 4, n % 4
                    ta = 0 if b < 2 else SEQ
                    if b >= 2 or ns == 2:
                        v.scalar_tensor_tensor(out=U[n % 2][:, ta:ta + SEQ],
                                               in0=K.neg_m[:, bass.ds(h + 4 * d, 1), ta:ta + SEQ].rearrange("p a t -> p (a t)"),
                                               scalar=K.gate_cols[:, 0, b, bass.ds(h + 32 * d, 1)],
                                               in1=K.masks[:, d, b % 2, :], op0=ALU.add, op1=ALU.min).then_inc(bounded, 1)
                    else:
                        v.sem_inc(bounded, 1)
                bound(0)
                for n in range(8):
                    d, b = n // 4, n % 4
                    if n < 7:
                        if n >= 1:
                            v.wait_ge(weighted, h * 8 + n)
                        bound(n + 1)
                    if n == 0:
                        v.wait_ge(scored, h + 1)
                    v.wait_ge(exped, h * 8 + (n + 1))
                    ta = parts[b][1]
                    v.scalar_tensor_tensor(out=W[d][:, b, ta:], in0=score_of(b, ta, NTOK), scalar=1.0 / 64,
                                           in1=U[n % 2][:, ta:], op0=ALU.mult, op1=ALU.mult).then_inc(weighted, 1)
                v.wait_ge(weighted, h * 8 + 8)

            def outputs(h):
                for n, (t, d) in enumerate(outs):
                    bank = K.ps[:, (7, 4, 5, 6)[n % 4], 0:257]
                    hs = K.hs[:, t, bass.ds(h, 1), :].rearrange("p a c -> p (a c)")
                    e = K.gate_cols[:, 1, t, bass.ds(h + 32 * d, 1)]
                    c = h * (3 * NO) + 3 * n
                    v.wait_ge(summed, h * NO + (n + 1))
                    dn = den[:, 2 * (n % 2):2 * (n % 2) + 1]
                    v.scalar_tensor_tensor(out=dn, in0=bank[:, 256:257], scalar=-1.0, in1=e, op0=ALU.mult,
                                           op1=ALU.max).then_inc(den_step, 1)
                    v.wait_ge(den_step, c + 1)
                    v.tensor_tensor(dn, bank[:, 256:257], dn, ALU.max).then_inc(den_step, 1)
                    v.wait_ge(den_step, c + 2)
                    v.reciprocal(den[:, 2 * (n % 2) + 1:2 * (n % 2) + 2], dn).then_inc(den_step, 1)
                    v.wait_ge(den_step, c + 3)
                    r = den[:, 2 * (n % 2) + 1:2 * (n % 2) + 2]
                    if d == 0:
                        v.tensor_scalar(hs, bank[:, 0:256], r, None, ALU.mult).then_inc(normed, 1)
                    else:
                        v.wait_ge(normed, h * NO + n)
                        v.scalar_tensor_tensor(out=hs, in0=bank[:, 0:256], scalar=r, in1=hs, op0=ALU.mult,
                                               op1=ALU.add).then_inc(normed, 1)

            prepare(0)
            weights(0)
            with v.Fori(0, M_HEADS - 1) as h:
                prepare(h + 1)
                outputs(h)
                weights(h + 1)
            outputs(M_HEADS - 1)
            v.wait_ge(normed, M_HEADS * NO)


def stage_mlstm_out(nc, K, l):
    t0, ns = spans(l)
    tiles = list(range(4 - 2 * ns, 4))
    nt = len(tiles)
    with stage(nc, "squared", "rooted", "root_step", "scaled", "turned", "unit_out") as (
            squared, rooted, root_step, scaled, turned, unit_out), nc.Block() as block:
        sums = K.f(100, 4 * nt).rearrange("p (t h) -> p t h", h=4)
        junk = K.f(101, 256)

        @block.sync
        def _(sp):
            for s in range(2):
                K.early.issue(sp, s, *merge_tile(K, l, 0, s, s))

        @block.scalar
        def _(act):
            for i, t in enumerate(tiles):
                for h in range(M_HEADS):
                    last = act.activation(junk, K.hs[:, t, h, :], ACT.Square, accum_out=sums[:, i, h:h + 1])
                    last.then_inc(squared, 1)
                    act.wait_ge(squared, i * M_HEADS + h + 1)
            act.wait_ge(root_step, 1)
            act.activation(sums, sums, ACT.Sqrt).then_inc(rooted, 1)

        @block.tensor
        def _(pe):
            for c in range(KC):
                pe.wait_ge(scaled, nt * (c // 2 + 1))
                if c >= 2:
                    pe.wait_ge(unit_out, c - 1)
                for i, t in enumerate(tiles):
                    last = pe.transpose(K.ps[:, c % 2, i * P:i * P + P], K.hs[:, t, c // 2, c % 2 * P:c % 2 * P + P], K.ident)
                last.then_inc(turned, 1)

        @block.vector
        def _(v):
            v.wait_ge(squared, nt * M_HEADS)
            v.tensor_scalar(sums, sums, 1.0 / M_DH, EPS, ALU.mult, ALU.add).then_inc(root_step, 1)
            v.wait_ge(rooted, 1)
            v.reciprocal(sums, sums).then_inc(root_step, 1)
            v.wait_ge(root_step, 2)
            for h in range(M_HEADS):
                for i, t in enumerate(tiles):
                    v.tensor_scalar(K.hs[:, t, h, :], K.hs[:, t, h, :], sums[:, i, h:h + 1], None, ALU.mult).then_inc(scaled, 1)
            for c in range(KC):
                v.wait_ge(turned, c + 1)
                v.scalar_tensor_tensor(out=K.YB[:, c, t0:], in0=K.ps[:, c % 2, 0:nt * P],
                                       scalar=K.cols[:, l, C_MN + c % 2:C_MN + c % 2 + 1], in1=K.og[:, c, t0:],
                                       op0=ALU.mult, op1=ALU.mult).then_inc(unit_out, 1)
            v.wait_ge(unit_out, KC)


def moe_consts(K, l):
    n_pairs = TOP_K * SEQ * spans(l)[1]
    return [(K.f(184, KC * 32).rearrange("p (k e) -> p k e", k=KC), K.A["d_rw"]), (K.f(185, 32), K.A["d_rb"]),
            (K.f(194, n_pairs), K.A["d_slots"][:, 0:n_pairs])]


def expert_tiles(K, l, e, s):
    up = lambda kib: K.f(kib, KC * D_EXP).rearrange("p (k f) -> p k f", k=KC)
    down = lambda kib: K.f(kib, 4 * D).rearrange("p (f d) -> p f d", f=4)
    places = (up(104 + 48 * s), up(120 + 48 * s), down(136 + 48 * s))
    return [(dst, K.A[w][l, bass.ds(e, 1)].rearrange("a (k p) f -> p (a k) f", p=P)) for dst, w in zip(places, ("e_w1", "e_w3", "e_w2"))]


def stage_moe(nc, K, l):
    t0, ns = spans(l)
    nt = ns * SEQ
    T = nt // P
    A = TOP_K * nt
    SC = A // P
    n_over = A // SLOT - 1
    names = ("consts_in", "w_in0", "w_in1", "w2_in0", "w2_in1", "logits", "exped", "routed", "counted", "h_turned",
             "h_copied", "onehot", "gathered", "sorted_", "starts_turned", "starts_ready",
             "o_in", "o_taken", "o_up", "o_tanh", "o_gated", "o_down", "o_out", "o_chain",
             "taken", "up_done", "tanh_done", "gate_step", "gated", "down_done", "stored",
             "spread", "pt_turned", "pt_copied", "y_turned", "y_copied", "combined", "added", "combine_step", "chain")
    with stage(nc, *names) as (consts_in, w_in0, w_in1, w2_in0, w2_in1, logits, exped, routed, counted, h_turned,
                               h_copied, onehot, gathered, sorted_, starts_turned, starts_ready,
                               o_in, o_taken, o_up, o_tanh, o_gated, o_down, o_out, o_chain,
                               taken, up_done, tanh_done, gate_step, gated, down_done, stored,
                               spread, pt_turned, pt_copied, y_turned, y_copied, combined, added, combine_step, chain):
        w_in, w2_in = [w_in0, w_in1], [w2_in0, w2_in1]
        w1, w3, w2 = ([expert_tiles(K, l, 0, s)[i][0] for s in range(2)] for i in range(3))
        xg = [K.f(16 + 4 * s, KC * SLOT).rearrange("p (k t) -> p k t", k=KC) for s in range(2)]
        gg = [K.f(24 + 2 * s, 4 * SLOT) for s in range(2)]
        th = [K.f(28 + 2 * s, 4 * SLOT) for s in range(2)]
        xs = K.f(32, KC * (A + SLOT)).rearrange("p (k t) -> p k t", k=KC)
        ys = K.f(68, KC * (A + SLOT)).rearrange("p (k t) -> p k t", k=KC)
        dest = K.route[:, 0:2 * T].rearrange("p (t j) -> p t j", j=2)
        wsel = K.route[:, 8:8 + 2 * T].rearrange("p (t j) -> p t j", j=2)
        ints = K.ints
        START, OVER_E, OVER_S, OVER_N = 0, 32, 48, 64

        def load_expert(sp, e, s, up_used=None, down_used=None):
            if up_used:
                up_used()
            tiles = expert_tiles(K, l, e, s)
            for dst, src in tiles[0:2]:
                sp.dma_start(dst, src).then_inc(w_in[s], 16)
            if down_used:
                down_used()
            sp.dma_start(*tiles[2]).then_inc(w2_in[s], 16)

        def up_products(pe, s, bank):
            for i, w in enumerate((w1[s], w3[s])):
                for f in range(4):
                    last = accumulate(pe, K.ps[:, bank + i, f * SLOT:f * SLOT + SLOT], lambda k: w[:, k, f * P:f * P + P], lambda k: xg[s][:, k, :], KC)
            return last

        def down_products(pe, s, bank):
            g = gg[s].rearrange("p (f t) -> p f t", f=4)
            for d in range(KC):
                last = accumulate(pe, K.ps[:, bank + d // 4, d % 4 * SLOT:d % 4 * SLOT + SLOT], lambda f: w2[s][:, f, d * P:d * P + P],
                                  lambda f: g[:, f, :], 4)
            return last

        def outputs_of(bank):
            return K.ps[:, bank:bank + 2, :].rearrange("p b (k t) -> p (b k) t", k=4)

        with nc.Block() as block:
            sb3 = lambda kib, n=32: K.f(kib, T * n).rearrange("p (t e) -> p t e", e=n)
            htok = K.f(152, T * D).rearrange("p (t d) -> p t d", t=T)
            oh = K.f(168, T * A).rearrange("p (t n) -> p t n", t=T)
            rw, rb, slot_iota = (dst for dst, _ in moe_consts(K, l))
            s_, sbias, s2, first, second, both = (sb3(185.5 + 0.5 * i) for i in range(1, 7))
            prod, destt = sb3(189), sb3(189.5)
            top8 = K.f(190, T * 4 * 8).rearrange("p (t g n) -> p t g n", g=4, n=8)
            g4 = K.f(190.5, T * 4).rearrange("p (t g) -> p t g", g=4)
            g4b = K.f(190.625, T * 4).rearrange("p (t g) -> p t g", g=4)
            gmax = K.f(190.75, T)
            t8 = K.f(191, T * 8).rearrange("p (t n) -> p t n", n=8)
            i8 = K.f(191.25, T * 8).bitcast(U32).rearrange("p (t n) -> p t n", n=8)
            i2 = K.f(191.5, T * 2).rearrange("p (t n) -> p t n", n=2)
            wsum = K.f(191.75, T)
            cnt, cum, start, nb, cumb, ovr, le = (K.f(192 + 0.125 * i, 32) for i in range(7))
            zero32 = K.f(193, 32)
            eb = K.f(193.25, 8)

            @block.sync
            def _(sp):
                K.early.hand_over(sp, 3, consts_in)
                K.early.hand_over(sp, 0, w_in0)
                sp.sem_inc(w_in0, 16)
                K.early.hand_over(sp, 1, w2_in0)

            @block.tensor
            def _(pe):
                pe.wait_ge(consts_in, 16)
                for i in range(T):
                    t = slice(t0 + i * P, t0 + i * P + P)
                    last = accumulate(pe, K.ps[:, 0, i * 32:i * 32 + 32], lambda k: K.H[:, k, t], lambda k: rw[:, k, :], KC)
                last.then_inc(logits, 1)
                for i in range(T):
                    for hf in range(2):
                        n = 2 * i + hf
                        if n >= 2:
                            pe.wait_ge(h_copied, n - 1)
                        for c in range(4):
                            k = 4 * hf + c
                            last = pe.transpose(K.ps[:, 1 + n % 2, c * P:c * P + P], K.H[:, k, t0 + i * P:t0 + i * P + P], K.ident)
                        last.then_inc(h_turned, 1)
                pe.wait_ge(routed, 1)
                for i in range(T):
                    for j in range(i + 1):
                        last = pe.matmul(K.ps[:, 3, i * 32:i * 32 + 32], K.before if j == i else K.ones, both[:, j, :],
                                         start=(j == 0), stop=(j == i))
                last = accumulate(pe, K.ps[:, 3, T * 32:T * 32 + 32], lambda j: K.ones, lambda j: both[:, j, :], T)
                last.then_inc(counted, 1)
                pe.wait_ge(starts_ready, 1)
                for j in range(2):
                    last = pe.transpose(K.ps[0:1, 0, 128 + j * P:256 + j * P], eb[:, j:j + 1], K.ident)
                last.then_inc(starts_turned, 1)
                pe.wait_ge(h_copied, 2 * T)
                pe.wait_ge(onehot, T)
                for n in range(KC * A // 512):
                    d, c = n % KC, n // KC
                    if n >= 4:
                        pe.wait_ge(gathered, n - 3)
                    accumulate(pe, K.ps[:, 4 + n % 4, :], lambda i: htok[:, i, d * P:d * P + P],
                               lambda i: oh[:, i, c * 512:c * 512 + 512], T).then_inc(sorted_, 1)

            @block.scalar
            def _(act):
                act.wait_ge(logits, 1)
                act.activation(s_, K.ps[:, 0, 0:T * 32].rearrange("p (t e) -> p t e", e=32), ACT.Exp, scale=-1.0).then_inc(exped, 1)
                for n in range(2 * T):
                    act.wait_ge(h_turned, n + 1)
                    act.activation(htok[:, n // 2, n % 2 * 512:n % 2 * 512 + 512], K.ps[:, 1 + n % 2, :], ACT.Copy).then_inc(h_copied, 1)
                for n in range(KC * A // 512):
                    d, c = n % KC, n // KC
                    act.wait_ge(sorted_, n + 1)
                    act.activation(xs[:, d, c * 512:c * 512 + 512], K.ps[:, 4 + n % 4, :], ACT.Copy).then_inc(gathered, 1)
                act.wait_ge(gathered, KC * A // 512)

            @block.vector
            def _(v):
                ch = Chain(v, chain)

                def do(ins):
                    ch.then(ins)
                    ch.wait()
                do(v.memset(zero32, 0.0))
                do(v.memset(xs[:, :, A:], 0.0))
                v.wait_ge(consts_in, 16)
                v.wait_ge(exped, 1)
                do(v.tensor_scalar(s_, s_, 1.0, None, ALU.add))
                do(v.reciprocal(s_, s_))
                do(v.tensor_tensor(sbias, s_, rb.rearrange("p (a e) -> p a e", a=1).to_broadcast([P, T, 32]), ALU.add))
                for i in range(T):
                    for g in range(N_GRP):
                        ch.then(v.max(top8[:, i, g, :], sbias[:, i, g * GRP:g * GRP + GRP]))
                ch.wait()
                do(v.tensor_tensor(g4, top8[:, :, :, 0], top8[:, :, :, 1], ALU.add))
                do(v.tensor_reduce(gmax, g4, AX.X, ALU.max))
                gm = gmax.rearrange("p (t a) -> p t a", a=1).to_broadcast([P, T, 4])
                do(v.tensor_tensor(g4, g4, gm, ALU.is_equal))
                rank = K.iota[:, 28:32]
                do(v.tensor_scalar(g4b, rank.rearrange("p (a e) -> p a e", a=1).to_broadcast([P, T, 4]), -1.0, 32.0, ALU.mult, ALU.add))
                do(v.tensor_tensor(g4, g4, g4b, ALU.mult))
                do(v.tensor_reduce(gmax, g4, AX.X, ALU.max))
                do(v.tensor_tensor(g4, g4, gm, ALU.is_equal))
                do(v.tensor_scalar(g4, g4, -1.0, 1e30, ALU.add, ALU.mult))
                do(v.tensor_tensor(s2.rearrange("p t (g e) -> p t g e", e=GRP), sbias.rearrange("p t (g e) -> p t g e", e=GRP),
                                   g4.rearrange("p t (g a) -> p t g a", a=1).to_broadcast([P, T, 4, GRP]), ALU.add))
                for i in range(T):
                    do(v.max(t8[:, i, :], s2[:, i, :]))
                    do(v.max_index(i8[:, i, :], t8[:, i, :], s2[:, i, :]))
                do(v.tensor_copy(i2, i8[:, :, 0:2]))
                io = K.iota.rearrange("p (a e) -> p a e", a=1).to_broadcast([P, T, 32])
                for j, o in enumerate((first, second)):
                    ch.then(v.tensor_tensor(o, io, i2[:, :, j:j + 1].to_broadcast([P, T, 32]), ALU.is_equal))
                ch.wait()
                v.tensor_tensor(both, first, second, ALU.add).then_inc(routed, 1)
                for j, o in enumerate((first, second)):
                    do(v.tensor_tensor(prod, o, s_, ALU.mult))
                    do(v.tensor_reduce(wsel[:, :, j:j + 1], prod, AX.X, ALU.add))
                do(v.tensor_tensor(wsum.rearrange("p (t a) -> p t a", a=1), wsel[:, :, 0:1], wsel[:, :, 1:2], ALU.add))
                do(v.reciprocal(wsum, wsum))
                do(v.tensor_tensor(wsel, wsel, wsum.rearrange("p (t a) -> p t a", a=1).to_broadcast([P, T, 2]), ALU.mult))
                v.wait_ge(counted, 1)
                do(v.tensor_copy(cnt, K.ps[:, 3, T * 32:T * 32 + 32]))
                do(v.tensor_tensor_scan(cum, cnt, zero32, 0.0, ALU.add, ALU.add))
                do(v.tensor_tensor(start, cum, cnt, ALU.subtract))
                do(v.tensor_tensor(destt, K.ps[:, 3, 0:T * 32].rearrange("p (t e) -> p t e", e=32),
                                   start.rearrange("p (a e) -> p a e", a=1).to_broadcast([P, T, 32]), ALU.add))
                for j, o in enumerate((first, second)):
                    do(v.tensor_tensor(prod, o, destt, ALU.mult))
                    do(v.tensor_reduce(dest[:, :, j:j + 1], prod, AX.X, ALU.add))
                for i in range(T):
                    do(v.tensor_scalar(oh[:, i, :], slot_iota, dest[:, i, 0:1], None, ALU.is_equal))
                    v.scalar_tensor_tensor(out=oh[:, i, :], in0=slot_iota, scalar=dest[:, i, 1:2], in1=oh[:, i, :],
                                           op0=ALU.is_equal, op1=ALU.add).then_inc(onehot, 1)
                do(v.tensor_scalar(nb, cnt, float(SLOT), None, ALU.is_gt))
                for j in range(2, nt // SLOT):
                    do(v.scalar_tensor_tensor(out=nb, in0=cnt, scalar=float(SLOT * j), in1=nb, op0=ALU.is_gt, op1=ALU.add))
                do(v.tensor_tensor_scan(cumb, nb, zero32, 0.0, ALU.add, ALU.add))
                do(v.tensor_tensor(ovr, cumb, nb, ALU.subtract))
                do(v.scalar_tensor_tensor(out=ovr, in0=ovr, scalar=-float(SLOT), in1=start, op0=ALU.mult, op1=ALU.add))
                do(v.tensor_scalar(le, cumb, K.pidx, None, ALU.is_le))
                do(v.tensor_reduce(eb[:, 0:1], le, AX.X, ALU.add))
                do(v.tensor_scalar(eb[:, 0:1], eb[:, 0:1], float(N_EXP - 1), None, ALU.min))
                do(v.tensor_scalar(le, K.iota, eb[:, 0:1], None, ALU.is_equal))
                do(v.tensor_tensor(le, le, ovr, ALU.mult))
                do(v.tensor_reduce(eb[:, 1:2], le, AX.X, ALU.add))
                do(v.tensor_scalar(eb[:, 2:3], K.pidx, float(SLOT), float(SLOT - A), ALU.mult, ALU.add))
                do(v.tensor_tensor(eb[:, 1:2], eb[:, 1:2], eb[:, 2:3], ALU.add))
                do(v.tensor_tensor(eb[:, 3:4], cumb[:, N_EXP - 1:N_EXP], K.pidx, ALU.is_gt))
                do(v.tensor_tensor(eb[:, 1:2], eb[:, 1:2], eb[:, 3:4], ALU.mult))
                v.tensor_scalar(eb[:, 1:2], eb[:, 1:2], float(A), None, ALU.add).then_inc(starts_ready, 1)
                do(v.tensor_copy(ints[:, START:START + 32], start[0:1, :]))
                do(v.tensor_copy(ints[:, OVER_N:OVER_N + 1], cumb[0:1, N_EXP - 1:N_EXP]))
                v.wait_ge(starts_turned, 1)
                do(v.tensor_copy(ints[:, OVER_E:OVER_E + 16], K.ps[0:1, 0, P:P + 16]))
                do(v.tensor_copy(ints[:, OVER_S:OVER_S + 16], K.ps[0:1, 0, 2 * P:2 * P + 16]))
                v.wait_ge(onehot, T)

        with nc.Block() as block:
            number = lambda eng: eng.value_load(ints[0:1, OVER_N:OVER_N + 1], min_val=0, max_val=n_over)

            @block.sync
            def _(sp):
                n = number(sp)
                with sp.Fori(0, n_over) as b:
                    with sp.If(n > b):
                        e = sp.value_load(ints[0:1, bass.ds(b + OVER_E, 1)], min_val=0, max_val=N_EXP - 1)
                        sp.wait_ge(o_down, b)
                        for dst, src in expert_tiles(K, l, e, 1):
                            sp.dma_start(dst, src).then_inc(o_in, 16)

            @block.vector
            def _(v):
                n = number(v)
                with v.Fori(0, n_over) as b:
                    with v.If(n > b):
                        r = v.value_load(ints[0:1, bass.ds(b + OVER_S, 1)], min_val=0, max_val=A)
                        v.wait_ge(o_up, b)
                        v.tensor_copy(xg[1], xs[:, :, bass.ds(r, SLOT)]).then_inc(o_taken, 1)
                        v.wait_ge(o_tanh, b + 1)
                        v.scalar_tensor_tensor(out=th[1], in0=th[1], scalar=1.0, in1=K.ps[:, 2, :], op0=ALU.add,
                                               op1=ALU.mult).then_inc(o_chain, 1)
                        v.wait_ge(o_chain, b + 1)
                        v.wait_ge(o_down, b)
                        v.scalar_tensor_tensor(out=gg[1], in0=th[1], scalar=0.5, in1=K.ps[:, 3, :], op0=ALU.mult,
                                               op1=ALU.mult).then_inc(o_gated, 1)

            @block.tensor
            def _(pe):
                n = number(pe)
                with pe.Fori(0, n_over) as b:
                    with pe.If(n > b):
                        pe.wait_ge(o_in, b * 48 + 48)
                        pe.wait_ge(o_taken, b + 1)
                        up_products(pe, 1, 2).then_inc(o_up, 1)
                        pe.wait_ge(o_gated, b + 1)
                        pe.wait_ge(o_out, b)
                        down_products(pe, 1, 6).then_inc(o_down, 1)

            @block.scalar
            def _(act):
                n = number(act)
                with act.Fori(0, n_over) as b:
                    with act.If(n > b):
                        r = act.value_load(ints[0:1, bass.ds(b + OVER_S, 1)], min_val=0, max_val=A)
                        act.wait_ge(o_up, b + 1)
                        act.wait_ge(o_gated, b)
                        act.activation(th[1], K.ps[:, 2, :], ACT.Tanh, scale=0.5).then_inc(o_tanh, 1)
                        act.wait_ge(o_down, b + 1)
                        act.activation(ys[:, :, bass.ds(r, SLOT)], outputs_of(6), ACT.Copy).then_inc(o_out, 1)

        with nc.Block() as block:
            @block.sync
            def _(sp):
                load_expert(sp, 1, 1)
                with sp.Fori(0, N_EXP // 2 - 1) as i:
                    for s in range(2):
                        load_expert(sp, i * 2 + (s + 2), s, lambda: sp.wait_ge(up_done, i * 2 + (s + 1)),
                                    lambda: sp.wait_ge(down_done, i * 2 + (s + 1)))

            @block.vector
            def _(v):
                def take(e, s):
                    r = v.value_load(ints[0:1, bass.ds(e + START, 1)], min_val=0, max_val=A)
                    v.tensor_copy(xg[s], xs[:, :, bass.ds(r, SLOT)]).then_inc(taken, 1)

                take(0, 0)

                def step(e, s, more=True):
                    if more:
                        v.wait_ge(up_done, e)
                        take(e + 1, 1 - s)
                    v.wait_ge(tanh_done, e + 1)
                    v.scalar_tensor_tensor(out=th[s], in0=th[s], scalar=1.0, in1=K.ps[:, 2 * s, :], op0=ALU.add,
                                           op1=ALU.mult).then_inc(gate_step, 1)
                    v.wait_ge(gate_step, e + 1)
                    v.scalar_tensor_tensor(out=gg[s], in0=th[s], scalar=0.5, in1=K.ps[:, 2 * s + 1, :], op0=ALU.mult,
                                           op1=ALU.mult).then_inc(gated, 1)
                with v.Fori(0, N_EXP // 2 - 1) as i:
                    for s in range(2):
                        step(i * 2 + s, s)
                step(N_EXP - 2, 0)
                step(N_EXP - 1, 1, more=False)

            @block.tensor
            def _(pe):
                def raise_(e, s, first=False):
                    pe.wait_ge(w_in[s], (e - s) * 16 + 32)
                    pe.wait_ge(taken, e + 1)
                    if not first:
                        pe.wait_ge(gated, e - 1)
                    up_products(pe, s, 2 * s).then_inc(up_done, 1)

                def lower(e, s):
                    pe.wait_ge(w2_in[s], (e - s) * 8 + 16)
                    pe.wait_ge(gated, e + 1)
                    pe.wait_ge(stored, e)
                    down_products(pe, s, 4 + 2 * s).then_inc(down_done, 1)

                raise_(0, 0, first=True)

                def step(e, s, more=True):
                    if more:
                        raise_(e + 1, 1 - s)
                    lower(e, s)
                with pe.Fori(0, N_EXP // 2 - 1) as i:
                    for s in range(2):
                        step(i * 2 + s, s)
                step(N_EXP - 2, 0)
                step(N_EXP - 1, 1, more=False)

            @block.scalar
            def _(act):
                act.preload_act_table(ACT.Exp)

                def up_part(e, s):
                    act.wait_ge(up_done, e + 1)
                    act.activation(th[s], K.ps[:, 2 * s, :], ACT.Tanh, scale=0.5).then_inc(tanh_done, 1)

                def step(e, s, more=True):
                    if more:
                        act.wait_ge(gated, e)
                        up_part(e + 1, 1 - s)
                    r = act.value_load(ints[0:1, bass.ds(e + START, 1)], min_val=0, max_val=A)
                    act.wait_ge(down_done, e + 1)
                    act.activation(ys[:, :, bass.ds(r, SLOT)], outputs_of(4 + 2 * s), ACT.Copy).then_inc(stored, 1)
                up_part(0, 0)
                with act.Fori(0, N_EXP // 2 - 1) as i:
                    for s in range(2):
                        step(i * 2 + s, s)
                step(N_EXP - 2, 0)
                step(N_EXP - 1, 1, more=False)
                act.wait_ge(stored, N_EXP)

        with nc.Block() as block:
            ytok = K.f(104, SC * D).rearrange("p (c d) -> p c d", c=SC)
            pt = K.f(136, SC * nt).rearrange("p (c t) -> p c t", c=SC)
            pw = K.f(152, T * A).rearrange("p (t n) -> p t n", t=T)
            half = K.f(168, A)
            slot_iota = K.f(172, A)

            @block.sync
            def _(sp):
                sp.dma_start(slot_iota, K.A["d_slots"][:, 0:A]).then_inc(consts_in, 16)

            @block.vector
            def _(v):
                v.wait_ge(consts_in, 32)
                for i in range(T):
                    if i >= 1:
                        v.wait_ge(spread, i)
                    for j, out in enumerate((pw[:, i, :], half)):
                        v.tensor_scalar(out, slot_iota, dest[:, i, j:j + 1], wsel[:, i, j:j + 1], ALU.is_equal,
                                        ALU.mult).then_inc(combine_step, 1)
                    v.wait_ge(combine_step, 2 * i + 2)
                    v.tensor_tensor(pw[:, i, :], pw[:, i, :], half, ALU.add).then_inc(spread, 1)
                for d in range(KC):
                    v.wait_ge(combined, d + 1)
                    for q in range(2 - ns, 2):
                        v.scalar_tensor_tensor(out=K.X[:, d, q * SEQ:q * SEQ + SEQ], in0=K.ps[:, 4 + d % 4, q * SEQ - t0:q * SEQ - t0 + SEQ],
                                               scalar=K.mod[:, 48 * l + G2 + d, q:q + 1], in1=K.X[:, d, q * SEQ:q * SEQ + SEQ],
                                               op0=ALU.mult, op1=ALU.add).then_inc(added, 1)
                v.wait_ge(added, KC * ns)

            @block.tensor
            def _(pe):
                for n in range(2 * SC):
                    c, hf = n // 2, n % 2
                    if n >= 2:
                        pe.wait_ge(y_copied, n - 1)
                    for k in range(4):
                        last = pe.transpose(K.ps[:, n % 2, k * P:k * P + P], ys[:, 4 * hf + k, c * P:c * P + P], K.ident)
                    last.then_inc(y_turned, 1)
                pe.wait_ge(spread, T)
                for c in range(SC):
                    if c >= 2:
                        pe.wait_ge(pt_copied, c - 1)
                    for i in range(T):
                        last = pe.transpose(K.ps[:, 2 + c % 2, i * P:i * P + P], pw[:, i, c * P:c * P + P], K.ident)
                    last.then_inc(pt_turned, 1)
                pe.wait_ge(y_copied, 2 * SC)
                pe.wait_ge(pt_copied, SC)
                for d in range(KC):
                    if d >= 4:
                        pe.wait_ge(added, (d - 3) * ns)
                    accumulate(pe, K.ps[:, 4 + d % 4, 0:nt], lambda c: ytok[:, c, d * P:d * P + P], lambda c: pt[:, c, :],
                               SC).then_inc(combined, 1)

            @block.scalar
            def _(act):
                for n in range(2 * SC):
                    act.wait_ge(y_turned, n + 1)
                    act.activation(ytok[:, n // 2, n % 2 * 512:n % 2 * 512 + 512], K.ps[:, n % 2, :], ACT.Copy).then_inc(y_copied, 1)
                for c in range(SC):
                    act.wait_ge(pt_turned, c + 1)
                    act.activation(pt[:, c, :], K.ps[:, 2 + c % 2, 0:nt], ACT.Copy).then_inc(pt_copied, 1)


def stage_result(nc, K):
    with stage(nc, "result_out") as (result_out,), nc.Block() as block:
        @block.sync
        def _(sp):
            sp.dma_start(K.A["outT"], K.X[:, :, SEQ:]).then_inc(result_out, 16)
            sp.wait_ge(result_out, 16)


def build(nc, A):
    K = Core(A)
    with ExitStack() as ctx:
        sb = lambda n, s, d=F32: ctx.enter_context(nc.sbuf_tensor(n, s, d))
        arena = sb("arena", [P, 51200])
        K.arena = arena
        K.f = lambda kib, n: arena[:, int(kib * 256):int(kib * 256) + n]
        K.i = lambda kib, n: arena[:, int(kib * 256):int(kib * 256) + n].bitcast(I32)
        K.ring = lambda s, n=3072: arena[:, (64 + 12 * s) * 256:(64 + 12 * s) * 256 + n]
        chunked = lambda kib: K.f(kib, KC * NTOK).rearrange("p (k t) -> p k t", k=KC)
        K.X, K.H, K.Y, K.YB = chunked(0), chunked(16), chunked(32), chunked(48)
        K.dft = K.f(172, 4 * 2 * SEQ).rearrange("p (c t n) -> p c t n", c=4, t=2)
        K.spec = K.f(180, 2 * 2 * D).rearrange("p (c f n) -> p c f n", c=2, f=2)
        K.neg_m = K.f(132, 8 * NTOK).rearrange("p (r t) -> p r t", r=8)
        K.gate_cols = K.f(148, 2 * 4 * 36).rearrange("p (j t r) -> p j t r", j=2, t=4)
        K.masks = K.f(150, 2 * 2 * SEQ).rearrange("p (d b t) -> p d b t", d=2, b=2)
        K.hs = K.f(154, 4 * D).rearrange("p (t h c) -> p t h c", t=4, h=M_HEADS)
        K.og = chunked(170)
        ident = sb("ident", [P, P]); K.ident = ident[:, :]
        ones = sb("ones", [P, P]); K.ones = ones[:, :]
        group64 = sb("group64", [P, P]); K.group64 = group64[:, :]
        rot = sb("rot", [P, P]); K.rot = rot[:, :]
        before = sb("before", [P, P]); K.before = before[:, :]
        iota = sb("iota", [P, 32]); K.iota = iota[:, :]
        cols = sb("cols", [P, DEPTH * N_COLS]); K.cols = cols[:, :].rearrange("p (l n) -> p l n", l=DEPTH)
        mod = sb("mod", [P, DEPTH * 48 * 2]); K.mod = mod[:, :].rearrange("p (j s) -> p j s", s=2)
        gain = sb("gain", [P, DEPTH * 2 * KC * 2]); K.gain = gain[:, :].rearrange("p (l h k s) -> p l h k s", l=DEPTH, h=2, s=2)
        hmb = sb("half_mb", [P, DEPTH * 24]); K.half_mb = hmb[:, :].rearrange("p (l n) -> p l n", l=DEPTH)
        rn = sb("rn", [P, KC]); K.rn = rn[:, :]
        eps = sb("eps", [P, 1]); K.eps = eps[:, :]
        pidx = sb("pidx", [P, 1]); K.pidx = pidx[:, :]
        route = sb("route", [P, 16]); K.route = route[:, :]
        ints = sb("ints", [1, 96], I32); K.ints = ints[:, :]
        lam4 = sb("lam4", [A_DH, DEPTH * 4]); K.lam4 = lam4[:, :].rearrange("p (l n) -> p l n", l=DEPTH)
        ps = ctx.enter_context(nc.psum_tensor("ps", [P, 8, 512], F32))
        K.ps = ps[:, :, :]

        K.early = Early(nc, 4)
        stage_modulation(nc, K)
        for l in range(DEPTH):
            stage_norm(nc, K, l, 0)
            stage_filter(nc, K, l)
            stage_hyena(nc, K, l)
            stage_merge(nc, K, l, 2, first=True)
            stage_attention(nc, K, l)
            stage_merge(nc, K, l, 1, first=False)
            stage_gates(nc, K, l)
            stage_mlstm(nc, K, l)
            stage_mlstm_out(nc, K, l)
            stage_merge(nc, K, l, 0, first=False)
            stage_out(nc, K, l)
            stage_norm(nc, K, l, 1)
            stage_moe(nc, K, l)
        stage_result(nc, K)
    return K


def tables():
    f = np.float32
    t = np.arange(SEQ)
    ang = np.pi * np.outer(t, 2 * t + 1) / (2 * SEQ)
    tiles = lambda a: a.reshape(2, P, SEQ).transpose(1, 0, 2)
    dft = np.stack([tiles(np.cos(ang)), tiles(np.sin(ang)), tiles(np.cos(ang).T / SEQ), tiles(np.sin(ang).T / SEQ)], 1)
    out = {"dft": dft.astype(f), "ident": np.eye(P, dtype=f)}
    out["group64"] = np.kron(np.eye(2), np.ones((A_DH, A_DH))).astype(f)
    r = np.zeros((P, P), f)
    for b in range(0, P, 32):
        for i in range(16):
            r[b + 16 + i, b + i] = -1
            r[b + i, b + 16 + i] = 1
    out["rot"] = r
    nf = A_DH // 4
    inv = 10000.0 ** (-np.arange(nf, dtype=f) / f(nf))
    ar, ac = np.outer(t // GRID_W, inv), np.outer(t % GRID_W, inv)
    a = np.concatenate([ar, ar, ac, ac], 1).astype(f)
    out["rope"] = np.stack([np.tile(np.cos(a).T, (2, 1)), np.tile(np.sin(a).T, (2, 1))], 1).astype(f)
    out["before"] = np.triu(np.ones((P, P), f), 1)
    out["pidx"] = np.arange(P, dtype=f)[:, None]
    out["slots"] = np.tile(np.arange(SORTED, dtype=f), (P, 1))
    out["iota"] = np.tile(np.arange(32, dtype=f), (P, 1))
    lin = np.linspace(0.0, 1.0, SEQ, dtype=f)
    bands = (H_EMB - 1) // 2
    w = (2.0 * math.pi * np.arange(SEQ, dtype=f) / f(SEQ)).astype(f)
    fr = np.linspace(1e-4, bands - 1, bands, dtype=f)
    fw = (fr[None, :] * w[:, None]).astype(f)
    out["zT"] = np.concatenate([lin[:, None], np.cos(fw), -np.sin(fw)], 1).T.astype(f)
    out["negt"] = -lin[None, :]
    s_, t_ = np.arange(SEQ).reshape(2, P).T[:, :, None], t[None, None, :]
    far = f(-30000.0)
    out["masks"] = np.stack([np.where(s_ <= t_, f(0), far), np.where(s_ >= t_, f(0), far)], 1)
    sel = np.zeros((36, 8, P), f)
    for r in range(8):
        sel[(0, 32)[r // 4] + r % 4, r, :] = 1
    out["sel"] = sel
    return out


def lay_out(inp):
    g = {k: np.asarray(v) for k, v in inp.items()}
    f = np.float32
    A = {"d_" + k: v for k, v in tables().items()}
    chan = lambda a: a.reshape(KC, P, -1).transpose(1, 0, 2)
    A["xT"] = chan(np.concatenate([g["ctx"][0], g["x"][0]], 0).T)
    A["cT"] = chan(np.stack([g["c_ctx"], g["c"][0]], 1))
    A["d_modb"] = g["mod_b"].reshape(DEPTH * 48, P).T
    tiles = lambda w, c: w.reshape(KC, P, -1, c * P).transpose(2, 1, 0, 3).reshape(-1, P, KC * c * P)
    A["d_modw"] = np.concatenate([tiles(g["mod_w"][l], 3) for l in range(DEPTH)])
    cols = np.zeros((DEPTH, P, N_COLS), f)
    for l in range(DEPTH):
        c = cols[l]
        c[:, C_N1:C_N1 + 8] = g["norm1_g"][l].reshape(-1, P).T
        c[:, C_N2:C_N2 + 8] = g["norm2_g"][l].reshape(-1, P).T
        c[:, C_MB:C_MB + 24] = g["merge_b"][l].reshape(-1, P).T
        c[:, C_MCW:C_MCW + 48] = g["m_conv_w"][l].reshape(-1, P).T
        c[:, C_MCB:C_MCB + 16] = g["m_conv_b"][l].reshape(-1, P).T
        c[:, C_HCW:C_HCW + 72] = g["h_conv_w"][l].reshape(-1, P).T
        c[:, C_HCB:C_HCB + 24] = g["h_conv_b"][l].reshape(-1, P).T
        c[:, C_HBIAS:C_HBIAS + 8] = g["h_bias"][l].reshape(-1, P).T
        c[:, C_QG] = np.concatenate([g["a_qnorm_g"][l]] * 2)
        c[:, C_KG] = np.concatenate([g["a_knorm_g"][l]] * 2)
        c[:, C_SUB] = g["a_subln_g"][l]
        c[:, C_MN:C_MN + 2] = g["m_norm_g"][l].reshape(2, P).T
        c[0:H_FFN, C_FREQ] = g["h_freq"][l]
        c[0:H_FFN, C_FB1] = g["h_ffn_b1"][l]
        c[0:H_FFN, C_FB2] = g["h_ffn_b2"][l]
        for row, src in ((0, 0), (32, 8), (64, 4), (96, 12)):
            c[row:row + 4, C_GB] = g["m_gate_b"][l][src:src + 4]
    A["d_cols"] = cols.transpose(1, 0, 2)
    A["d_lam4"] = g["a_lambda"].transpose(2, 0, 1)
    A["d_fw1"], A["d_fw2"], A["d_fw3"], A["d_delta"] = g["h_ffn_w1"], g["h_ffn_w2"], g["h_ffn_w3"], g["h_decay"]
    hyena = g["w_in"][:, :, 4 * D + 16 + 3 * D:4 * D + 16 + 6 * D].reshape(DEPTH, KC, P, 3, KC, P)
    A["d_wh"] = hyena.transpose(0, 4, 2, 1, 3, 5).reshape(DEPTH, KC, P, KC * 3 * P)
    w = g["w_in"].reshape(DEPTH, KC, P, -1)
    pick = lambda at, n: w[..., at:at + n]
    slab = lambda parts: np.concatenate(parts, -1).transpose(0, 2, 1, 3).reshape(DEPTH, P, -1)
    q0, k0, v0, o0, g0 = (i * D for i in range(5))
    aq, ak, av = (4 * D + 16 + i * D for i in range(3))
    gates = 4 * D + 16 + 6 * D
    wm = []
    for b, name in enumerate(("w_br_m", "w_br_a", "w_br_h")):
        wb = g[name].reshape(DEPTH, KC, P, D)
        wm.append(np.stack([slab([wb[..., m * P:m * P + P], pick(gates + b * D + m * P, P)]) for m in range(KC)], 1))
    A["d_wm"] = np.stack(wm, 1)
    wo = g["w_out"].reshape(DEPTH, KC, P, D)
    A["d_wo"] = np.stack([slab([wo[..., m * 256:m * 256 + 256]]) for m in range(KC // 2)], 1)
    A["d_wa"] = np.stack([slab([pick(aq + h * P, P), pick(ak + h * P, P), pick(av + h * P, P)]) for h in range(A_HEADS)], 1)
    A["d_wma"] = np.stack([np.stack([slab([pick(q0 + h * 256, 256), pick(k0 + h * 256, P)]),
                                     slab([pick(k0 + h * 256 + P, P), pick(v0 + h * 256, 256)])], 1)
                           for h in range(M_HEADS)], 1)
    A["d_wmc"] = np.stack([slab([pick(o0 + h * 256, 256)]) for h in range(M_HEADS)], 1)
    A["d_rw"] = chan(g["router_w"])
    A["d_rb"] = np.broadcast_to(g["router_b"], (P, N_EXP))
    A["e_w1"], A["e_w3"], A["e_w2"] = g["e_w1"], g["e_w3"], g["e_w2"]
    none = np.zeros((DEPTH, KC, P, 28), f)
    A["d_wg"] = slab([pick(g0, 4), none, pick(g0 + 8, 4), none, pick(g0 + 4, 4), none, pick(g0 + 12, 4), none])
    return {k: np.ascontiguousarray(v, f) for k, v in A.items()}


def kernel(**inputs):
    import concourse.bacc as bacc
    from concourse.bass_utils import run_bass_kernel_spmd

    arrays = lay_out(inputs)
    nc = bacc.Bacc("TRN2", target_bir_lowering=False, num_devices=1)
    args = {name: nc.dram_tensor("in_" + name, a.shape, F32, kind="ExternalInput").ap() for name, a in arrays.items()}
    args["outT"] = nc.dram_tensor("outT", (P, KC, SEQ), F32, kind="ExternalOutput").ap()
    build(nc, args)
    r = run_bass_kernel_spmd(nc, [{"in_" + name: a for name, a in arrays.items()}], core_ids=[0])
    out = np.asarray(r.results[0]["outT"])
    return np.ascontiguousarray(out.transpose(2, 1, 0).reshape(1, SEQ, D))
```

```python
import math
from contextlib import ExitStack, contextmanager

import numpy as np

import concourse.bass as bass
from concourse import mybir

P = 128
D = 1024
KC = D // P
SEQ = 256
NTOK = 2 * SEQ
DEPTH = 2
EPS = 1e-6
M_HEADS, M_DH = 4, 256
A_HEADS, A_DH = 8, 64
N_EXP, N_GRP, D_EXP, TOP_K = 32, 4, 512, 2
GRP = N_EXP // N_GRP
H_EMB, H_FFN = 33, 64
GRID_W = 64
SLOT = 128
SORTED = TOP_K * NTOK
SORTED_PAD = SORTED + SLOT

CUT = 104

F32 = mybir.dt.float32
I32 = mybir.dt.int32
U32 = mybir.dt.uint32
F32R = mybir.dt.float32r
ALU = mybir.AluOpType
ACT = mybir.ActivationFunctionType
AX = mybir.AxisListType
LN_EXP = "natural_log_exp_and_others"

C_N1, C_N2, C_MB = 0, 8, 16
C_MCW, C_MCB = 40, 88
C_HCW, C_HCB, C_HBIAS = 104, 176, 200
C_QG, C_KG, C_SUB, C_MN = 208, 209, 210, 211
C_FREQ, C_FB1, C_FB2, C_GB = 213, 214, 215, 216
N_COLS = 217
SH1, SC1, G1, SH2, SC2, G2 = (8 * i for i in range(6))


def pairs(eng, n, body):
    with eng.Fori(0, n // 2) as i:
        for s in range(2):
            body(i * 2 + s, s)


def prefetch(sp, n, load, free, early, tile_in):
    for s in range(2):
        early.hand_over(sp, s, tile_in[s])
    with sp.Fori(0, n // 2 - 1) as i:
        for s in range(2):
            free(i * 2 + s)
            load(i * 2 + (s + 2), s)


class Early:

    def __init__(self, nc, n):
        self.sems = [nc.alloc_semaphore(f"early_in{i}") for i in range(n)]
        self.counts = [0] * n

    def issue(self, sp, i, dst, src):
        sp.dma_start(dst, src).then_inc(self.sems[i], 16)
        self.counts[i] += 16

    def hand_over(self, sp, i, sem):
        sp.wait_ge(self.sems[i], self.counts[i])
        sp.sem_inc(sem, 16)


class Chain:

    def __init__(self, eng, sem, base=0):
        self.eng, self.sem, self.base, self.n = eng, sem, base, 0

    def then(self, ins):
        ins.then_inc(self.sem, 1)
        self.n += 1

    def wait(self):
        self.eng.wait_ge(self.sem, self.base + self.n)


class Core:

    def __init__(self, A):
        self.A = A


@contextmanager
def stage(nc, *names):
    sems = [nc.alloc_semaphore(name) for name in names]
    yield sems
    for s in sems:
        nc.sync.sem_clear(s)
    nc.all_engine_barrier()
    for s in sems:
        nc.release_semaphore(s)


def accumulate(pe, out, lhs, rhs, n):
    for k in range(n):
        last = pe.matmul(out, lhs(k), rhs(k), start=(k == 0), stop=(k == n - 1))
    return last


def hyena_tile(K, l, u, s):
    return K.ring(s), K.A["d_wh"][l, bass.ds(u, 1)].rearrange("a p n -> p (a n)")


def merge_tile(K, l, branch, u, s):
    return K.ring(s, KC * 256), K.A["d_wm"][l, branch, bass.ds(u, 1)].rearrange("a p n -> p (a n)")


def out_tile(K, l, u, s):
    return K.ring(s, KC * 256), K.A["d_wo"][l, bass.ds(u, 1)].rearrange("a p n -> p (a n)")


def attention_tile(K, l, u, s):
    return K.ring(s), K.A["d_wa"][l, bass.ds(u, 1)].rearrange("a p n -> p (a n)")


def mlstm_tile(K, l, h, s):
    if s < 2:
        return K.ring(s), K.A["d_wma"][l, bass.ds(h, 1), s].rearrange("a p n -> p (a n)")
    return K.ring(2, KC * 256), K.A["d_wmc"][l, bass.ds(h, 1)].rearrange("a p n -> p (a n)")


def mod_tile(K, u, s):
    return K.ring(s) if s < 3 else K.f(48, 3072), K.A["d_modw"][bass.ds(u, 1)].rearrange("a p n -> p (a n)")


def spans(l):
    return (0, 2) if l < DEPTH - 1 else (SEQ, 1)


def stage_modulation(nc, K):
    WIDE = 48
    SLOTS = 4
    names = ["cond_in", "constants_in", "ones_set", "tanh_done", "silu_done", "projected", "copied", "mod_done"] + [f"tile_in{s}" for s in range(SLOTS)]
    with stage(nc, *names) as (cond_in, constants_in, ones_set, tanh_done, silu_done, projected, copied, mod_done, *tile_in), nc.Block() as block:
        cT = K.f(60, KC * 2).rearrange("p (k s) -> p k s", s=2)
        th = K.f(60.25, KC * 2).rearrange("p (k s) -> p k s", s=2)
        modb = K.f(60.5, 96)
        sil = K.f(61, KC * 2 * WIDE).rearrange("p (k n) -> p k n", k=KC)
        slots = [mod_tile(K, 0, s)[0] for s in range(SLOTS)]
        n_tiles = DEPTH * 16
        CH = 3

        @block.sync
        def _(sp):
            sp.dma_start(cT, K.A["cT"]).then_inc(cond_in, 16)
            sp.dma_start(modb, K.A["d_modb"]).then_inc(cond_in, 16)

            def load(u, s):
                sp.dma_start(*mod_tile(K, u, s)).then_inc(tile_in[s], 16)
            for s in range(SLOTS):
                load(s, s)
            constants = [(K.X[:, :, :], K.A["xT"]), (K.ident, K.A["d_ident"]), (K.group64, K.A["d_group64"]),
                         (K.rot, K.A["d_rot"]), (K.before, K.A["d_before"]), (K.iota, K.A["d_iota"]),
                         (K.cols, K.A["d_cols"]), (K.lam4, K.A["d_lam4"]), (K.pidx, K.A["d_pidx"])]
            for dst, src in constants:
                sp.dma_start(dst, src).then_inc(constants_in, 16)
            with sp.Fori(0, n_tiles // SLOTS - 1) as i:
                for s in range(SLOTS):
                    sp.wait_ge(projected, i * SLOTS + (s + 1))
                    load(i * SLOTS + (s + SLOTS), s)
            for dst, src in filter_consts(K, 0):
                K.early.issue(sp, 3, dst, src)
            sp.wait_ge(constants_in, 16 * len(constants))

        @block.scalar
        def _(act):
            act.wait_ge(cond_in, 32)
            act.activation(th, cT, ACT.Tanh, scale=0.5).then_inc(tanh_done, 1)

        @block.vector
        def _(v):
            v.wait_ge(tanh_done, 1)
            v.scalar_tensor_tensor(out=th, in0=th, scalar=1.0, in1=cT, op0=ALU.add, op1=ALU.mult).then_inc(silu_done, 1)
            v.wait_ge(silu_done, 1)
            v.tensor_scalar(sil.rearrange("p k (s n) -> p (k s) n", s=2),
                            th.rearrange("p k (s a) -> p (k s) a", a=1).to_broadcast([P, 2 * KC, WIDE]), 0.5, None,
                            ALU.mult).then_inc(silu_done, 1)
            v.memset(K.ones, 1.0).then_inc(ones_set, 1)
            v.memset(K.half_mb, 0.0).then_inc(ones_set, 1)
            v.memset(K.eps, EPS).then_inc(ones_set, 1)

            def tile(u, s):
                v.wait_ge(projected, u + 1)
                v.tensor_copy(K.mod[:, bass.ds(u * CH, CH), :],
                              K.ps[:, s, 0:CH * 2 * WIDE].rearrange("p (j s n) -> p j s n", s=2, n=WIDE)[:, :, :, 0]).then_inc(copied, 1)
            pairs(v, n_tiles, tile)
            v.wait_ge(ones_set, 3)
            v.wait_ge(constants_in, 16 * 9)
            for l in range(DEPTH):
                v.tensor_scalar(K.half_mb[:, l, :], K.cols[:, l, C_MB:C_MB + 24], 0.5, None, ALU.mult).then_inc(ones_set, 1)
            v.wait_ge(copied, n_tiles + 2)
            for s in range(2):
                v.tensor_tensor(K.mod[:, :, s], K.mod[:, :, s], modb, ALU.add).then_inc(mod_done, 1)
            v.wait_ge(mod_done, 2)
            for l in range(DEPTH):
                for i, (sc, g) in enumerate(((SC1, C_N1), (SC2, C_N2))):
                    for s in range(2):
                        v.scalar_tensor_tensor(out=K.gain[:, l, i, :, s], in0=K.mod[:, 48 * l + sc:48 * l + sc + KC, s],
                                               scalar=1.0, in1=K.cols[:, l, g:g + KC], op0=ALU.add,
                                               op1=ALU.mult).then_inc(mod_done, 1)
            v.wait_ge(mod_done, 2 + 4 * DEPTH)

        @block.tensor
        def _(pe):
            pe.wait_ge(silu_done, 2)
            pe.sem_inc(copied, 2)
            with pe.Fori(0, n_tiles // SLOTS) as i:
                for s in range(SLOTS):
                    u = i * SLOTS + s
                    pe.wait_ge(tile_in[s], i * 16 + 16)
                    pe.wait_ge(copied, u + 1)
                    w = slots[s].rearrange("p (k c) -> p k c", k=KC)
                    for c in range(CH):
                        last = accumulate(pe, K.ps[:, s % 2, c * 2 * WIDE:(c + 1) * 2 * WIDE],
                                          lambda k: w[:, k, c * P:c * P + P], lambda k: sil[:, k, :], KC)
                    last.then_inc(projected, 1)


def stage_norm2(nc, K, l):
    half = 1
    t0, ns = spans(l)
    nt = ns * SEQ
    with stage(nc, "meaned", "rooted", "rstd_done", "scaled", "normed") as (
            meaned, rooted, rstd_done, scaled, normed), nc.Block() as block:
        total = K.ps[:, 4, t0:NTOK]
        rstd = K.f(198, NTOK)[:, t0:NTOK]

        @block.scalar
        def _(act):
            act.wait_ge(meaned, 1)
            act.activation(rstd, rstd, ACT.Sqrt).then_inc(rooted, 1)
            for k in range(KC):
                act.wait_ge(scaled, k + 1)
                for s in range(2 - ns, 2):
                    t = slice(s * SEQ, s * SEQ + SEQ)
                    act.activation(K.H[:, k, t], K.H[:, k, t], ACT.Identity, scale=K.gain[:, l, half, k, s:s + 1],
                                   bias=K.mod[:, 48 * l + SH2 + k, s:s + 1]).then_inc(normed, 1)
            act.wait_ge(normed, KC * ns)

        @block.vector
        def _(v):
            v.tensor_scalar(rstd, total, 1.0 / D, EPS, ALU.mult, ALU.add).then_inc(meaned, 1)
            v.wait_ge(rooted, 1)
            v.reciprocal(rstd, rstd).then_inc(rstd_done, 1)
            v.wait_ge(rstd_done, 1)
            for k in range(KC):
                v.tensor_tensor(K.H[:, k, t0:], K.X[:, k, t0:], rstd, ALU.mult).then_inc(scaled, 1)


def filter_consts(K, l):
    A = K.A
    return [(K.f(180, SEQ)[0:H_EMB, :], A["d_zT"]), (K.f(181, H_FFN)[0:H_EMB, :], A["d_fw1"][l]),
            (K.f(181.25, H_FFN)[0:H_FFN, :], A["d_fw2"][l]), (K.f(181.5, 2), A["d_negt"]),
            (K.f(182, 2 * D)[0:H_FFN, :], A["d_fw3"][l]), (K.f(190, 2 * D), A["d_delta"][l]),
            (K.dft, A["d_dft"])]


def stage_norm_filter(nc, K, l):
    names = ("consts_in", "layer_done", "sin_in", "sin_done", "decay_done", "taps_made", "taps_summed", "rn_step",
             "spectra_done", "copied", "chain", "acts", "hidden", "padded", "x_squared", "x_summed", "meaned", "rooted", "rstd_done",
             "scaled", "h_done")
    with stage(nc, *names) as (consts_in, layer_done, sin_in, sin_done, decay_done, taps_made, taps_summed, rn_step,
                               spectra_done, copied, chain, acts, hidden, padded, x_squared, x_summed, meaned, rooted, rstd_done,
                               scaled, h_done), nc.Block() as block:
        zT, w1, w2, neg_t, w3, delta, _ = (dst for dst, _ in filter_consts(K, l))
        delta_step = 10
        total = K.ps[:, 7, :]
        rstd = K.f(198, NTOK)
        arg = K.f(120, SEQ)[0:H_FFN, :]
        turns_i = K.i(121, SEQ)[0:H_FFN, :]
        turns = K.f(122, SEQ)[0:H_FFN, :]
        hid = [K.f(123, SEQ)[0:H_FFN, :], K.f(124, SEQ)[0:H_FFN, :]]
        hid_all, w3_all = K.f(124, SEQ), K.f(182, 2 * D)
        fix = K.f(125, SEQ)[0:H_FFN, :]
        decay = [K.f(126, 512), K.f(128, 512)]
        taps = K.f(130, 2 * 2 * D).rearrange("p (t n) -> p t n", t=2)
        taps2 = K.f(146, 2 * 2 * D).rearrange("p (t n) -> p t n", t=2)
        sums = K.f(146, 2 * 2 * D).rearrange("p (t n) -> p t n", t=2)
        two_pi_hi = 6.28125
        two_pi_lo = 2 * math.pi - two_pi_hi

        @block.sync
        def _(sp):
            for s in range(2):
                K.early.issue(sp, s, *hyena_tile(K, l, s, s))
            K.early.hand_over(sp, 3, consts_in)
            sp.wait_ge(consts_in, 16)

        @block.tensor
        def _(pe):
            pe.wait_ge(consts_in, 16)
            pe.matmul(K.ps[0:H_FFN, 0, 0:SEQ], w1, zT, start=True, stop=True).then_inc(layer_done, 1)
            for k in range(KC):
                pe.wait_ge(x_squared, k + 1)
                last = pe.matmul(total, K.ones, K.H[:, k, :], start=(k == 0), stop=(k == KC - 1))
            last.then_inc(x_summed, 1)
            pe.wait_ge(sin_done, 1)
            pe.matmul(K.ps[0:H_FFN, 1, 0:SEQ], w2, hid[0], start=True, stop=True).then_inc(layer_done, 1)
            pe.wait_ge(sin_done, 2)
            pe.wait_ge(padded, 2)
            for tt in range(2):
                for n in range(4):
                    q = 4 * tt + n
                    if q >= 4:
                        pe.wait_ge(taps_made, q - 3)
                    t, c = slice(tt * P, tt * P + P), slice(n * 512, n * 512 + 512)
                    pe.matmul(K.ps[:, 2 + q % 4, :], hid_all[:, t], w3_all[:, c], start=True, stop=True).then_inc(hidden, 1)
            pe.wait_ge(acts, 4)
            for c in range(KC):
                for q in range(4):
                    last = pe.matmul(K.ps[:, 6 - c // 4, c % 4 * P:c % 4 * P + P], taps2[:, q // 2, (q % 2) * D + c * P:(q % 2) * D + c * P + P],
                                     K.ones, start=(q == 0), stop=(q == 3))
            last.then_inc(taps_summed, 1)
            pe.wait_ge(rn_step, 5)
            pe.wait_ge(meaned, 1)
            for q in range(8):
                cs, ft, half = q // 4, q // 2 % 2, q % 2
                bank = (0, 1, 2, 3, 4, 5, 7, 6)[q]
                last = accumulate(pe, K.ps[:, bank, :], lambda t: K.dft[:, cs, t, ft * P:ft * P + P],
                                  lambda t: sums[:, t, cs * D + half * 512:cs * D + half * 512 + 512], 2)
                last.then_inc(spectra_done, 1)

        @block.vector
        def _(v):
            ch = Chain(v, chain)
            v.wait_ge(consts_in, 16)
            v.memset(hid_all[H_FFN:, :], 0.0).then_inc(padded, 1)
            v.memset(w3_all[H_FFN:, :], 0.0).then_inc(padded, 1)
            for i, b in enumerate((C_FB1, C_FB2)):
                v.wait_ge(layer_done, i + 1)
                ch.then(v.tensor_scalar(arg, K.ps[0:H_FFN, i, 0:SEQ], K.cols[0:H_FFN, l, b:b + 1],
                                        K.cols[0:H_FFN, l, C_FREQ:C_FREQ + 1], ALU.add, ALU.mult))
                ch.wait()
                ch.then(v.tensor_scalar(turns_i, arg, 1.0 / (2 * math.pi), None, ALU.mult))
                ch.wait()
                ch.then(v.tensor_copy(turns, turns_i))
                ch.wait()
                for part in (two_pi_hi, two_pi_lo):
                    ch.then(v.scalar_tensor_tensor(out=arg, in0=turns, scalar=-part, in1=arg, op0=ALU.mult, op1=ALU.add))
                    ch.wait()
                for op, bound, turn in ((ALU.is_gt, math.pi, -2 * math.pi), (ALU.is_lt, -math.pi, 2 * math.pi)):
                    ch.then(v.tensor_scalar(fix, arg, bound, turn, op, ALU.mult))
                    ch.wait()
                    ch.then(v.tensor_tensor(arg, arg, fix, ALU.add))
                    ch.wait()
                v.tensor_scalar(arg, arg, 3.1415925, -3.1415925, ALU.min, ALU.max).then_inc(sin_in, 1)
                if i == 0:
                    v.wait_ge(x_summed, 1)
                    v.tensor_scalar(rstd, total, 1.0 / D, EPS, ALU.mult, ALU.add).then_inc(meaned, 1)
                    v.scalar_tensor_tensor(out=delta, in0=delta, scalar=-1.0, in1=delta, op0=ALU.mult, op1=ALU.max).then_inc(chain, 1)
                    ch.n += 1
                    v.wait_ge(sin_done, 1)
            v.wait_ge(rooted, 1)
            v.reciprocal(rstd, rstd).then_inc(rstd_done, 1)
            v.wait_ge(rstd_done, 1)
            for q in range(8):
                v.wait_ge(decay_done, q + 1)
                v.wait_ge(hidden, q + 1)
                v.tensor_tensor(taps[:, q // 4, (q % 4) * 512:(q % 4) * 512 + 512], K.ps[:, 2 + q % 4, :], decay[q % 2],
                                ALU.mult).then_inc(taps_made, 1)
            for k in range(KC):
                v.tensor_tensor(K.H[:, k, :], K.X[:, k, :], rstd, ALU.mult).then_inc(scaled, 1)
            v.wait_ge(taps_summed, 1)
            for i in range(2):
                v.tensor_scalar(K.rn[:, 4 * i:4 * i + 4], K.ps[:, 6 - i, :].rearrange("p (c n) -> p c n", n=P)[:, :, 0], EPS, None,
                                ALU.add).then_inc(rn_step, 1)
            v.memset(taps[0:1, 0, D:2 * D], 0.0).then_inc(rn_step, 1)
            v.wait_ge(rn_step, 3)
            v.tensor_tensor(sums[:, :, 0:D], taps[:, :, 0:D], taps[:, :, D:2 * D], ALU.add).then_inc(rn_step, 1)
            v.tensor_tensor(sums[:, :, D:2 * D], taps[:, :, 0:D], taps[:, :, D:2 * D], ALU.subtract).then_inc(rn_step, 1)
            v.wait_ge(acts, 5)
            v.reciprocal(K.rn, K.rn).then_inc(rn_step, 1)
            v.wait_ge(rn_step, 6)

        @block.scalar
        def _(act):
            for k in range(KC):
                act.activation(K.H[:, k, :], K.X[:, k, :], ACT.Square).then_inc(x_squared, 1)
            for i in range(2):
                act.wait_ge(sin_in, i + 1)
                act.activation(hid[i], arg, ACT.Sin).then_inc(sin_done, 1)
            act.wait_ge(meaned, 1)
            act.activation(rstd, rstd, ACT.Sqrt).then_inc(rooted, 1)
            act.wait_ge(chain, delta_step)
            for q in range(8):
                if q >= 2:
                    act.wait_ge(taps_made, q - 1)
                act.activation(decay[q % 2], delta[:, (q % 4) * 512:(q % 4) * 512 + 512], ACT.Exp,
                               scale=neg_t[:, q // 4:q // 4 + 1]).then_inc(decay_done, 1)
            act.wait_ge(taps_made, 8)
            for q in range(4):
                act.activation(taps2[:, q // 2, (q % 2) * D:(q % 2) * D + D], taps[:, q // 2, (q % 2) * D:(q % 2) * D + D],
                               ACT.Square).then_inc(acts, 1)

            def shift(k):
                act.wait_ge(scaled, k + 1)
                for s in range(2):
                    t = slice(s * SEQ, s * SEQ + SEQ)
                    act.activation(K.H[:, k, t], K.H[:, k, t], ACT.Identity, scale=K.gain[:, l, 0, k, s:s + 1],
                                   bias=K.mod[:, 48 * l + SH1 + k, s:s + 1]).then_inc(h_done, 1)
            for k in range(4):
                shift(k)
            act.wait_ge(rn_step, 2)
            act.activation(K.rn, K.rn, ACT.Sqrt).then_inc(acts, 1)
            for k in range(4, KC):
                shift(k)
            for q in range(8):
                cs, ft, half = q // 4, q // 2 % 2, q % 2
                bank = (0, 1, 2, 3, 4, 5, 7, 6)[q]
                act.wait_ge(spectra_done, q + 1)
                act.activation(K.spec[:, cs, ft, half * 512:half * 512 + 512], K.ps[:, bank, :], ACT.Copy).then_inc(copied, 1)
            act.wait_ge(copied, 8)
            act.wait_ge(h_done, 2 * KC)


def stage_hyena(nc, K, l):
    t0, ns = spans(l)
    nt = ns * SEQ
    names = ("tile_in0", "tile_in1", "tile_used", "projected", "centred", "convolved", "z_ready", "z_turned",
             "z_copied", "analysed", "mixed", "synthesised", "descaled", "unit_out", "chain")
    with stage(nc, *names) as (tile_in0, tile_in1, tile_used, projected, centred, convolved, z_ready, z_turned,
                               z_copied, analysed, mixed, synthesised, descaled, unit_out, chain), nc.Block() as block:
        tile_in = [tile_in0, tile_in1]
        slots = [K.ring(s).rearrange("p (k c) -> p k c", k=KC) for s in range(2)]
        seqs = lambda a: a.rearrange("p (s t) -> p s t", t=SEQ)
        x0 = [K.f(100 + 2 * s, nt) for s in range(2)]
        x1 = K.f(104, nt)
        vv = K.f(106, nt)
        z = [K.f(108 + 2 * s, nt) for s in range(2)]
        ztok = K.f(112, nt).rearrange("p (t s c) -> p t s c", t=2, c=P)
        yr = K.f(114, 2 * nt // 2).rearrange("p (f s c) -> p f s c", f=2, c=P)
        yi = K.f(116, 2 * nt // 2).rearrange("p (f s c) -> p f s c", f=2, c=P)
        tmp = K.f(118, 2 * nt // 2).rearrange("p (f s c) -> p f s c", f=2, c=P)
        tmp2 = K.f(120, 2 * nt // 2).rearrange("p (f s c) -> p f s c", f=2, c=P)
        yc = K.f(122, nt)
        turned = K.ps[:, 3, 0:nt]
        zr = K.ps[:, 4, 0:nt].rearrange("p (f s c) -> p f s c", f=2, c=P)
        zi = K.ps[:, 5, 0:nt].rearrange("p (f s c) -> p f s c", f=2, c=P)
        back = K.ps[:, 6, 0:nt]
        CHAIN = 8

        def projection(j, s):
            return K.ps[:, 7 if j == 0 and s == 1 else j, 0:nt]

        @block.sync
        def _(sp):
            def load(u, s):
                sp.dma_start(*hyena_tile(K, l, u, s)).then_inc(tile_in[s], 16)
            prefetch(sp, KC, load, lambda u: sp.wait_ge(projected, u * 3 + 3), K.early, tile_in)
            for s in range(2):
                sp.wait_ge(projected, (KC - 2 + s) * 3 + 3)
                K.early.issue(sp, s, *merge_tile(K, l, 2, s, s))

        @block.tensor
        def _(pe):
            def project(u, s, j, before=None):
                if j == 0:
                    pe.wait_ge(tile_in[s], (u - s) * 8 + 16)
                if before is not None:
                    pe.wait_ge(convolved, before * 3 + j + 1)
                last = accumulate(pe, projection(j, s), lambda k: slots[s][:, k, j * P:j * P + P],
                                  lambda k: K.H[:, k, t0:], KC)
                last.then_inc(projected, 1)

            def turn(u, s):
                pe.wait_ge(z_ready, u + 1)
                pe.wait_ge(z_copied, u)
                for q in range(2 * ns):
                    last = pe.transpose(turned[:, q * P:q * P + P], z[s][:, q * P:q * P + P], K.ident)
                last.then_inc(z_turned, 1)

            def analyse(u):
                pe.wait_ge(z_copied, u + 1)
                pe.wait_ge(mixed, u * 2)
                for cs, out in enumerate((zr, zi)):
                    for ft in range(2):
                        last = accumulate(pe, out[:, ft], lambda t: K.dft[:, cs, t, ft * P:ft * P + P],
                                          lambda t: ztok[:, t], 2)
                last.then_inc(analysed, 1)

            def synthesise(u):
                pe.wait_ge(mixed, u * 2 + 2)
                pe.wait_ge(descaled, u)
                for q in range(ns):
                    last = accumulate(pe, back[:, q * SEQ:q * SEQ + SEQ],
                                      lambda f: (yr if f < 2 else yi)[:, f % 2, q, :],
                                      lambda f: K.dft[:, 2 + f // 2, f % 2, :], 4)
                last.then_inc(synthesised, 1)

            def step(u, s, more=True, first=False):
                if more:
                    project(u + 1, 1 - s, 0, None if first else u - 1)
                turn(u, s)
                if more:
                    project(u + 1, 1 - s, 1, u)
                analyse(u)
                if more:
                    project(u + 1, 1 - s, 2, u)
                synthesise(u)

            for j in range(3):
                project(0, 0, j)
            step(0, 0, first=True)
            with pe.Fori(0, KC // 2 - 1) as i:
                for s in range(1, 3):
                    step(i * 2 + s, s % 2)
            step(KC - 1, 1, more=False)

        @block.scalar
        def _(act):
            def unit(u, s):
                for j, out in enumerate((x0[s], x1, vv)):
                    act.wait_ge(projected, u * 3 + j + 1)
                    if j == 0:
                        act.wait_ge(unit_out, u + 1)
                    else:
                        act.wait_ge(z_ready, u)
                    col = u + (C_HCW + 24 + 8 * j)
                    act.activation(out, projection(j, s), ACT.Identity, scale=K.cols[:, l, bass.ds(col, 1)],
                                   bias=K.cols[:, l, bass.ds(u + (C_HCB + 8 * j), 1)]).then_inc(centred, 1)
                act.wait_ge(z_turned, u + 1)
                act.wait_ge(analysed, u)
                act.activation(ztok.rearrange("p t s c -> p s t c"),
                               turned.rearrange("p (s t c) -> p s t c", t=2, c=P), ACT.Copy).then_inc(z_copied, 1)
                act.wait_ge(synthesised, u + 1)
                act.wait_ge(unit_out, u + 2)
                act.activation(yc, back, ACT.Copy, scale=K.rn[:, bass.ds(u, 1)]).then_inc(descaled, 1)
            pairs(act, KC, unit)

        @block.vector
        def _(v):
            v.sem_inc(unit_out, 2)

            def unit(u, s):
                ch = Chain(v, chain, u * CHAIN)
                for j, out in enumerate((x0[s], x1, vv)):
                    src, dst = seqs(projection(j, s)), seqs(out)
                    v.wait_ge(centred, u * 3 + j + 1)
                    ch.then(v.scalar_tensor_tensor(out=dst[:, :, 1:], in0=src[:, :, 0:SEQ - 1],
                                                   scalar=K.cols[:, l, bass.ds(u + (C_HCW + 8 * j), 1)],
                                                   in1=dst[:, :, 1:], op0=ALU.mult, op1=ALU.add))
                    ch.wait()
                    v.scalar_tensor_tensor(out=dst[:, :, 0:SEQ - 1], in0=src[:, :, 1:],
                                           scalar=K.cols[:, l, bass.ds(u + (C_HCW + 48 + 8 * j), 1)],
                                           in1=dst[:, :, 0:SEQ - 1], op0=ALU.mult, op1=ALU.add).then_inc(convolved, 1)
                v.wait_ge(convolved, u * 3 + 3)
                v.tensor_tensor(z[s], x1, vv, ALU.mult).then_inc(z_ready, 1)
                v.wait_ge(analysed, u + 1)
                v.wait_ge(synthesised, u)
                taps = lambda cs: K.spec[:, cs, :, bass.ds(u * P, P)].rearrange("p f (s c) -> p f s c", s=1).to_broadcast([P, 2, ns, P])
                hr, hi = taps(0), taps(1)
                ch.then(v.tensor_tensor(yr, zr, hr, ALU.mult))
                ch.then(v.tensor_tensor(tmp, zi, hi, ALU.mult))
                ch.then(v.tensor_tensor(yi, zi, hr, ALU.mult))
                ch.then(v.tensor_tensor(tmp2, zr, hi, ALU.mult))
                ch.wait()
                v.tensor_tensor(yr, yr, tmp, ALU.subtract).then_inc(mixed, 1)
                v.tensor_tensor(yi, yi, tmp2, ALU.add).then_inc(mixed, 1)
                v.wait_ge(descaled, u + 1)
                ch.then(v.scalar_tensor_tensor(out=yc, in0=z[s], scalar=K.cols[:, l, bass.ds(u + C_HBIAS, 1)],
                                               in1=yc, op0=ALU.mult, op1=ALU.add))
                ch.wait()
                v.tensor_tensor(K.YB[:, bass.ds(u, 1), t0:].rearrange("p a t -> p (a t)"), yc, x0[s],
                                ALU.mult).then_inc(unit_out, 1)
                assert ch.n == CHAIN, ch.n
            pairs(v, KC, unit)


def stage_merge(nc, K, l, branch, first):
    t0, ns = spans(l)
    nt = ns * SEQ
    with stage(nc, "tile_in0", "tile_in1", "projected", "tanh_done", "gated", "merged") as (
            tile_in0, tile_in1, projected, tanh_done, gated, merged), nc.Block() as block:
        tile_in = [tile_in0, tile_in1]
        slots = [K.ring(s, KC * 256).rearrange("p (k c) -> p k c", k=KC) for s in range(2)]
        th = [K.f(190 + 2 * s, nt) for s in range(2)]

        @block.sync
        def _(sp):
            def load(u, s):
                sp.dma_start(*merge_tile(K, l, branch, u, s)).then_inc(tile_in[s], 16)
            if branch == 1:
                for dst, src in gate_consts(K, l):
                    K.early.issue(sp, 3, dst, src)
            prefetch(sp, KC, load, lambda u: sp.wait_ge(projected, u * 2 + 2), K.early, tile_in)
            for s in range(2):
                sp.wait_ge(projected, (KC - 2 + s) * 2 + 2)
                if branch != 1:
                    K.early.issue(sp, s, *(attention_tile if branch == 2 else out_tile)(K, l, s, s))

        @block.tensor
        def _(pe):
            pe.sem_inc(merged, 2)

            def unit(u, s):
                pe.wait_ge(tile_in[s], (u - s) * 8 + 16)
                pe.wait_ge(merged, u + 1)
                accumulate(pe, K.ps[:, 2 * s, 0:nt], lambda k: slots[s][:, k, P:2 * P], lambda k: K.H[:, k, t0:],
                           KC).then_inc(projected, 1)
                accumulate(pe, K.ps[:, 2 * s + 1, 0:nt], lambda k: slots[s][:, k, 0:P], lambda k: K.YB[:, k, t0:],
                           KC).then_inc(projected, 1)
            pairs(pe, KC, unit)

        @block.scalar
        def _(act):
            def unit(u, s):
                act.wait_ge(projected, u * 2 + 1)
                act.wait_ge(merged, u + 1)
                act.activation(th[s], K.ps[:, 2 * s, 0:nt], ACT.Tanh, scale=0.5,
                               bias=K.half_mb[:, l, bass.ds(u + 8 * branch, 1)]).then_inc(tanh_done, 1)
            pairs(act, KC, unit)

        @block.vector
        def _(v):
            def unit(u, s):
                y = K.Y[:, bass.ds(u, 1), t0:].rearrange("p a t -> p (a t)")
                v.wait_ge(tanh_done, u + 1)
                v.wait_ge(projected, u * 2 + 2)
                v.scalar_tensor_tensor(out=th[s], in0=th[s], scalar=1.0, in1=K.ps[:, 2 * s + 1, 0:nt], op0=ALU.add,
                                       op1=ALU.mult).then_inc(gated, 1)
                v.wait_ge(gated, u + 1)
                if first:
                    v.tensor_scalar(y, th[s], 0.5, None, ALU.mult).then_inc(merged, 1)
                else:
                    v.scalar_tensor_tensor(out=y, in0=th[s], scalar=0.5, in1=y, op0=ALU.mult,
                                           op1=ALU.add).then_inc(merged, 1)
            pairs(v, KC, unit)
            v.wait_ge(merged, KC + 2)


class Split:

    def __init__(self, K, raw_kib, hi_kib, lo_kib, chunks, width):
        shape = lambda a: a.rearrange("p (k t) -> p k t", k=chunks)
        self.raw = shape(K.f(raw_kib, chunks * width))
        self.hi, self.lo = (shape(K.r(kib, chunks * width)) for kib in (hi_kib, lo_kib))

    def round(self, act, k=slice(None)):
        return act.activation(self.hi[:, k], self.raw[:, k], ACT.Copy)

    def rest(self, v, k=slice(None)):
        return v.tensor_tensor(self.lo[:, k], self.raw[:, k], self.hi[:, k].bitcast(F32), ALU.subtract)


def split_accumulate(pe, out, w, cols, x, before=None):
    for k in range(KC):
        if before:
            before(k)
        pe.matmul(out, w.hi[:, k, cols], x.hi[:, k, :], start=(k == 0), stop=False)
        pe.matmul(out, w.lo[:, k, cols], x.hi[:, k, :], start=False, stop=False)
        last = pe.matmul(out, w.hi[:, k, cols], x.lo[:, k, :], start=False, stop=(k == KC - 1))
    return last


def stage_merge_split(nc, K, l, branch, first):
    with stage(nc, "tile_in0", "tile_in1", "w_rounded", "w_split", "x_rounded", "x_split", "projected", "tanh_done", "gated",
               "merged") as (tile_in0, tile_in1, w_rounded, w_split, x_rounded, x_split, projected, tanh_done, gated,
                             merged), nc.Block() as block:
        tile_in = [tile_in0, tile_in1]
        H, YB = Split(K, 16, 100, 116, KC, NTOK), Split(K, 48, 132, 148, KC, NTOK)
        W = [Split(K, 64 + 12 * s, 164 + 16 * s, 172 + 16 * s, KC, 256) for s in range(2)]
        th = [K.f(88 + 2 * s, NTOK) for s in range(2)]

        @block.sync
        def _(sp):
            def load(u, s):
                sp.dma_start(*merge_tile(K, l, branch, u, s)).then_inc(tile_in[s], 16)
            if branch == 1:
                for dst, src in gate_consts(K, l):
                    K.early.issue(sp, 3, dst, src)
            prefetch(sp, KC, load, lambda u: sp.wait_ge(w_split, u + 1), K.early, tile_in)
            for s in range(2):
                sp.wait_ge(w_split, KC - 1 + s)
                if branch != 1:
                    K.early.issue(sp, s, *(attention_tile if branch == 2 else out_tile)(K, l, s, s))

        @block.tensor
        def _(pe):
            pe.sem_inc(merged, 2)

            def unit(u, s, split_now=False):
                pe.wait_ge(w_split, u + 1)
                pe.wait_ge(merged, u + 1)
                for i, x in enumerate((H, YB)):
                    split_accumulate(pe, K.ps[:, 2 * s + i, :], W[s], slice(P - P * i, 2 * P - P * i), x,
                                     (lambda k: pe.wait_ge(x_split, KC * i + k + 1)) if split_now else None).then_inc(projected, 1)
            unit(0, 0, split_now=True)
            with pe.Fori(0, KC // 2 - 1) as i:
                for s in range(1, 3):
                    unit(i * 2 + s, s % 2)
            unit(KC - 1, 1)

        @block.scalar
        def _(act):
            def weights(u, s):
                act.wait_ge(tile_in[s], (u - s) * 8 + 16)
                W[s].round(act).then_inc(w_rounded, 1)
            weights(0, 0)
            for x in (H, YB):
                for k in range(KC):
                    x.round(act, k).then_inc(x_rounded, 1)
            weights(1, 1)

            def unit(u, s, more=True):
                act.wait_ge(projected, u * 2 + 1)
                act.wait_ge(merged, u + 1)
                act.activation(th[s], K.ps[:, 2 * s, :], ACT.Tanh, scale=0.5,
                               bias=K.half_mb[:, l, bass.ds(u + 8 * branch, 1)]).then_inc(tanh_done, 1)
                if more:
                    act.wait_ge(projected, u * 2 + 2)
                    weights(u + 2, s)
            with act.Fori(0, KC // 2 - 1) as i:
                for s in range(2):
                    unit(i * 2 + s, s)
            for s in range(2):
                unit(KC - 2 + s, s, more=False)

        @block.vector
        def _(v):
            def weights(u, s):
                v.wait_ge(w_rounded, u + 1)
                W[s].rest(v).then_inc(w_split, 1)
            weights(0, 0)
            for i, x in enumerate((H, YB)):
                for k in range(KC):
                    v.wait_ge(x_rounded, KC * i + k + 1)
                    x.rest(v, k).then_inc(x_split, 1)
            weights(1, 1)

            def unit(u, s, more=True):
                y = K.Y[:, bass.ds(u, 1), :].rearrange("p a t -> p (a t)")
                v.wait_ge(tanh_done, u + 1)
                v.wait_ge(projected, u * 2 + 2)
                v.scalar_tensor_tensor(out=th[s], in0=th[s], scalar=1.0, in1=K.ps[:, 2 * s + 1, :], op0=ALU.add,
                                       op1=ALU.mult).then_inc(gated, 1)
                if more:
                    weights(u + 2, s)
                v.wait_ge(gated, u + 1)
                if first:
                    v.tensor_scalar(y, th[s], 0.5, None, ALU.mult).then_inc(merged, 1)
                else:
                    v.scalar_tensor_tensor(out=y, in0=th[s], scalar=0.5, in1=y, op0=ALU.mult,
                                           op1=ALU.add).then_inc(merged, 1)
            with v.Fori(0, KC // 2 - 1) as i:
                for s in range(2):
                    unit(i * 2 + s, s)
            for s in range(2):
                unit(KC - 2 + s, s, more=False)
            v.wait_ge(merged, KC + 2)


def stage_out(nc, K, l):
    t0, ns = spans(l)
    nt = ns * SEQ
    with stage(nc, "tile_in0", "tile_in1", "projected", "added", "squared", "summed") as (
            tile_in0, tile_in1, projected, added, squared, summed), nc.Block() as block:
        tile_in = [tile_in0, tile_in1]
        slots = [K.ring(s, KC * 256).rearrange("p (k c) -> p k c", k=KC) for s in range(2)]

        @block.sync
        def _(sp):
            def load(u, s):
                sp.dma_start(*out_tile(K, l, u, s)).then_inc(tile_in[s], 16)
            prefetch(sp, KC // 2, load, lambda u: sp.wait_ge(projected, u * 2 + 2), K.early, tile_in)
            for dst, src in moe_consts(K, l):
                K.early.issue(sp, 3, dst, src)
            for n, (dst, src) in enumerate(expert_tiles(K, l, 0, 0)):
                K.early.issue(sp, n // 2, dst, src)

        @block.tensor
        def _(pe):
            pe.sem_inc(added, 4 * ns)

            def tile(u, s):
                pe.wait_ge(tile_in[s], (u - s) * 8 + 16)
                for c in range(2):
                    pe.wait_ge(added, (u * 2 + c + 1) * ns)
                    accumulate(pe, K.ps[:, 2 * s + c, 0:nt], lambda k: slots[s][:, k, c * P:c * P + P],
                               lambda k: K.Y[:, k, t0:], KC).then_inc(projected, 1)
            pairs(pe, KC // 2, tile)
            for k in range(KC):
                pe.wait_ge(squared, k + 1)
                last = pe.matmul(K.ps[:, 4, t0:], K.ones, K.H[:, k, t0:], start=(k == 0), stop=(k == KC - 1))
            last.then_inc(summed, 1)

        @block.scalar
        def _(act):
            def tile(u, s):
                for c in range(2):
                    act.wait_ge(added, (u * 2 + (c + 5)) * ns)
                    act.activation(K.H[:, bass.ds(u * 2 + c, 1), t0:].rearrange("p a t -> p (a t)"),
                                   K.X[:, bass.ds(u * 2 + c, 1), t0:].rearrange("p a t -> p (a t)"), ACT.Square).then_inc(squared, 1)
            pairs(act, KC // 2, tile)
            act.wait_ge(squared, KC)

        @block.vector
        def _(v):
            def tile(u, s):
                for c in range(2):
                    v.wait_ge(projected, u * 2 + c + 1)
                    for q in range(2 - ns, 2):
                        x = K.X[:, bass.ds(u * 2 + c, 1), q * SEQ:q * SEQ + SEQ].rearrange("p a t -> p (a t)")
                        v.scalar_tensor_tensor(out=x, in0=K.ps[:, 2 * s + c, q * SEQ - t0:q * SEQ - t0 + SEQ],
                                               scalar=K.mod[:, bass.ds(u * 2 + (48 * l + G1 + c), 1), q:q + 1].rearrange("p a b -> p (a b)"),
                                               in1=x, op0=ALU.mult, op1=ALU.add).then_inc(added, 1)
            pairs(v, KC // 2, tile)
            v.wait_ge(added, ns * (KC + 4))


def stage_attention(nc, K, l):
    t0, ns = spans(l)
    nt = ns * SEQ
    lam_init = 0.8 - 0.6 * math.exp(-0.3 * l)
    qtiles = [(SEQ, NTOK), (SEQ + P, NTOK)] + ([(0, SEQ), (P, SEQ)] if ns == 2 else [])
    nq = len(qtiles)
    names = ("consts_in", "tile_in0", "tile_in1", "lam_step", "lam_sum", "q_projected", "k_projected", "v_projected",
             "squared", "v_copied", "summed", "rooted", "normed", "rotated", "roped", "scored", "maxed", "exped",
             "weighted", "turned", "copied", "mixed", "o_squared", "o_summed", "o_rooted", "unit_out", "chain", "acts",
             "q_split", "zeroed", "root_logs", "o_logs")
    with stage(nc, *names) as (consts_in, tile_in0, tile_in1, lam_step, lam_sum, q_projected, k_projected, v_projected,
                               squared, v_copied, summed, rooted, normed, rotated, roped, scored, maxed, exped,
                               weighted, turned, copied, mixed, o_squared, o_summed, o_rooted, unit_out, chain,
                               acts, q_split, zeroed, root_logs, o_logs), nc.Block() as block:
        tile_in = [tile_in0, tile_in1]
        slots = [K.ring(s).rearrange("p (k c) -> p k c", k=KC) for s in range(2)]
        rope = K.f(190, 2 * SEQ).rearrange("p (c t) -> p c t", c=2)
        sq = [K.f(100, NTOK), K.f(102, NTOK)]
        rs = [K.f(138, NTOK), K.f(140, NTOK)]
        qk = [[K.f(104 + 2 * s, NTOK) for s in range(2)], [K.f(108 + 2 * s, NTOK) for s in range(2)]]
        qz = [[K.f(149 + 4 * s + 2 * c, NTOK) for c in range(2)] for s in range(2)]
        vt = [K.f(112 + 2 * s, NTOK).rearrange("p (t d) -> p t d", d=P) for s in range(2)]
        pr = [K.f(116 + 4 * s, 2 * NTOK).rearrange("p (c k) -> p c k", c=2) for s in range(2)]
        w = [K.f(124 + 2 * s, NTOK) for s in range(2)]
        wt_lat = K.f(128, 4 * SEQ).rearrange("p (b q) -> p b q", b=4)
        wt_ctx = K.f(132, 2 * SEQ).rearrange("p (b q) -> p b q", b=2)
        st = K.f(134, 8 * nq).rearrange("p (n k c) -> p n k c", k=4, c=2)
        osq, ors = K.f(136, NTOK), K.f(142, NTOK)
        tmp = [K.f(144, SEQ), K.f(145, SEQ)]
        lam = K.f(146, 8)
        prod = K.f(147, 2)[0:A_DH, :]
        gsub = K.f(148, 1)
        widths = (nt, NTOK)
        starts = (t0, 0)
        CHAIN = 4 * nq + 4

        @block.sync
        def _(sp):
            sp.dma_start(rope, K.A["d_rope"]).then_inc(consts_in, 16)

            def load(u, s):
                sp.dma_start(*attention_tile(K, l, u, s)).then_inc(tile_in[s], 16)
            prefetch(sp, KC, load, lambda u: sp.wait_ge(k_projected, u + 1), K.early, tile_in)
            for s in range(2):
                sp.wait_ge(k_projected, KC - 1 + s)
                K.early.issue(sp, s, *merge_tile(K, l, 1, s, s))
            sp.wait_ge(consts_in, 16)

        @block.tensor
        def _(pe):
            def project_v(u, s, ts, wait=True):
                if 0 in ts:
                    pe.wait_ge(tile_in[s], (u - s) * 8 + 16)
                    if wait:
                        pe.wait_ge(v_copied, u)
                for t in ts:
                    last = accumulate(pe, K.ps[:, 2, t * P:t * P + P], lambda k: K.H[:, k, t * P:t * P + P],
                                      lambda k: slots[s][:, k, 2 * P:], KC)
                if 3 in ts:
                    last.then_inc(v_projected, 1)

            def project(j, s, ks, done):
                t = starts[j]
                for k in ks:
                    last = pe.matmul(K.ps[:, j, t:], slots[s][:, k, j * P:j * P + P], K.H[:, k, t:], start=(k == 0), stop=(k == KC - 1))
                if KC - 1 in ks:
                    last.then_inc(done, 1)

            def sums(u):
                for j in range(2):
                    pe.wait_ge(squared, u * 2 + (j + 1))
                    if j == 0:
                        pe.wait_ge(exped, u * nq)
                    pe.matmul(K.ps[:, 4 + j, starts[j]:], K.group64, sq[j][:, starts[j]:], start=True, stop=True).then_inc(summed, 1)

            def rotate(u, s):
                pe.wait_ge(normed, u * 2 + 2)
                pe.wait_ge(o_rooted, u)
                for j in range(2):
                    last = pe.matmul(K.ps[:, 3, j * SEQ:j * SEQ + SEQ], K.rot, qk[j][s][:, SEQ:], start=True, stop=True)
                last.then_inc(rotated, 1)

            def score(u, s, n):
                q0, keys = qtiles[n]
                if n == 0:
                    pe.wait_ge(roped, u * 3 + 3)
                    pe.wait_ge(q_split, u + 1)
                pe.wait_ge(exped, u * nq + n)
                for c in range(2):
                    last = pe.matmul(K.ps[:, 4 + c, 0:keys], qz[s][c][:, q0:q0 + P], qk[1][s][:, 0:keys],
                                     start=True, stop=True)
                last.then_inc(scored, 1)

            def turn(u, n):
                pe.wait_ge(weighted, u * nq + n + 1)
                pe.wait_ge(copied, u * nq + n)
                for b in range(qtiles[n][1] // P):
                    last = pe.transpose(K.ps[:, 6, b * P:b * P + P], w[n % 2][:, b * P:b * P + P], K.ident)
                last.then_inc(turned, 1)

            def mix(u, s):
                pe.wait_ge(copied, u * nq + nq)
                pe.wait_ge(unit_out, u)
                last = accumulate(pe, K.ps[:, 7, SEQ:], lambda b: vt[s][:, b, :], lambda b: wt_lat[:, b, :], 4)
                if ns == 2:
                    last = accumulate(pe, K.ps[:, 7, 0:SEQ], lambda b: vt[s][:, b, :], lambda b: wt_ctx[:, b, :], 2)
                last.then_inc(mixed, 1)

            def o_sums(u):
                pe.wait_ge(o_squared, u + 1)
                pe.wait_ge(roped, u * 3 + 3)
                pe.matmul(K.ps[:, 3, t0:], K.ones, osq[:, t0:], start=True, stop=True).then_inc(o_summed, 1)

            def step(u, s, first=False, more=True):
                v = (lambda *ts: project_v(u + 1, 1 - s, ts)) if more else (lambda *ts: None)
                q, k = (lambda *ks: project(0, 1 - s, ks, q_projected), lambda *ks: project(1, 1 - s, ks, k_projected)) if more else (
                    lambda *ks: None, lambda *ks: None)
                sums(u)
                if not first:
                    o_sums(u - 1)
                v(0, 1)
                rotate(u, s)
                v(2, 3)
                score(u, s, 0)
                pieces = [lambda: q(0, 1, 2, 3), lambda: q(4, 5, 6, 7), lambda: k(0, 1, 2, 3), lambda: k(4, 5, 6, 7)]
                for n in range(nq):
                    pieces[n]()
                    if n == nq - 1:
                        for piece in pieces[nq:]:
                            piece()
                    else:
                        score(u, s, n + 1)
                    turn(u, n)
                mix(u, s)

            pe.wait_ge(lam_step, 2)
            pe.matmul(K.ps[:, 0, 0:2], K.ones[0:A_DH, :], prod, start=True, stop=True).then_inc(lam_sum, 1)
            pe.wait_ge(acts, 1)
            project_v(0, 0, range(4), wait=False)
            project(0, 0, range(KC), q_projected)
            project(1, 0, range(KC), k_projected)
            step(0, 0, first=True)
            with pe.Fori(0, KC // 2 - 1) as i:
                for s in range(1, 3):
                    step(i * 2 + s, s % 2)
            step(KC - 1, 1, more=False)
            o_sums(KC - 1)

        @block.scalar
        def _(act):
            act.preload_act_table_set(LN_EXP)
            act.wait_ge(lam_sum, 1)
            act.activation(lam[:, 0:2], K.ps[:, 0, 0:2], ACT.Exp).then_inc(acts, 1)

            def squares(u, s):
                for j, done in enumerate((q_projected, k_projected)):
                    act.wait_ge(done, u + 1)
                    act.activation(sq[j][:, starts[j]:], K.ps[:, j, starts[j]:], ACT.Square).then_inc(squared, 1)
                act.wait_ge(v_projected, u + 1)
                act.activation(vt[s], K.ps[:, 2, :].rearrange("p (t d) -> p t d", d=P), ACT.Copy).then_inc(v_copied, 1)

            def exps(u, n):
                keys = qtiles[n][1]
                act.wait_ge(maxed, u * nq + n + 1)
                act.wait_ge(weighted, u * nq + (n - 1) if n else u * nq)
                for c in range(2):
                    last = act.activation(pr[n % 2][:, c, 0:keys], K.ps[:, 4 + c, 0:keys], ACT.Exp, scale=A_DH ** -0.5,
                                          bias=st[:, n, 0, c:c + 1], accum_out=st[:, n, 1, c:c + 1])
                last.then_inc(exped, 1)

            def copy(u, n):
                q0, keys = qtiles[n]
                act.wait_ge(turned, u * nq + n + 1)
                if n == 0:
                    act.wait_ge(mixed, u)
                wt = wt_lat if keys == NTOK else wt_ctx
                act.activation(wt[:, :, q0 % SEQ:q0 % SEQ + P],
                               K.ps[:, 6, 0:keys].rearrange("p (b q) -> p b q", q=P), ACT.Copy).then_inc(copied, 1)

            def o_root(u):
                act.wait_ge(o_summed, u + 1)
                act.wait_ge(unit_out, u)
                act.activation(ors[:, t0:], K.ps[:, 3, t0:], ACT.Ln, scale=1.0 / P, bias=K.eps).then_inc(o_logs, 1)
                act.wait_ge(o_logs, u + 1)
                act.activation(ors[:, t0:], ors[:, t0:], ACT.Exp, scale=-0.5).then_inc(o_rooted, 1)

            def step(u, s, first=False, more=True):
                for j in range(2):
                    act.wait_ge(summed, u * 2 + j + 1)
                    t = slice(starts[j], NTOK)
                    act.activation(rs[j][:, t], K.ps[:, 4 + j, t], ACT.Ln, scale=1.0 / A_DH, bias=K.eps).then_inc(root_logs, 1)
                    act.wait_ge(root_logs, u * 2 + (j + 1))
                    act.activation(rs[j][:, t], rs[j][:, t], ACT.Exp, scale=-0.5).then_inc(rooted, 1)
                if not first:
                    o_root(u - 1)
                if ns == 2:
                    act.wait_ge(normed, u * 2 + 1)
                    if first:
                        act.wait_ge(zeroed, 4)
                    for c in range(2):
                        part = slice(c * A_DH, c * A_DH + A_DH)
                        last = act.activation(qz[s][c][part, 0:SEQ], qk[0][s][part, 0:SEQ], ACT.Copy)
                    last.then_inc(q_split, 1)
                exps(u, 0)
                for n in range(1, nq):
                    exps(u, n)
                    copy(u, n - 1)
                copy(u, nq - 1)
                act.wait_ge(mixed, u + 1)
                act.activation(osq[:, t0:], K.ps[:, 7, t0:], ACT.Square).then_inc(o_squared, 1)
                if more:
                    squares(u + 1, 1 - s)

            squares(0, 0)
            step(0, 0, first=True)
            with act.Fori(0, KC // 2 - 1) as i:
                for s in range(1, 3):
                    step(i * 2 + s, s % 2)
            step(KC - 1, 1, more=False)
            o_root(KC - 1)

        @block.vector
        def _(v):
            v.tensor_tensor(prod, K.lam4[:, l, 0:4:2], K.lam4[:, l, 1:4:2], ALU.mult).then_inc(lam_step, 1)
            v.tensor_scalar(gsub, K.cols[:, l, C_SUB:C_SUB + 1], 1.0 - lam_init, None, ALU.mult).then_inc(lam_step, 1)
            v.wait_ge(acts, 1)
            v.tensor_tensor(lam[:, 2:3], lam[:, 1:2], lam[:, 0:1], ALU.subtract).then_inc(lam_step, 1)
            v.wait_ge(lam_step, 3)
            v.tensor_scalar(lam[:, 3:4], lam[:, 2:3], -lam_init, None, ALU.add).then_inc(lam_step, 1)
            v.wait_ge(lam_step, 4)
            for s in range(2):
                for c in range(2):
                    v.memset(qz[s][c][A_DH - c * A_DH:P - c * A_DH, :], 0.0).then_inc(zeroed, 1)
            v.wait_ge(consts_in, 16)

            def output(u):
                v.wait_ge(o_rooted, u + 1)
                v.scalar_tensor_tensor(out=K.YB[:, bass.ds(u, 1), t0:].rearrange("p a t -> p (a t)"), in0=K.ps[:, 7, t0:],
                                       scalar=gsub, in1=ors[:, t0:], op0=ALU.mult, op1=ALU.mult).then_inc(unit_out, 1)

            def unit(u, s, first=False):
                ch = Chain(v, chain, u * CHAIN)
                for j, g in enumerate((C_QG, C_KG)):
                    v.wait_ge(rooted, u * 2 + j + 1)
                    t = slice(starts[j], NTOK)
                    v.scalar_tensor_tensor(out=qk[j][s][:, t], in0=K.ps[:, j, t], scalar=K.cols[:, l, g:g + 1],
                                           in1=rs[j][:, t], op0=ALU.mult, op1=ALU.mult).then_inc(normed, 1)
                v.wait_ge(rotated, u + 1)
                for j in range(2):
                    lat = qk[j][s][:, SEQ:]
                    ch.then(v.tensor_tensor(tmp[j], K.ps[:, 3, j * SEQ:j * SEQ + SEQ], rope[:, 1, :], ALU.mult))
                    ch.then(v.tensor_tensor(lat, lat, rope[:, 0, :], ALU.mult))
                    ch.wait()
                    if j == 1:
                        v.tensor_tensor(lat, lat, tmp[j], ALU.add).then_inc(roped, 1)
                    else:
                        for c in range(2):
                            part = slice(c * A_DH, c * A_DH + A_DH)
                            v.tensor_tensor(qz[s][c][part, SEQ:], lat[part, :], tmp[j][part, :], ALU.add).then_inc(roped, 1)
                if ns == 1:
                    v.sem_inc(q_split, 1)
                if not first:
                    output(u - 1)
                for n, (q0, keys) in enumerate(qtiles):
                    v.wait_ge(scored, u * nq + n + 1)
                    ch.then(v.tensor_reduce(st[:, n, 2, :], K.ps[:, 4:6, 0:keys], AX.X, ALU.max))
                    ch.wait()
                    v.tensor_scalar(st[:, n, 0, :], st[:, n, 2, :], -A_DH ** -0.5, None, ALU.mult).then_inc(maxed, 1)
                    v.wait_ge(exped, u * nq + n + 1)
                    ch.then(v.reciprocal(st[:, n, 3, :], st[:, n, 1, :]))
                    ch.wait()
                    ch.then(v.tensor_tensor(st[:, n, 3, 1:2], st[:, n, 3, 1:2], lam[:, 3:4], ALU.mult))
                    if n >= 2:
                        v.wait_ge(turned, u * nq + n - 1)
                    else:
                        v.wait_ge(turned, u * nq)
                    ch.then(v.tensor_scalar(w[n % 2][:, 0:keys], pr[n % 2][:, 0, 0:keys], st[:, n, 3, 0:1], None, ALU.mult))
                    ch.wait()
                    v.scalar_tensor_tensor(out=w[n % 2][:, 0:keys], in0=pr[n % 2][:, 1, 0:keys], scalar=st[:, n, 3, 1:2],
                                           in1=w[n % 2][:, 0:keys], op0=ALU.mult, op1=ALU.add).then_inc(weighted, 1)
                assert ch.n == CHAIN, ch.n
            unit(0, 0, first=True)
            with v.Fori(0, KC // 2 - 1) as i:
                for s in range(1, 3):
                    unit(i * 2 + s, s % 2)
            unit(KC - 1, 1)
            output(KC - 1)
            v.wait_ge(unit_out, KC)


def gate_consts(K, l):
    return [(K.f(196, KC * P), K.A["d_wg"][l]), (K.f(96, 8 * P).rearrange("p (r m) -> p r m", r=8), K.A["d_sel"])]


def stage_gates(nc, K, l):
    names = ("weights_in", "masks_in", "projected", "biased", "logged", "acts", "scanned", "turned", "spread", "copied")
    with stage(nc, *names) as (weights_in, masks_in, projected, biased, logged, acts, scanned, turned, spread,
                               copied), nc.Block() as block:
        wg = K.f(196, KC * P).rearrange("p (k c) -> p k c", k=KC)
        sel = K.f(96, 8 * P).rearrange("p (r m) -> p r m", r=8)
        g = K.f(108, NTOK)
        mag = K.f(110, NTOK)
        low = K.f(112, NTOK)
        B, A, M, E, zero = (K.f(114 + 2 * i, NTOK)[0:36, :] for i in range(5))
        M_all = K.f(118, NTOK)

        @block.sync
        def _(sp):
            for s in range(3):
                K.early.issue(sp, s, *mlstm_tile(K, l, 0, s))
            sp.dma_start(K.masks, K.A["d_masks"]).then_inc(masks_in, 16)
            K.early.hand_over(sp, 3, weights_in)
            sp.wait_ge(masks_in, 16)

        @block.tensor
        def _(pe):
            pe.wait_ge(weights_in, 16)
            accumulate(pe, K.ps[:, 0, :], lambda k: wg[:, k, :], lambda k: K.H[:, k, :], KC).then_inc(projected, 1)
            pe.wait_ge(scanned, 9)
            pe.wait_ge(acts, 3)
            for j, rows in enumerate((A, E)):
                for t in range(4):
                    last = pe.transpose(K.ps[:, 1, (j * 4 + t) * 36:(j * 4 + t) * 36 + 36], rows[:, t * P:t * P + P],
                                        K.ident[0:36, 0:36])
            last.then_inc(turned, 1)
            for r in range(8):
                if r >= 4:
                    pe.wait_ge(copied, r - 3)
                pe.matmul(K.ps[:, 2 + r % 4, :], sel[:, r, :], M_all, start=True, stop=True).then_inc(spread, 1)

        @block.scalar
        def _(act):
            act.preload_act_table_set(LN_EXP)
            act.wait_ge(biased, 3)
            act.activation(mag[64:100, :], mag[64:100, :], ACT.Exp, scale=-1.0).then_inc(acts, 1)
            act.wait_ge(acts, 1)
            act.activation(mag[64:100, :], mag[64:100, :], ACT.Ln, bias=1.0).then_inc(acts, 1)
            act.wait_ge(scanned, 9)
            act.activation(E, E, ACT.Exp, scale=-1.0).then_inc(acts, 1)
            for r in range(8):
                act.wait_ge(spread, r + 1)
                act.activation(K.neg_m[:, r, :], K.ps[:, 2 + r % 4, :], ACT.Copy).then_inc(copied, 1)
            act.wait_ge(copied, 8)

        @block.vector
        def _(v):
            v.memset(zero, 0.0).then_inc(scanned, 1)
            v.memset(B, 0.0).then_inc(scanned, 1)
            v.memset(M_all, 0.0).then_inc(scanned, 1)
            v.wait_ge(projected, 1)
            v.tensor_scalar(g, K.ps[:, 0, :], K.cols[:, l, C_GB:C_GB + 1], None, ALU.add).then_inc(biased, 1)
            v.wait_ge(biased, 1)
            x = g[64:100, :]
            v.scalar_tensor_tensor(out=mag[64:100, :], in0=x, scalar=-1.0, in1=x, op0=ALU.mult, op1=ALU.max).then_inc(biased, 1)
            v.tensor_scalar(low[64:100, :], x, 0.0, None, ALU.min).then_inc(biased, 1)
            v.wait_ge(biased, 3)
            v.wait_ge(acts, 2)
            v.tensor_tensor(low[0:36, :], low[64:100, :], mag[64:100, :], ALU.subtract).then_inc(logged, 1)
            v.wait_ge(logged, 1)
            v.wait_ge(scanned, 3)
            fwd, bwd, bctx, blat = slice(0, 4), slice(32, 36), slice(SEQ - 1, None, -1), slice(NTOK - 1, SEQ - 1, -1)

            def scan(out, src, other, op, sem_now):
                v.tensor_tensor_scan(out[fwd, :], src[fwd, :], other[fwd, :], 0.0, op, op).then_inc(scanned, 1)
                v.tensor_tensor_scan(out[bwd, bctx], src[bwd, bctx], other[bwd, bctx], 0.0, op, op).then_inc(scanned, 1)
                v.wait_ge(scanned, sem_now + 2)
                v.tensor_tensor_scan(out[bwd, blat], src[bwd, blat], other[bwd, blat], out[bwd, 0:1], op,
                                     op).then_inc(scanned, 1)
                v.wait_ge(scanned, sem_now + 3)
            scan(B, low[0:36, :], zero, ALU.add, 3)
            v.tensor_tensor(A, g[0:36, :], B, ALU.subtract).then_inc(logged, 1)
            v.wait_ge(logged, 2)
            v.tensor_tensor_scan(M[fwd, :], A[fwd, :], A[fwd, :], 0.0, ALU.max, ALU.max).then_inc(logged, 1)
            v.tensor_tensor_scan(M[bwd, bctx], A[bwd, bctx], A[bwd, bctx], 0.0, ALU.max, ALU.max).then_inc(logged, 1)
            v.wait_ge(logged, 4)
            v.tensor_tensor_scan(M[bwd, blat], A[bwd, blat], A[bwd, blat], M[bwd, 0:1], ALU.max, ALU.max).then_inc(scanned, 1)
            v.wait_ge(scanned, 7)
            v.tensor_tensor(E, B, M, ALU.add).then_inc(scanned, 1)
            v.wait_ge(scanned, 8)
            v.tensor_scalar(M, M, -1.0, None, ALU.mult).then_inc(scanned, 1)
            v.wait_ge(turned, 1)
            cols = K.ps[:, 1, 0:288].rearrange("p (j t r) -> p j t r", j=2, t=4)
            v.tensor_copy(K.gate_cols, cols).then_inc(logged, 1)
            v.wait_ge(logged, 5)


def stage_mlstm(nc, K, l):
    t0, ns = spans(l)
    nt = ns * SEQ
    tiles = list(range(4 - 2 * ns, 4))
    names = ("tile_a", "tile_b", "tile_c", "qk_projected", "centred", "tapped", "tanhed", "qk_ready", "v_projected",
             "v_copied", "o_projected", "o_tanhed", "o_ready", "scored", "bounded", "exped", "weighted", "summed",
             "normed", "half_tapped", "den_step", "ones_set")
    with stage(nc, *names) as (tile_a, tile_b, tile_c, qk_projected, centred, tapped, tanhed, qk_ready, v_projected,
                               v_copied, o_projected, o_tanhed, o_ready, scored, bounded, exped, weighted, summed,
                               normed, half_tapped, den_step, ones_set), nc.Block() as block:
        wa, wb = (K.ring(s).rearrange("p (k c) -> p k c", k=KC) for s in range(2))
        wc = K.ring(2, KC * 256).rearrange("p (k c) -> p k c", k=KC)
        q, k_ = (K.f(a, 2 * NTOK).rearrange("p (c t) -> p c t", c=2) for a in (186, 190))
        qk = [q, q, k_, k_]
        first = [t0, t0, 0, 0]
        th = K.f(194, NTOK)
        V = K.f(127, 4 * 257).rearrange("p (t d) -> p t d", t=4)
        U = [K.f(105 + 2 * i, NTOK) for i in range(2)]
        W = [K.f(109 + 8 * i, 4 * NTOK).rearrange("p (b t) -> p b t", b=4) for i in range(2)]
        den = K.f(125, 16)
        parts = [(b, t0 if b < 2 else SEQ) for b in range(4)]
        banks = [K.ps[:, 4, :], K.ps[:, 5, :], K.ps[:, 6, :], K.ps[:, 6, :]]

        def score_of(b, ta, tb):
            off = 0 if b < 3 else SEQ
            return banks[b][:, off + ta - parts[b][1]:off + tb - parts[b][1]]

        def sources(t, d):
            own = [b for b in range(4) if b // 2 == t // 2 and (b <= t if d == 0 else b >= t)]
            return ([0, 1] if t >= 2 else []) + own
        outs = [(t, d) for t in tiles for d in range(2)]
        NO = len(outs)

        @block.sync
        def _(sp):
            for s, sem in enumerate((tile_a, tile_b, tile_c)):
                K.early.hand_over(sp, s, sem)
            with sp.Fori(0, M_HEADS - 1) as h:
                sp.wait_ge(qk_projected, h * 4 + 3)
                sp.dma_start(*mlstm_tile(K, l, h + 1, 0)).then_inc(tile_a, 16)
                sp.wait_ge(v_projected, h + 1)
                sp.dma_start(*mlstm_tile(K, l, h + 1, 1)).then_inc(tile_b, 16)
                sp.wait_ge(o_projected, h * 2 + 2)
                sp.dma_start(*mlstm_tile(K, l, h + 1, 2)).then_inc(tile_c, 16)

        @block.tensor
        def _(pe):
            def project_qk(h, peeled=False):
                pe.wait_ge(tile_a, h * 16 + 16)
                for j in range(4):
                    if j == 3:
                        pe.wait_ge(tile_b, h * 16 + 16)
                    if not peeled:
                        pe.wait_ge(tapped, h * 4 + (j - 3))
                    w, c = ((wa, j * P), (wb, 0))[j == 3]
                    accumulate(pe, K.ps[:, j, first[j]:], lambda k: w[:, k, c:c + P], lambda k: K.H[:, k, first[j]:],
                               KC).then_inc(qk_projected, 1)

            def project_vo(h, peeled=False):
                if not peeled:
                    pe.wait_ge(normed, h * NO)
                for t in range(4):
                    last = accumulate(pe, K.ps[:, 4 + t // 2, t % 2 * 256:t % 2 * 256 + 256],
                                      lambda k: K.H[:, k, t * P:t * P + P], lambda k: wb[:, k, P:], KC)
                last.then_inc(v_projected, 1)
                pe.wait_ge(tile_c, h * 16 + 16)
                for c in range(2):
                    accumulate(pe, K.ps[:, 6 + c, t0:], lambda k: wc[:, k, c * P:c * P + P], lambda k: K.H[:, k, t0:],
                               KC).then_inc(o_projected, 1)

            def score(h):
                pe.wait_ge(qk_ready, h * 4 + 4)
                pe.wait_ge(v_copied, h * 2 + 2)
                pe.wait_ge(o_tanhed, h * 2 + 2)
                for b, ta in parts:
                    last = accumulate(pe, score_of(b, ta, NTOK), lambda c: k_[:, c, b * P:b * P + P], lambda c: q[:, c, ta:], 2)
                last.then_inc(scored, 1)

            def mix(h):
                for n, (t, d) in enumerate(outs):
                    if n == 0:
                        pe.wait_ge(weighted, h * 8 + 8)
                    if n >= 4:
                        pe.wait_ge(normed, h * NO + (n - 3))
                    src = sources(t, d)
                    bank = K.ps[:, (7, 4, 5, 6)[n % 4], 0:257]
                    accumulate(pe, bank, lambda i: W[d][:, src[i], t * P:t * P + P], lambda i: V[:, src[i], :],
                               len(src)).then_inc(summed, 1)

            pe.wait_ge(ones_set, 1)
            project_qk(0, True)
            project_vo(0, True)
            score(0)
            with pe.Fori(0, M_HEADS - 1) as h:
                project_qk(h + 1)
                mix(h)
                project_vo(h + 1)
                score(h + 1)
            mix(M_HEADS - 1)

        @block.scalar
        def _(act):
            def prepare(h, peeled=False):
                def centre(j):
                    act.wait_ge(qk_projected, h * 4 + (j + 1))
                    if j % 2 == 0 and not peeled:
                        act.wait_ge(scored, h)
                    col = h * 2 + (C_MCW + 16 + 8 * (j // 2) + j % 2)
                    act.activation(qk[j][:, j % 2, first[j]:], K.ps[:, j, first[j]:], ACT.Identity,
                                   scale=K.cols[:, l, bass.ds(col, 1)],
                                   bias=K.cols[:, l, bass.ds(h * 2 + (C_MCB + 8 * (j // 2) + j % 2), 1)]).then_inc(centred, 1)
                centre(0)
                for j in range(4):
                    if j < 3:
                        centre(j + 1)
                    act.wait_ge(tapped, h * 4 + (j + 1))
                    act.wait_ge(qk_ready, h * 4 + j)
                    act.activation(th[:, first[j]:], qk[j][:, j % 2, first[j]:], ACT.Tanh, scale=0.5).then_inc(tanhed, 1)

            def values(h, peeled=False):
                act.wait_ge(v_projected, h + 1)
                for i in range(2):
                    act.activation(V[:, 2 * i:2 * i + 2, 0:256], K.ps[:, 4 + i, :].rearrange("p (t d) -> p t d", t=2),
                                   ACT.Copy).then_inc(v_copied, 1)
                for c in range(2):
                    act.wait_ge(o_projected, h * 2 + (c + 1))
                    act.activation(K.og[:, bass.ds(h * 2 + c, 1), t0:].rearrange("p a t -> p (a t)"), K.ps[:, 6 + c, t0:],
                                   ACT.Tanh, scale=0.5).then_inc(o_tanhed, 1)

            def weights(h):
                for n in range(8):
                    d, b = n // 4, n % 4
                    u = U[n % 2]
                    a = K.gate_cols[:, 0, b, bass.ds(h + 32 * d, 1)]
                    act.wait_ge(bounded, h * 8 + (n + 1))
                    if b >= 2:
                        last = act.activation(u[:, SEQ:], u[:, SEQ:], ACT.Exp)
                    elif ns == 2:
                        act.activation(u[:, 0:SEQ], u[:, 0:SEQ], ACT.Exp)
                    if b < 2:
                        last = act.activation(u[:, SEQ:], K.neg_m[:, bass.ds(h + 4 * d, 1), SEQ:].rearrange("p a t -> p (a t)"),
                                              ACT.Exp, bias=a)
                    last.then_inc(exped, 1)

            prepare(0, True)
            values(0, True)
            weights(0)
            with act.Fori(0, M_HEADS - 1) as h:
                prepare(h + 1)
                act.wait_ge(summed, h * NO + NO)
                values(h + 1)
                weights(h + 1)

        @block.vector
        def _(v):
            v.memset(V[:, :, 256:257], 1.0).then_inc(ones_set, 1)

            def prepare(h):
                for j in range(4):
                    n = (NTOK - first[j]) // SEQ
                    src = K.ps[:, j, first[j]:].rearrange("p (s t) -> p s t", s=n)
                    dst = qk[j][:, j % 2, first[j]:].rearrange("p (s t) -> p s t", s=n)
                    tap = lambda i: K.cols[:, l, bass.ds(h * 2 + (C_MCW + 16 * i + 8 * (j // 2) + j % 2), 1)]
                    v.wait_ge(centred, h * 4 + (j + 1))
                    v.scalar_tensor_tensor(out=dst[:, :, 1:], in0=src[:, :, 0:SEQ - 1], scalar=tap(0), in1=dst[:, :, 1:],
                                           op0=ALU.mult, op1=ALU.add).then_inc(half_tapped, 1)
                    v.wait_ge(half_tapped, h * 4 + (j + 1))
                    v.scalar_tensor_tensor(out=dst[:, :, 0:SEQ - 1], in0=src[:, :, 1:], scalar=tap(2),
                                           in1=dst[:, :, 0:SEQ - 1], op0=ALU.mult, op1=ALU.add).then_inc(tapped, 1)
                    v.wait_ge(tanhed, h * 4 + (j + 1))
                    x = qk[j][:, j % 2, first[j]:]
                    v.scalar_tensor_tensor(out=x, in0=th[:, first[j]:], scalar=1.0, in1=x, op0=ALU.add,
                                           op1=ALU.mult).then_inc(qk_ready, 1)

            def weights(h):
                for c in range(2):
                    v.wait_ge(o_tanhed, h * 2 + (c + 1))
                    og = K.og[:, bass.ds(h * 2 + c, 1), t0:].rearrange("p a t -> p (a t)")
                    v.tensor_scalar(og, og, 0.5, 0.5, ALU.mult, ALU.add).then_inc(o_ready, 1)

                def bound(n):
                    d, b = n // 4, n % 4
                    ta = 0 if b < 2 else SEQ
                    if b >= 2 or ns == 2:
                        v.scalar_tensor_tensor(out=U[n % 2][:, ta:ta + SEQ],
                                               in0=K.neg_m[:, bass.ds(h + 4 * d, 1), ta:ta + SEQ].rearrange("p a t -> p (a t)"),
                                               scalar=K.gate_cols[:, 0, b, bass.ds(h + 32 * d, 1)],
                                               in1=K.masks[:, d, b % 2, :], op0=ALU.add, op1=ALU.min).then_inc(bounded, 1)
                    else:
                        v.sem_inc(bounded, 1)
                bound(0)
                for n in range(8):
                    d, b = n // 4, n % 4
                    if n < 7:
                        if n >= 1:
                            v.wait_ge(weighted, h * 8 + n)
                        bound(n + 1)
                    if n == 0:
                        v.wait_ge(scored, h + 1)
                    v.wait_ge(exped, h * 8 + (n + 1))
                    ta = parts[b][1]
                    v.scalar_tensor_tensor(out=W[d][:, b, ta:], in0=score_of(b, ta, NTOK), scalar=1.0 / 64,
                                           in1=U[n % 2][:, ta:], op0=ALU.mult, op1=ALU.mult).then_inc(weighted, 1)
                v.wait_ge(weighted, h * 8 + 8)

            def outputs(h):
                for n, (t, d) in enumerate(outs):
                    bank = K.ps[:, (7, 4, 5, 6)[n % 4], 0:257]
                    hs = K.hs[:, t, bass.ds(h, 1), :].rearrange("p a c -> p (a c)")
                    e = K.gate_cols[:, 1, t, bass.ds(h + 32 * d, 1)]
                    c = h * (3 * NO) + 3 * n
                    v.wait_ge(summed, h * NO + (n + 1))
                    dn = den[:, 2 * (n % 2):2 * (n % 2) + 1]
                    v.scalar_tensor_tensor(out=dn, in0=bank[:, 256:257], scalar=-1.0, in1=e, op0=ALU.mult,
                                           op1=ALU.max).then_inc(den_step, 1)
                    v.wait_ge(den_step, c + 1)
                    v.tensor_tensor(dn, bank[:, 256:257], dn, ALU.max).then_inc(den_step, 1)
                    v.wait_ge(den_step, c + 2)
                    v.reciprocal(den[:, 2 * (n % 2) + 1:2 * (n % 2) + 2], dn).then_inc(den_step, 1)
                    v.wait_ge(den_step, c + 3)
                    r = den[:, 2 * (n % 2) + 1:2 * (n % 2) + 2]
                    if d == 0:
                        v.tensor_scalar(hs, bank[:, 0:256], r, None, ALU.mult).then_inc(normed, 1)
                    else:
                        v.wait_ge(normed, h * NO + n)
                        v.scalar_tensor_tensor(out=hs, in0=bank[:, 0:256], scalar=r, in1=hs, op0=ALU.mult,
                                               op1=ALU.add).then_inc(normed, 1)

            prepare(0)
            weights(0)
            with v.Fori(0, M_HEADS - 1) as h:
                prepare(h + 1)
                outputs(h)
                weights(h + 1)
            outputs(M_HEADS - 1)
            v.wait_ge(normed, M_HEADS * NO)


def stage_mlstm_out(nc, K, l):
    t0, ns = spans(l)
    tiles = list(range(4 - 2 * ns, 4))
    nt = len(tiles)
    with stage(nc, "squared", "rooted", "root_step", "scaled", "turned", "unit_out") as (
            squared, rooted, root_step, scaled, turned, unit_out), nc.Block() as block:
        sums = K.f(100, 4 * nt).rearrange("p (t h) -> p t h", h=4)
        junk = K.f(101, 256)

        @block.sync
        def _(sp):
            for s in range(2):
                K.early.issue(sp, s, *merge_tile(K, l, 0, s, s))

        @block.scalar
        def _(act):
            for i, t in enumerate(tiles):
                for h in range(M_HEADS):
                    last = act.activation(junk, K.hs[:, t, h, :], ACT.Square, accum_out=sums[:, i, h:h + 1])
                    last.then_inc(squared, 1)
                    act.wait_ge(squared, i * M_HEADS + h + 1)
            act.wait_ge(root_step, 1)
            act.activation(sums, sums, ACT.Sqrt).then_inc(rooted, 1)

        @block.tensor
        def _(pe):
            for c in range(KC):
                pe.wait_ge(scaled, nt * (c // 2 + 1))
                if c >= 2:
                    pe.wait_ge(unit_out, c - 1)
                for i, t in enumerate(tiles):
                    last = pe.transpose(K.ps[:, c % 2, i * P:i * P + P], K.hs[:, t, c // 2, c % 2 * P:c % 2 * P + P], K.ident)
                last.then_inc(turned, 1)

        @block.vector
        def _(v):
            v.wait_ge(squared, nt * M_HEADS)
            v.tensor_scalar(sums, sums, 1.0 / M_DH, EPS, ALU.mult, ALU.add).then_inc(root_step, 1)
            v.wait_ge(rooted, 1)
            v.reciprocal(sums, sums).then_inc(root_step, 1)
            v.wait_ge(root_step, 2)
            for h in range(M_HEADS):
                for i, t in enumerate(tiles):
                    v.tensor_scalar(K.hs[:, t, h, :], K.hs[:, t, h, :], sums[:, i, h:h + 1], None, ALU.mult).then_inc(scaled, 1)
            for c in range(KC):
                v.wait_ge(turned, c + 1)
                v.scalar_tensor_tensor(out=K.YB[:, c, t0:], in0=K.ps[:, c % 2, 0:nt * P],
                                       scalar=K.cols[:, l, C_MN + c % 2:C_MN + c % 2 + 1], in1=K.og[:, c, t0:],
                                       op0=ALU.mult, op1=ALU.mult).then_inc(unit_out, 1)
            v.wait_ge(unit_out, KC)


def moe_consts(K, l):
    n_pairs = TOP_K * SEQ * spans(l)[1]
    return [(K.f(184, KC * 32).rearrange("p (k e) -> p k e", k=KC), K.A["d_rw"]), (K.f(185, 32), K.A["d_rb"]),
            (K.f(194, n_pairs), K.A["d_slots"][:, 0:n_pairs])]


def expert_tiles(K, l, e, s):
    up = lambda kib: K.f(kib, KC * D_EXP).rearrange("p (k f) -> p k f", k=KC)
    down = lambda kib: K.f(kib, 4 * D).rearrange("p (f d) -> p f d", f=4)
    places = (up(104 + 48 * s), up(120 + 48 * s), down(136 + 48 * s))
    return [(dst, K.A[w][l, bass.ds(e, 1)].rearrange("a (k p) f -> p (a k) f", p=P)) for dst, w in zip(places, ("e_w1", "e_w3", "e_w2"))]


def stage_moe(nc, K, l):
    t0, ns = spans(l)
    nt = ns * SEQ
    T = nt // P
    A = TOP_K * nt
    SC = A // P
    n_over = (A - 1) // SLOT
    names = ("consts_in", "w2_in0", "w2_in1", "logits", "exped", "routed", "counted", "h_turned",
             "h_copied", "onehot", "gathered", "sorted_", "starts_turned", "starts_ready",
             "o_in", "o_taken", "o_up", "o_tanh", "o_gated", "o_down", "o_out", "o_chain",
             "raw_in0", "raw_in1", "raw_in2", "raw_in3", "w_rounded", "w_split", "w_used", "x_rounded", "x_split",
             "tanh_done", "gate_step", "gated", "g_turned", "g_copied", "down_done", "stored",
             "spread", "pt_turned", "pt_copied", "y_turned", "y_copied", "combined", "added", "combine_step", "chain")
    with stage(nc, *names) as (consts_in, w2_in0, w2_in1, logits, exped, routed, counted, h_turned,
                               h_copied, onehot, gathered, sorted_, starts_turned, starts_ready,
                               o_in, o_taken, o_up, o_tanh, o_gated, o_down, o_out, o_chain,
                               raw_in0, raw_in1, raw_in2, raw_in3, w_rounded, w_split, w_used, x_rounded, x_split,
                               tanh_done, gate_step, gated, g_turned, g_copied, down_done, stored,
                               spread, pt_turned, pt_copied, y_turned, y_copied, combined, added, combine_step, chain):
        raw_in, w2_in = [raw_in0, raw_in1, raw_in2, raw_in3], [w2_in0, w2_in1]
        w1, w3, w2 = ([expert_tiles(K, l, 0, s)[i][0] for s in range(2)] for i in range(3))
        xg = [K.f(16 + 4 * s, KC * SLOT).rearrange("p (k t) -> p k t", k=KC) for s in range(2)]
        gg = [K.f(24 + 2 * s, 4 * SLOT) for s in range(2)]
        th = [K.f(28 + 2 * s, 4 * SLOT) for s in range(2)]
        xs = K.f(32, KC * (A + SLOT)).rearrange("p (k t) -> p k t", k=KC)
        ys = K.f(68, KC * (A + SLOT)).rearrange("p (k t) -> p k t", k=KC)
        dest = K.route[:, 0:2 * T].rearrange("p (t j) -> p t j", j=2)
        wsel = K.route[:, 8:8 + 2 * T].rearrange("p (t j) -> p t j", j=2)
        ints = K.ints
        START, OVER_E, OVER_S, OVER_N = 0, 32, 48, 64

        def load_quarter(sp, e, p):
            k = 4 * (p % 2)
            src = K.A[("e_w1", "e_w3")[p // 2]][l, bass.ds(e, 1)].rearrange("a (k p) f -> p (a k) f", p=P)
            sp.dma_start((w1, w3)[p // 2][0][:, k:k + 4, :], src[:, k:k + 4, :]).then_inc(raw_in[p], 16)

        def load_down(sp, e, s):
            sp.dma_start(*expert_tiles(K, l, e, s)[2]).then_inc(w2_in[s], 16)

        def up_products(pe, s, bank):
            for i, w in enumerate((w1[s], w3[s])):
                for f in range(4):
                    last = accumulate(pe, K.ps[:, bank + i, f * SLOT:f * SLOT + SLOT], lambda k: w[:, k, f * P:f * P + P], lambda k: xg[s][:, k, :], KC)
            return last

        def down_products(pe, s, bank):
            g = gg[s].rearrange("p (f t) -> p f t", f=4)
            for d in range(KC):
                last = accumulate(pe, K.ps[:, bank + d // 4, d % 4 * SLOT:d % 4 * SLOT + SLOT], lambda f: w2[s][:, f, d * P:d * P + P],
                                  lambda f: g[:, f, :], 4)
            return last

        def outputs_of(bank):
            return K.ps[:, bank:bank + 2, 0:4 * SLOT].rearrange("p b (k t) -> p b k t", k=4)

        with nc.Block() as block:
            sb3 = lambda kib, n=32: K.f(kib, T * n).rearrange("p (t e) -> p t e", e=n)
            htok = K.f(152, T * D).rearrange("p (t d) -> p t d", t=T)
            oh = K.f(168, T * A).rearrange("p (t n) -> p t n", t=T)
            rw, rb, slot_iota = (dst for dst, _ in moe_consts(K, l))
            s_, sbias, s2, first, second, both = (sb3(185.5 + 0.5 * i) for i in range(1, 7))
            prod, destt = sb3(189), sb3(189.5)
            top8 = K.f(190, T * 4 * 8).rearrange("p (t g n) -> p t g n", g=4, n=8)
            g4 = K.f(190.5, T * 4).rearrange("p (t g) -> p t g", g=4)
            g4b = K.f(190.625, T * 4).rearrange("p (t g) -> p t g", g=4)
            gmax = K.f(190.75, T)
            t8 = K.f(191, T * 8).rearrange("p (t n) -> p t n", n=8)
            i8 = K.f(191.25, T * 8).bitcast(U32).rearrange("p (t n) -> p t n", n=8)
            i2 = K.f(191.5, T * 2).rearrange("p (t n) -> p t n", n=2)
            wsum = K.f(191.75, T)
            cnt, cum, start, nb, cumb, ovr, le = (K.f(192 + 0.125 * i, 32) for i in range(7))
            zero32 = K.f(193, 32)
            eb = K.f(193.25, 8)

            @block.sync
            def _(sp):
                K.early.hand_over(sp, 3, consts_in)
                K.early.hand_over(sp, 0, raw_in0)
                for p in range(1, 4):
                    sp.sem_inc(raw_in[p], 16)
                K.early.hand_over(sp, 1, w2_in0)

            @block.tensor
            def _(pe):
                pe.wait_ge(consts_in, 16)
                for i in range(T):
                    t = slice(t0 + i * P, t0 + i * P + P)
                    last = accumulate(pe, K.ps[:, 0, i * 32:i * 32 + 32], lambda k: K.H[:, k, t], lambda k: rw[:, k, :], KC)
                last.then_inc(logits, 1)
                for i in range(T):
                    for hf in range(2):
                        n = 2 * i + hf
                        if n >= 2:
                            pe.wait_ge(h_copied, n - 1)
                        for c in range(4):
                            k = 4 * hf + c
                            last = pe.transpose(K.ps[:, 1 + n % 2, c * P:c * P + P], K.H[:, k, t0 + i * P:t0 + i * P + P], K.ident)
                        last.then_inc(h_turned, 1)
                pe.wait_ge(routed, 1)
                for i in range(T):
                    for j in range(i + 1):
                        last = pe.matmul(K.ps[:, 3, i * 32:i * 32 + 32], K.before if j == i else K.ones, both[:, j, :],
                                         start=(j == 0), stop=(j == i))
                last = accumulate(pe, K.ps[:, 3, T * 32:T * 32 + 32], lambda j: K.ones, lambda j: both[:, j, :], T)
                last.then_inc(counted, 1)
                pe.wait_ge(starts_ready, 1)
                for j in range(2):
                    last = pe.transpose(K.ps[0:1, 0, 128 + j * P:256 + j * P], eb[:, j:j + 1], K.ident)
                last.then_inc(starts_turned, 1)
                pe.wait_ge(h_copied, 2 * T)
                pe.wait_ge(onehot, T)
                for n in range(KC * A // 512):
                    d, c = n % KC, n // KC
                    if n >= 4:
                        pe.wait_ge(gathered, n - 3)
                    accumulate(pe, K.ps[:, 4 + n % 4, :], lambda i: htok[:, i, d * P:d * P + P],
                               lambda i: oh[:, i, c * 512:c * 512 + 512], T).then_inc(sorted_, 1)

            @block.scalar
            def _(act):
                act.wait_ge(logits, 1)
                act.activation(s_, K.ps[:, 0, 0:T * 32].rearrange("p (t e) -> p t e", e=32), ACT.Exp, scale=-1.0).then_inc(exped, 1)
                for n in range(2 * T):
                    act.wait_ge(h_turned, n + 1)
                    act.activation(htok[:, n // 2, n % 2 * 512:n % 2 * 512 + 512], K.ps[:, 1 + n % 2, :], ACT.Copy).then_inc(h_copied, 1)
                for n in range(KC * A // 512):
                    d, c = n % KC, n // KC
                    act.wait_ge(sorted_, n + 1)
                    act.activation(xs[:, d, c * 512:c * 512 + 512], K.ps[:, 4 + n % 4, :], ACT.Copy).then_inc(gathered, 1)
                act.wait_ge(gathered, KC * A // 512)

            @block.vector
            def _(v):
                ch = Chain(v, chain)

                def do(ins):
                    ch.then(ins)
                    ch.wait()
                do(v.memset(zero32, 0.0))
                do(v.memset(xs[:, :, A:], 0.0))
                v.wait_ge(consts_in, 16)
                v.wait_ge(exped, 1)
                do(v.tensor_scalar(s_, s_, 1.0, None, ALU.add))
                do(v.reciprocal(s_, s_))
                do(v.tensor_tensor(sbias, s_, rb.rearrange("p (a e) -> p a e", a=1).to_broadcast([P, T, 32]), ALU.add))
                for i in range(T):
                    for g in range(N_GRP):
                        ch.then(v.max(top8[:, i, g, :], sbias[:, i, g * GRP:g * GRP + GRP]))
                ch.wait()
                do(v.tensor_tensor(g4, top8[:, :, :, 0], top8[:, :, :, 1], ALU.add))
                do(v.tensor_reduce(gmax, g4, AX.X, ALU.max))
                gm = gmax.rearrange("p (t a) -> p t a", a=1).to_broadcast([P, T, 4])
                do(v.tensor_tensor(g4, g4, gm, ALU.is_equal))
                rank = K.iota[:, 28:32]
                do(v.tensor_scalar(g4b, rank.rearrange("p (a e) -> p a e", a=1).to_broadcast([P, T, 4]), -1.0, 32.0, ALU.mult, ALU.add))
                do(v.tensor_tensor(g4, g4, g4b, ALU.mult))
                do(v.tensor_reduce(gmax, g4, AX.X, ALU.max))
                do(v.tensor_tensor(g4, g4, gm, ALU.is_equal))
                do(v.tensor_scalar(g4, g4, -1.0, 1e30, ALU.add, ALU.mult))
                do(v.tensor_tensor(s2.rearrange("p t (g e) -> p t g e", e=GRP), sbias.rearrange("p t (g e) -> p t g e", e=GRP),
                                   g4.rearrange("p t (g a) -> p t g a", a=1).to_broadcast([P, T, 4, GRP]), ALU.add))
                for i in range(T):
                    do(v.max(t8[:, i, :], s2[:, i, :]))
                    do(v.max_index(i8[:, i, :], t8[:, i, :], s2[:, i, :]))
                do(v.tensor_copy(i2, i8[:, :, 0:2]))
                io = K.iota.rearrange("p (a e) -> p a e", a=1).to_broadcast([P, T, 32])
                for j, o in enumerate((first, second)):
                    ch.then(v.tensor_tensor(o, io, i2[:, :, j:j + 1].to_broadcast([P, T, 32]), ALU.is_equal))
                ch.wait()
                v.tensor_tensor(both, first, second, ALU.add).then_inc(routed, 1)
                for j, o in enumerate((first, second)):
                    do(v.tensor_tensor(prod, o, s_, ALU.mult))
                    do(v.tensor_reduce(wsel[:, :, j:j + 1], prod, AX.X, ALU.add))
                do(v.tensor_tensor(wsum.rearrange("p (t a) -> p t a", a=1), wsel[:, :, 0:1], wsel[:, :, 1:2], ALU.add))
                do(v.reciprocal(wsum, wsum))
                do(v.tensor_tensor(wsel, wsel, wsum.rearrange("p (t a) -> p t a", a=1).to_broadcast([P, T, 2]), ALU.mult))
                v.wait_ge(counted, 1)
                do(v.tensor_copy(cnt, K.ps[:, 3, T * 32:T * 32 + 32]))
                do(v.tensor_tensor_scan(cum, cnt, zero32, 0.0, ALU.add, ALU.add))
                do(v.tensor_tensor(start, cum, cnt, ALU.subtract))
                do(v.tensor_tensor(destt, K.ps[:, 3, 0:T * 32].rearrange("p (t e) -> p t e", e=32),
                                   start.rearrange("p (a e) -> p a e", a=1).to_broadcast([P, T, 32]), ALU.add))
                for j, o in enumerate((first, second)):
                    do(v.tensor_tensor(prod, o, destt, ALU.mult))
                    do(v.tensor_reduce(dest[:, :, j:j + 1], prod, AX.X, ALU.add))
                for i in range(T):
                    do(v.tensor_scalar(oh[:, i, :], slot_iota, dest[:, i, 0:1], None, ALU.is_equal))
                    v.scalar_tensor_tensor(out=oh[:, i, :], in0=slot_iota, scalar=dest[:, i, 1:2], in1=oh[:, i, :],
                                           op0=ALU.is_equal, op1=ALU.add).then_inc(onehot, 1)
                do(v.tensor_scalar(nb, cnt, float(SLOT), None, ALU.is_gt))
                for j in range(2, -(-nt // SLOT)):
                    do(v.scalar_tensor_tensor(out=nb, in0=cnt, scalar=float(SLOT * j), in1=nb, op0=ALU.is_gt, op1=ALU.add))
                do(v.tensor_tensor_scan(cumb, nb, zero32, 0.0, ALU.add, ALU.add))
                do(v.tensor_tensor(ovr, cumb, nb, ALU.subtract))
                do(v.scalar_tensor_tensor(out=ovr, in0=ovr, scalar=-float(SLOT), in1=start, op0=ALU.mult, op1=ALU.add))
                do(v.tensor_scalar(le, cumb, K.pidx, None, ALU.is_le))
                do(v.tensor_reduce(eb[:, 0:1], le, AX.X, ALU.add))
                do(v.tensor_scalar(eb[:, 0:1], eb[:, 0:1], float(N_EXP - 1), None, ALU.min))
                do(v.tensor_scalar(le, K.iota, eb[:, 0:1], None, ALU.is_equal))
                do(v.tensor_tensor(le, le, ovr, ALU.mult))
                do(v.tensor_reduce(eb[:, 1:2], le, AX.X, ALU.add))
                do(v.tensor_scalar(eb[:, 2:3], K.pidx, float(SLOT), float(SLOT - A), ALU.mult, ALU.add))
                do(v.tensor_tensor(eb[:, 1:2], eb[:, 1:2], eb[:, 2:3], ALU.add))
                do(v.tensor_tensor(eb[:, 3:4], cumb[:, N_EXP - 1:N_EXP], K.pidx, ALU.is_gt))
                do(v.tensor_tensor(eb[:, 1:2], eb[:, 1:2], eb[:, 3:4], ALU.mult))
                v.tensor_scalar(eb[:, 1:2], eb[:, 1:2], float(A), None, ALU.add).then_inc(starts_ready, 1)
                do(v.tensor_copy(ints[:, START:START + 32], start[0:1, :]))
                do(v.tensor_copy(ints[:, OVER_N:OVER_N + 1], cumb[0:1, N_EXP - 1:N_EXP]))
                v.wait_ge(starts_turned, 1)
                do(v.tensor_copy(ints[:, OVER_E:OVER_E + 16], K.ps[0:1, 0, P:P + 16]))
                do(v.tensor_copy(ints[:, OVER_S:OVER_S + 16], K.ps[0:1, 0, 2 * P:2 * P + 16]))
                v.wait_ge(onehot, T)

        with nc.Block() as block:
            number = lambda eng: eng.value_load(ints[0:1, OVER_N:OVER_N + 1], min_val=0, max_val=n_over)

            @block.sync
            def _(sp):
                n = number(sp)
                with sp.Fori(0, n_over) as b:
                    with sp.If(n > b):
                        e = sp.value_load(ints[0:1, bass.ds(b + OVER_E, 1)], min_val=0, max_val=N_EXP - 1)
                        sp.wait_ge(o_down, b)
                        for dst, src in expert_tiles(K, l, e, 1):
                            sp.dma_start(dst, src).then_inc(o_in, 16)

            @block.vector
            def _(v):
                n = number(v)
                with v.Fori(0, n_over) as b:
                    with v.If(n > b):
                        r = v.value_load(ints[0:1, bass.ds(b + OVER_S, 1)], min_val=0, max_val=A)
                        v.wait_ge(o_up, b)
                        v.tensor_copy(xg[1], xs[:, :, bass.ds(r, SLOT)]).then_inc(o_taken, 1)
                        v.wait_ge(o_tanh, b + 1)
                        v.scalar_tensor_tensor(out=th[1], in0=th[1], scalar=1.0, in1=K.ps[:, 2, 0:4 * SLOT], op0=ALU.add,
                                               op1=ALU.mult).then_inc(o_chain, 1)
                        v.wait_ge(o_chain, b + 1)
                        v.wait_ge(o_down, b)
                        v.scalar_tensor_tensor(out=gg[1], in0=th[1], scalar=0.5, in1=K.ps[:, 3, 0:4 * SLOT], op0=ALU.mult,
                                               op1=ALU.mult).then_inc(o_gated, 1)

            @block.tensor
            def _(pe):
                n = number(pe)
                with pe.Fori(0, n_over) as b:
                    with pe.If(n > b):
                        pe.wait_ge(o_in, b * 48 + 48)
                        pe.wait_ge(o_taken, b + 1)
                        up_products(pe, 1, 2).then_inc(o_up, 1)
                        pe.wait_ge(o_gated, b + 1)
                        pe.wait_ge(o_out, b)
                        down_products(pe, 1, 6).then_inc(o_down, 1)

            @block.scalar
            def _(act):
                n = number(act)
                with act.Fori(0, n_over) as b:
                    with act.If(n > b):
                        r = act.value_load(ints[0:1, bass.ds(b + OVER_S, 1)], min_val=0, max_val=A)
                        act.wait_ge(o_up, b + 1)
                        act.wait_ge(o_gated, b)
                        act.activation(th[1], K.ps[:, 2, 0:4 * SLOT], ACT.Tanh, scale=0.5).then_inc(o_tanh, 1)
                        act.wait_ge(o_down, b + 1)
                        act.activation(ys[:, :, bass.ds(r, SLOT)].rearrange("p (b k) t -> p b k t", b=2), outputs_of(6), ACT.Copy).then_inc(o_out, 1)

        with nc.Block() as block:
            GR = 2 * KC // 2
            AHEAD = 4
            pair_of = lambda i: (w1, w3)[i // 4][0][:, 2 * (i % 4):2 * (i % 4) + 2, :]
            part = lambda kib: K.r(kib, 2 * D_EXP).rearrange("p (k f) -> p k f", k=2)
            w_hi = [part(152 + 8 * q) for q in range(AHEAD)]
            w_lo = [part(156 + 8 * q) for q in range(AHEAD)]
            x_hi, x_lo = (K.r(kib, KC * SLOT).rearrange("p (k t) -> p k t", k=KC) for kib in (16, 20))
            tanh, g, gT = (K.f(kib, D_EXP) for kib in (24, 26, 28))

            def granules(e, which, one):
                for i in which:
                    one(e if i < GR else e + 1, i % GR)

            @block.sync
            def _(sp):
                def quarter(e, p):
                    sp.wait_ge(w_split, e * GR + (2 * p + 2 - GR))
                    load_quarter(sp, e, p)

                def body(e, s, first=False, last=False):
                    quarter(e + 1, 2)
                    quarter(e + 1, 3)
                    if not last:
                        quarter(e + 2, 0)
                        quarter(e + 2, 1)
                    if not first:
                        sp.wait_ge(down_done, e)
                    load_down(sp, e + 1, 1 - s)

                quarter(1, 0)
                quarter(1, 1)
                body(0, 0, first=True)
                with sp.Fori(0, N_EXP // 2 - 2) as i:
                    for s in range(1, 3):
                        body(i * 2 + s, s % 2)
                body(N_EXP - 3, 1)
                body(N_EXP - 2, 0, last=True)

            @block.tensor
            def _(pe):
                def raise_(e, first=False):
                    pe.wait_ge(x_split, e + 1)
                    if not first:
                        pe.wait_ge(gated, e)
                    for i in range(GR):
                        pe.wait_ge(w_split, e * GR + (i + 1))
                        for j in range(2):
                            k = 2 * (i % 4) + j
                            out = K.ps[:, i // 4, :]
                            pe.matmul(out, x_hi[:, k, :], w_hi[i % AHEAD][:, j, :], start=(k == 0), stop=False)
                            pe.matmul(out, x_lo[:, k, :], w_hi[i % AHEAD][:, j, :], start=False, stop=False)
                            last = pe.matmul(out, x_hi[:, k, :], w_lo[i % AHEAD][:, j, :], start=False, stop=(k == KC - 1))
                        last.then_inc(w_used, 1)

                def turn(e):
                    pe.wait_ge(gated, e + 1)
                    for f in range(4):
                        last = pe.transpose(K.ps[:, 2, f * P:f * P + P], g[:, f * P:f * P + P], K.ident)
                    last.then_inc(g_turned, 1)

                def lower(e, s):
                    pe.wait_ge(w2_in[s], (e - s) * 8 + 16)
                    pe.wait_ge(g_copied, e + 1)
                    pe.wait_ge(stored, e)
                    for d in range(KC):
                        last = accumulate(pe, K.ps[:, 4 + 2 * s + d // 4, d % 4 * SLOT:d % 4 * SLOT + SLOT],
                                          lambda f: w2[s][:, f, d * P:d * P + P], lambda f: gT[:, f * P:f * P + P], 4)
                    last.then_inc(down_done, 1)

                raise_(0, first=True)
                turn(0)
                with pe.Fori(0, N_EXP // 2 - 1) as i:
                    for s in range(2):
                        raise_(i * 2 + (s + 1))
                        lower(i * 2 + s, s)
                        turn(i * 2 + (s + 1))
                raise_(N_EXP - 1)
                lower(N_EXP - 2, 0)
                turn(N_EXP - 1)
                lower(N_EXP - 1, 1)

            @block.scalar
            def _(act):
                act.preload_act_table(ACT.Exp)

                def round_(e, i, free=True):
                    if i % 2 == 0:
                        act.wait_ge(raw_in[i // 2], e * 16 + 16)
                    if free:
                        act.wait_ge(w_used, e * GR + (i + 1 - AHEAD))
                    act.activation(w_hi[i % AHEAD], pair_of(i), ACT.Copy).then_inc(w_rounded, 1)

                def take(e):
                    r = act.value_load(ints[0:1, bass.ds(e + START, 1)], min_val=0, max_val=A)
                    act.activation(x_hi, xs[:, :, bass.ds(r, SLOT)], ACT.Copy).then_inc(x_rounded, 1)

                def step(e, s, first=False, more=True):
                    granules(e, range(4, GR + 3 if more else GR), round_)
                    act.wait_ge(w_used, e * GR + GR)
                    if not first:
                        act.wait_ge(gated, e)
                    act.activation(tanh, K.ps[:, 0, :], ACT.Tanh, scale=0.5).then_inc(tanh_done, 1)
                    if more:
                        take(e + 1)
                        round_(e + 1, 3)
                    if not first:
                        store(e - 1, 1 - s)
                    act.wait_ge(g_turned, e + 1)
                    act.activation(gT, K.ps[:, 2, :], ACT.Copy).then_inc(g_copied, 1)

                def store(e, s):
                    r = act.value_load(ints[0:1, bass.ds(e + START, 1)], min_val=0, max_val=A)
                    act.wait_ge(down_done, e + 1)
                    act.activation(ys[:, :, bass.ds(r, SLOT)], outputs_of(4 + 2 * s), ACT.Copy).then_inc(stored, 1)

                take(0)
                for i in range(AHEAD):
                    round_(0, i, free=False)
                step(0, 0, first=True)
                with act.Fori(0, N_EXP // 2 - 1) as i:
                    for s in range(1, 3):
                        step(i * 2 + s, s % 2)
                step(N_EXP - 1, 1, more=False)
                store(N_EXP - 1, 1)
                act.wait_ge(stored, N_EXP)

            @block.vector
            def _(v):
                def rest(e, i):
                    v.wait_ge(w_rounded, e * GR + (i + 1))
                    v.tensor_tensor(w_lo[i % AHEAD], pair_of(i), w_hi[i % AHEAD].bitcast(F32), ALU.subtract).then_inc(w_split, 1)

                def take(e):
                    r = v.value_load(ints[0:1, bass.ds(e + START, 1)], min_val=0, max_val=A)
                    v.wait_ge(x_rounded, e + 1)
                    v.tensor_tensor(x_lo, xs[:, :, bass.ds(r, SLOT)], x_hi.bitcast(F32), ALU.subtract).then_inc(x_split, 1)

                def step(e, s, first=False, more=True):
                    granules(e, range(4, GR + 3 if more else GR), rest)
                    v.wait_ge(tanh_done, e + 1)
                    v.scalar_tensor_tensor(out=tanh, in0=tanh, scalar=1.0, in1=K.ps[:, 0, :], op0=ALU.add,
                                           op1=ALU.mult).then_inc(gate_step, 1)
                    v.wait_ge(gate_step, e + 1)
                    if not first:
                        v.wait_ge(g_turned, e)
                    v.scalar_tensor_tensor(out=g, in0=tanh, scalar=0.5, in1=K.ps[:, 1, :], op0=ALU.mult,
                                           op1=ALU.mult).then_inc(gated, 1)
                    if more:
                        take(e + 1)
                        rest(e + 1, 3)

                take(0)
                for i in range(AHEAD):
                    rest(0, i)
                step(0, 0, first=True)
                with v.Fori(0, N_EXP // 2 - 1) as i:
                    for s in range(1, 3):
                        step(i * 2 + s, s % 2)
                step(N_EXP - 1, 1, more=False)

        with nc.Block() as block:
            ytok = K.f(104, SC * D).rearrange("p (c d) -> p c d", c=SC)
            pt = K.f(136, SC * nt).rearrange("p (c t) -> p c t", c=SC)
            pw = K.f(152, T * A).rearrange("p (t n) -> p t n", t=T)
            half = K.f(168, A)
            slot_iota = K.f(32, A)

            @block.sync
            def _(sp):
                sp.dma_start(slot_iota, K.A["d_slots"][:, 0:A]).then_inc(consts_in, 16)
                if l + 1 < DEPTH:
                    for dst, src in filter_consts(K, l + 1):
                        K.early.issue(sp, 3, dst, src)

            @block.vector
            def _(v):
                v.wait_ge(consts_in, 32)
                for i in range(T):
                    if i >= 1:
                        v.wait_ge(spread, i)
                    for j, out in enumerate((pw[:, i, :], half)):
                        v.tensor_scalar(out, slot_iota, dest[:, i, j:j + 1], wsel[:, i, j:j + 1], ALU.is_equal,
                                        ALU.mult).then_inc(combine_step, 1)
                    v.wait_ge(combine_step, 2 * i + 2)
                    v.tensor_tensor(pw[:, i, :], pw[:, i, :], half, ALU.add).then_inc(spread, 1)
                for d in range(KC):
                    v.wait_ge(combined, d + 1)
                    for q in range(2 - ns, 2):
                        v.scalar_tensor_tensor(out=K.X[:, d, q * SEQ:q * SEQ + SEQ], in0=K.ps[:, 4 + d % 4, q * SEQ - t0:q * SEQ - t0 + SEQ],
                                               scalar=K.mod[:, 48 * l + G2 + d, q:q + 1], in1=K.X[:, d, q * SEQ:q * SEQ + SEQ],
                                               op0=ALU.mult, op1=ALU.add).then_inc(added, 1)
                v.wait_ge(added, KC * ns)

            @block.tensor
            def _(pe):
                for n in range(2 * SC):
                    c, hf = n // 2, n % 2
                    if n >= 2:
                        pe.wait_ge(y_copied, n - 1)
                    for k in range(4):
                        last = pe.transpose(K.ps[:, n % 2, k * P:k * P + P], ys[:, 4 * hf + k, c * P:c * P + P], K.ident)
                    last.then_inc(y_turned, 1)
                pe.wait_ge(spread, T)
                for c in range(SC):
                    if c >= 2:
                        pe.wait_ge(pt_copied, c - 1)
                    for i in range(T):
                        last = pe.transpose(K.ps[:, 2 + c % 2, i * P:i * P + P], pw[:, i, c * P:c * P + P], K.ident)
                    last.then_inc(pt_turned, 1)
                pe.wait_ge(y_copied, 2 * SC)
                pe.wait_ge(pt_copied, SC)
                for d in range(KC):
                    if d >= 4:
                        pe.wait_ge(added, (d - 3) * ns)
                    accumulate(pe, K.ps[:, 4 + d % 4, 0:nt], lambda c: ytok[:, c, d * P:d * P + P], lambda c: pt[:, c, :],
                               SC).then_inc(combined, 1)

            @block.scalar
            def _(act):
                for n in range(2 * SC):
                    act.wait_ge(y_turned, n + 1)
                    act.activation(ytok[:, n // 2, n % 2 * 512:n % 2 * 512 + 512], K.ps[:, n % 2, :], ACT.Copy).then_inc(y_copied, 1)
                for c in range(SC):
                    act.wait_ge(pt_turned, c + 1)
                    act.activation(pt[:, c, :], K.ps[:, 2 + c % 2, 0:nt], ACT.Copy).then_inc(pt_copied, 1)


def stage_result(nc, K):
    with stage(nc, "result_out") as (result_out,), nc.Block() as block:
        @block.sync
        def _(sp):
            sp.dma_start(K.A["outT"], K.X[:, :, SEQ:]).then_inc(result_out, 16)
            sp.wait_ge(result_out, 16)


def build(nc, A):
    K = Core(A)
    with ExitStack() as ctx:
        sb = lambda n, s, d=F32: ctx.enter_context(nc.sbuf_tensor(n, s, d))
        arena_at = -(-nc.sbuf_base // 32) * 32
        low, high = sb("low_arena", [P, CUT * 256]), sb("high_arena", [P, (200 - CUT) * 256])
        rounded = {}

        def place(kib, n):
            at = int(kib * 256)
            assert at + n <= CUT * 256 or at >= CUT * 256, (kib, n)
            return low[:, at:at + n] if at < CUT * 256 else high[:, at - CUT * 256:at - CUT * 256 + n]

        def rounded_at(kib, n):
            if (kib, n) not in rounded:
                rounded[kib, n] = nc.alloc_sbuf_tensor_at(f"rounded_{kib}_{n}", [P, n], F32R, offset=arena_at + kib * 1024)
            return rounded[kib, n][:, :]
        K.f, K.r = place, rounded_at
        K.i = lambda kib, n: place(kib, n).bitcast(I32)
        K.ring = lambda s, n=3072: place(64 + 12 * s, n)
        chunked = lambda kib: K.f(kib, KC * NTOK).rearrange("p (k t) -> p k t", k=KC)
        K.X, K.H, K.Y, K.YB = chunked(0), chunked(16), chunked(32), chunked(48)
        K.dft = K.f(172, 4 * 2 * SEQ).rearrange("p (c t n) -> p c t n", c=4, t=2)
        K.spec = K.f(180, 2 * 2 * D).rearrange("p (c f n) -> p c f n", c=2, f=2)
        K.neg_m = K.f(132, 8 * NTOK).rearrange("p (r t) -> p r t", r=8)
        K.gate_cols = K.f(148, 2 * 4 * 36).rearrange("p (j t r) -> p j t r", j=2, t=4)
        K.masks = K.f(150, 2 * 2 * SEQ).rearrange("p (d b t) -> p d b t", d=2, b=2)
        K.hs = K.f(154, 4 * D).rearrange("p (t h c) -> p t h c", t=4, h=M_HEADS)
        K.og = chunked(170)
        ident = sb("ident", [P, P]); K.ident = ident[:, :]
        ones = sb("ones", [P, P]); K.ones = ones[:, :]
        group64 = sb("group64", [P, P]); K.group64 = group64[:, :]
        rot = sb("rot", [P, P]); K.rot = rot[:, :]
        before = sb("before", [P, P]); K.before = before[:, :]
        iota = sb("iota", [P, 32]); K.iota = iota[:, :]
        cols = sb("cols", [P, DEPTH * N_COLS]); K.cols = cols[:, :].rearrange("p (l n) -> p l n", l=DEPTH)
        mod = sb("mod", [P, DEPTH * 48 * 2]); K.mod = mod[:, :].rearrange("p (j s) -> p j s", s=2)
        gain = sb("gain", [P, DEPTH * 2 * KC * 2]); K.gain = gain[:, :].rearrange("p (l h k s) -> p l h k s", l=DEPTH, h=2, s=2)
        hmb = sb("half_mb", [P, DEPTH * 24]); K.half_mb = hmb[:, :].rearrange("p (l n) -> p l n", l=DEPTH)
        rn = sb("rn", [P, KC]); K.rn = rn[:, :]
        eps = sb("eps", [P, 1]); K.eps = eps[:, :]
        pidx = sb("pidx", [P, 1]); K.pidx = pidx[:, :]
        route = sb("route", [P, 16]); K.route = route[:, :]
        ints = sb("ints", [1, 96], I32); K.ints = ints[:, :]
        lam4 = sb("lam4", [A_DH, DEPTH * 4]); K.lam4 = lam4[:, :].rearrange("p (l n) -> p l n", l=DEPTH)
        ps = ctx.enter_context(nc.psum_tensor("ps", [P, 8, 512], F32))
        K.ps = ps[:, :, :]

        K.early = Early(nc, 4)
        stage_modulation(nc, K)
        for l in range(DEPTH):
            stage_norm_filter(nc, K, l)
            stage_hyena(nc, K, l)
            merge = stage_merge_split if spans(l)[1] == 2 else stage_merge
            merge(nc, K, l, 2, first=True)
            stage_attention(nc, K, l)
            merge(nc, K, l, 1, first=False)
            stage_gates(nc, K, l)
            stage_mlstm(nc, K, l)
            stage_mlstm_out(nc, K, l)
            merge(nc, K, l, 0, first=False)
            stage_out(nc, K, l)
            stage_norm2(nc, K, l)
            stage_moe(nc, K, l)
        stage_result(nc, K)
    return K


def tables():
    f = np.float32
    t = np.arange(SEQ)
    ang = np.pi * np.outer(t, 2 * t + 1) / (2 * SEQ)
    tiles = lambda a: a.reshape(2, P, SEQ).transpose(1, 0, 2)
    dft = np.stack([tiles(np.cos(ang)), tiles(np.sin(ang)), tiles(np.cos(ang).T / SEQ), tiles(np.sin(ang).T / SEQ)], 1)
    out = {"dft": dft.astype(f), "ident": np.eye(P, dtype=f)}
    out["group64"] = np.kron(np.eye(2), np.ones((A_DH, A_DH))).astype(f)
    r = np.zeros((P, P), f)
    for b in range(0, P, 32):
        for i in range(16):
            r[b + 16 + i, b + i] = -1
            r[b + i, b + 16 + i] = 1
    out["rot"] = r
    nf = A_DH // 4
    inv = 10000.0 ** (-np.arange(nf, dtype=f) / f(nf))
    ar, ac = np.outer(t // GRID_W, inv), np.outer(t % GRID_W, inv)
    a = np.concatenate([ar, ar, ac, ac], 1).astype(f)
    out["rope"] = np.stack([np.tile(np.cos(a).T, (2, 1)), np.tile(np.sin(a).T, (2, 1))], 1).astype(f)
    out["before"] = np.triu(np.ones((P, P), f), 1)
    out["pidx"] = np.arange(P, dtype=f)[:, None]
    out["slots"] = np.tile(np.arange(SORTED, dtype=f), (P, 1))
    out["iota"] = np.tile(np.arange(32, dtype=f), (P, 1))
    lin = np.linspace(0.0, 1.0, SEQ, dtype=f)
    bands = (H_EMB - 1) // 2
    w = (2.0 * math.pi * np.arange(SEQ, dtype=f) / f(SEQ)).astype(f)
    fr = np.linspace(1e-4, bands - 1, bands, dtype=f)
    fw = (fr[None, :] * w[:, None]).astype(f)
    out["zT"] = np.concatenate([lin[:, None], np.cos(fw), -np.sin(fw)], 1).T.astype(f)
    out["negt"] = -lin.reshape(2, P).T
    s_, t_ = np.arange(SEQ).reshape(2, P).T[:, :, None], t[None, None, :]
    far = f(-30000.0)
    out["masks"] = np.stack([np.where(s_ <= t_, f(0), far), np.where(s_ >= t_, f(0), far)], 1)
    sel = np.zeros((P, 8, P), f)
    for r in range(8):
        sel[(0, 32)[r // 4] + r % 4, r, :] = 1
    out["sel"] = sel
    return out


def lay_out(inp):
    g = {k: np.asarray(v) for k, v in inp.items()}
    f = np.float32
    A = {"d_" + k: v for k, v in tables().items()}
    chan = lambda a: a.reshape(KC, P, -1).transpose(1, 0, 2)
    A["xT"] = chan(np.concatenate([g["ctx"][0], g["x"][0]], 0).T)
    A["cT"] = chan(np.stack([g["c_ctx"], g["c"][0]], 1))
    A["d_modb"] = g["mod_b"].reshape(DEPTH * 48, P).T
    tiles = lambda w, c: w.reshape(KC, P, -1, c * P).transpose(2, 1, 0, 3).reshape(-1, P, KC * c * P)
    A["d_modw"] = np.concatenate([tiles(g["mod_w"][l], 3) for l in range(DEPTH)])
    cols = np.zeros((DEPTH, P, N_COLS), f)
    for l in range(DEPTH):
        c = cols[l]
        c[:, C_N1:C_N1 + 8] = g["norm1_g"][l].reshape(-1, P).T
        c[:, C_N2:C_N2 + 8] = g["norm2_g"][l].reshape(-1, P).T
        c[:, C_MB:C_MB + 24] = g["merge_b"][l].reshape(-1, P).T
        c[:, C_MCW:C_MCW + 48] = g["m_conv_w"][l].reshape(-1, P).T
        c[:, C_MCB:C_MCB + 16] = g["m_conv_b"][l].reshape(-1, P).T
        c[:, C_HCW:C_HCW + 72] = g["h_conv_w"][l].reshape(-1, P).T
        c[:, C_HCB:C_HCB + 24] = g["h_conv_b"][l].reshape(-1, P).T
        c[:, C_HBIAS:C_HBIAS + 8] = g["h_bias"][l].reshape(-1, P).T
        c[:, C_QG] = np.concatenate([g["a_qnorm_g"][l]] * 2)
        c[:, C_KG] = np.concatenate([g["a_knorm_g"][l]] * 2)
        c[:, C_SUB] = g["a_subln_g"][l]
        c[:, C_MN:C_MN + 2] = g["m_norm_g"][l].reshape(2, P).T
        c[0:H_FFN, C_FREQ] = g["h_freq"][l]
        c[0:H_FFN, C_FB1] = g["h_ffn_b1"][l]
        c[0:H_FFN, C_FB2] = g["h_ffn_b2"][l]
        for row, src in ((0, 0), (32, 8), (64, 4), (96, 12)):
            c[row:row + 4, C_GB] = g["m_gate_b"][l][src:src + 4]
    A["d_cols"] = cols.transpose(1, 0, 2)
    A["d_lam4"] = g["a_lambda"].transpose(2, 0, 1)
    A["d_fw1"], A["d_fw2"], A["d_fw3"], A["d_delta"] = g["h_ffn_w1"], g["h_ffn_w2"], g["h_ffn_w3"], np.broadcast_to(
        g["h_decay"].reshape(DEPTH, 1, 2 * D), (DEPTH, P, 2 * D))
    hyena = g["w_in"][:, :, 4 * D + 16 + 3 * D:4 * D + 16 + 6 * D].reshape(DEPTH, KC, P, 3, KC, P)
    A["d_wh"] = hyena.transpose(0, 4, 2, 1, 3, 5).reshape(DEPTH, KC, P, KC * 3 * P)
    w = g["w_in"].reshape(DEPTH, KC, P, -1)
    pick = lambda at, n: w[..., at:at + n]
    slab = lambda parts: np.concatenate(parts, -1).transpose(0, 2, 1, 3).reshape(DEPTH, P, -1)
    q0, k0, v0, o0, g0 = (i * D for i in range(5))
    aq, ak, av = (4 * D + 16 + i * D for i in range(3))
    gates = 4 * D + 16 + 6 * D
    wm = []
    for b, name in enumerate(("w_br_m", "w_br_a", "w_br_h")):
        wb = g[name].reshape(DEPTH, KC, P, D)
        wm.append(np.stack([slab([wb[..., m * P:m * P + P], pick(gates + b * D + m * P, P)]) for m in range(KC)], 1))
    A["d_wm"] = np.stack(wm, 1)
    wo = g["w_out"].reshape(DEPTH, KC, P, D)
    A["d_wo"] = np.stack([slab([wo[..., m * 256:m * 256 + 256]]) for m in range(KC // 2)], 1)
    A["d_wa"] = np.stack([slab([pick(aq + h * P, P), pick(ak + h * P, P), pick(av + h * P, P)]) for h in range(A_HEADS)], 1)
    A["d_wma"] = np.stack([np.stack([slab([pick(q0 + h * 256, 256), pick(k0 + h * 256, P)]),
                                     slab([pick(k0 + h * 256 + P, P), pick(v0 + h * 256, 256)])], 1)
                           for h in range(M_HEADS)], 1)
    A["d_wmc"] = np.stack([slab([pick(o0 + h * 256, 256)]) for h in range(M_HEADS)], 1)
    A["d_rw"] = chan(g["router_w"])
    A["d_rb"] = np.broadcast_to(g["router_b"], (P, N_EXP))
    A["e_w1"], A["e_w3"], A["e_w2"] = g["e_w1"], g["e_w3"], g["e_w2"]
    none = np.zeros((DEPTH, KC, P, 28), f)
    A["d_wg"] = slab([pick(g0, 4), none, pick(g0 + 8, 4), none, pick(g0 + 4, 4), none, pick(g0 + 12, 4), none])
    return {k: np.ascontiguousarray(v, f) for k, v in A.items()}


def kernel(**inputs):
    import concourse.bacc as bacc
    from concourse.bass_utils import run_bass_kernel_spmd

    arrays = lay_out(inputs)
    nc = bacc.Bacc("TRN2", target_bir_lowering=False, num_devices=1)
    args = {name: nc.dram_tensor("in_" + name, a.shape, F32, kind="ExternalInput").ap() for name, a in arrays.items()}
    args["outT"] = nc.dram_tensor("outT", (P, KC, SEQ), F32, kind="ExternalOutput").ap()
    build(nc, args)
    r = run_bass_kernel_spmd(nc, [{"in_" + name: a for name, a in arrays.items()}], core_ids=[0])
    out = np.asarray(r.results[0]["outT"])
    return np.ascontiguousarray(out.transpose(2, 1, 0).reshape(1, SEQ, D))
```
